# Optimizing a Trainium2 kernel written in Bass

```python
import math
import jax, jax.numpy as jnp
from jax import lax
import numpy as np

D_MODEL = 1024
BATCH = 1
SEQ = 256
DEPTH = 2

PLE_DIM = 256
EPS = 1e-6
BLOCK = 128
SB_HEADS = 8
SB_DIM = 64
SB_WIDTH = SB_HEADS * SB_DIM
HG_HEADS = 4
HG_DK = 128
HG_DV = 128
HG_QK = HG_HEADS * HG_DK
HG_V = HG_HEADS * HG_DV
HG_CHUNK = 64
AB_SPLITS = [SB_WIDTH] * 3 + [HG_QK] * 2 + [HG_V] * 2
AB_IN = sum(AB_SPLITS)
AB_OUT = SB_WIDTH + HG_V
SW_HEADS = 16
SW_KV_HEADS = 4
SW_DIM = 64
SW_GROUP = SW_HEADS // SW_KV_HEADS
WINDOW = 128
C_IN = (SW_HEADS + 2 * SW_KV_HEADS) * SW_DIM
C_OUT = SW_HEADS * SW_DIM
N_BUCKETS = 32
MAX_DISTANCE = 128
D_FF = 2816
CONV_W = 3
N_EVEN = (DEPTH + 1) // 2
N_ODD = DEPTH // 2


def rmsnorm(x, g):
    xf = x.astype(jnp.float32)
    y = xf * lax.rsqrt(jnp.mean(xf * xf, axis=-1, keepdims=True) + EPS)
    return (y * g.astype(jnp.float32)).astype(x.dtype)

def stick_breaking_attention(q, k, v):
    S = q.shape[1]
    qf = jnp.swapaxes(q, 1, 2).astype(jnp.float32)
    kf = jnp.swapaxes(k, 1, 2).astype(jnp.float32)
    vf = jnp.swapaxes(v, 1, 2).astype(jnp.float32)
    scale = SB_DIM ** -0.5
    outs = []
    for n in range(S // BLOCK):
        t0 = n * BLOCK
        kn = t0 + BLOCK
        z = jnp.einsum('bhtd,bhsd->bhts', qf[:, :, t0:kn], kf[:, :, :kn]) * scale
        t_pos = t0 + jnp.arange(BLOCK)[:, None]
        s_pos = jnp.arange(kn)[None, :]
        mask = s_pos < t_pos
        log_keep = jnp.where(mask, jax.nn.log_sigmoid(-z), 0.0)
        later = lax.cumsum(log_keep, axis=3, reverse=True) - log_keep
        w = jnp.where(mask, jnp.exp(jax.nn.log_sigmoid(z) + later), 0.0)
        outs.append(jnp.einsum('bhts,bhsd->bhtd', w, vf[:, :, :kn]))
    o = jnp.concatenate(outs, axis=2)
    return jnp.swapaxes(o, 1, 2)

def hgrn2(q, f_pre, i, lb):
    B, S = q.shape[:2]
    lb = lb.reshape(HG_HEADS, HG_DK).astype(jnp.float32)
    fp = f_pre.astype(jnp.float32)
    log_f = jnp.log(lb + (1.0 - lb) * jax.nn.sigmoid(fp))
    kk = (1.0 - lb) * jax.nn.sigmoid(-fp)
    qf = jax.nn.silu(q.astype(jnp.float32))
    nc = S // HG_CHUNK

    def to_chunks(a):
        return a.reshape(B, nc, HG_CHUNK, HG_HEADS, a.shape[-1]).transpose(1, 0, 3, 2, 4)

    causal = jnp.tril(jnp.ones((HG_CHUNK, HG_CHUNK), dtype=bool))

    def step(state, xs):
        qc, kc, lfc, ic = xs
        b = jnp.cumsum(lfc, axis=2)
        o_inter = jnp.einsum('bhtk,bhkv->bhtv', qc * jnp.exp(b), state)
        rel = jnp.where(causal[:, :, None], b[:, :, :, None, :] - b[:, :, None, :, :], -jnp.inf)
        scores = jnp.einsum('bhtk,bhsk,bhtsk->bhts', qc, kc, jnp.exp(rel))
        o = o_inter + jnp.einsum('bhts,bhsv->bhtv', scores, ic)
        b_last = b[:, :, -1:, :]
        state = jnp.exp(b_last[:, :, 0, :, None]) * state + jnp.einsum('bhsk,bhsv->bhkv', kc * jnp.exp(b_last - b), ic)
        return state, o

    s0 = jnp.zeros((B, HG_HEADS, HG_DK, HG_DV), jnp.float32)
    _, o = lax.scan(step, s0, (to_chunks(qf), to_chunks(kk), to_chunks(log_f), to_chunks(i.astype(jnp.float32))))
    return o.transpose(1, 0, 3, 2, 4).reshape(B, S, HG_HEADS, HG_DV)

def t5_band_buckets():
    t = np.arange(WINDOW)[:, None]
    s = np.arange(2 * WINDOW)[None, :]
    dist = t + WINDOW - s
    band = (dist >= 0) & (dist < WINDOW)
    max_exact = N_BUCKETS // 2
    large = max_exact + (np.log(np.maximum(dist, max_exact) / max_exact) / math.log(MAX_DISTANCE / max_exact) * (N_BUCKETS - max_exact)).astype(np.int32)
    large = np.minimum(large, N_BUCKETS - 1)
    bucket = np.where(dist < max_exact, np.maximum(dist, 0), large).astype(np.int32)
    return bucket, band

def sliding_window_attention(q, k, v, sinks, rel_bias):
    B, S = q.shape[:2]
    nb = S // WINDOW
    bucket, band = t5_band_buckets()
    bias = rel_bias.astype(jnp.float32)[bucket]
    bias = bias.transpose(2, 0, 1).reshape(SW_KV_HEADS, SW_GROUP, WINDOW, 2 * WINDOW)
    key_pos = np.arange(nb)[:, None] * WINDOW - WINDOW + np.arange(2 * WINDOW)[None, :]
    mask = jnp.asarray(band[None] & (key_pos >= 0)[:, None, :])
    qb = q.astype(jnp.float32).reshape(B, nb, WINDOW, SW_KV_HEADS, SW_GROUP, SW_DIM).transpose(1, 0, 2, 3, 4, 5)

    def band_keys(a):
        ap = jnp.pad(a.astype(jnp.float32), ((0, 0), (WINDOW, 0), (0, 0), (0, 0)))
        ap = ap.reshape(B, nb + 1, WINDOW, SW_KV_HEADS, SW_DIM)
        return jnp.concatenate([ap[:, :-1], ap[:, 1:]], axis=2).transpose(1, 0, 2, 3, 4)

    kb, vb = band_keys(k), band_keys(v)
    sink = sinks.astype(jnp.float32).reshape(SW_KV_HEADS, SW_GROUP, 1, 1)
    scale = SW_DIM ** -0.5

    def block_attn(args):
        qn, kn, vn, mn = args
        logits = jnp.einsum('bqhgd,bkhd->bhgqk', qn, kn) * scale + bias
        logits = jnp.where(mn, logits, -jnp.inf)
        m = jnp.maximum(jnp.max(logits, axis=-1, keepdims=True), sink)
        e = jnp.exp(logits - m)
        w = e / (jnp.sum(e, axis=-1, keepdims=True) + jnp.exp(sink - m))
        return jnp.einsum('bhgqk,bkhd->bqhgd', w, vn)

    o = lax.map(block_attn, (qb, kb, vb, mask))
    return o.transpose(1, 0, 2, 3, 4, 5).reshape(B, S, SW_HEADS, SW_DIM)

def mixer_ab(h, w_in, lb, hg_norm, w_out):
    B, S, _ = h.shape
    proj = h @ w_in
    qa, ka, va, qb, fb, ib, gb = jnp.split(proj, np.cumsum(AB_SPLITS)[:-1].tolist(), axis=-1)
    sb_shape = (B, S, SB_HEADS, SB_DIM)
    o_a = stick_breaking_attention(qa.reshape(sb_shape), ka.reshape(sb_shape), va.reshape(sb_shape))
    o_a = o_a.astype(h.dtype).reshape(B, S, SB_WIDTH)
    o_b = hgrn2(qb.reshape(B, S, HG_HEADS, HG_DK), fb.reshape(B, S, HG_HEADS, HG_DK), ib.reshape(B, S, HG_HEADS, HG_DV), lb)
    o_b = rmsnorm(o_b.astype(h.dtype), hg_norm) * jax.nn.silu(gb.reshape(B, S, HG_HEADS, HG_DV))
    o_b = o_b.reshape(B, S, HG_V)
    return jnp.concatenate([o_a, o_b], axis=-1) @ w_out

def mixer_c(h, w_in, q_norm, k_norm, sinks, rel_bias, w_out):
    B, S, _ = h.shape
    proj = h @ w_in
    q, k, v = jnp.split(proj, [SW_HEADS * SW_DIM, (SW_HEADS + SW_KV_HEADS) * SW_DIM], axis=-1)
    q = rmsnorm(q.reshape(B, S, SW_HEADS, SW_DIM), q_norm)
    k = rmsnorm(k.reshape(B, S, SW_KV_HEADS, SW_DIM), k_norm)
    v = v.reshape(B, S, SW_KV_HEADS, SW_DIM)
    o = sliding_window_attention(q, k, v, sinks, rel_bias).astype(h.dtype)
    return o.reshape(B, S, C_OUT) @ w_out

def conv_glu_ffn(h, w_up, conv_w, conv_b, w_down):
    u = h @ w_up
    u = lax.conv_general_dilated(u, conv_w[:, None, :], window_strides=(1,), padding=[(CONV_W - 1, 0)],
                                 dimension_numbers=('NWC', 'WIO', 'NWC'), feature_group_count=2 * D_FF) + conv_b
    gate, up = jnp.split(u, 2, axis=-1)
    return (jax.nn.silu(gate) * up) @ w_down

def first_inputs(seed: int = 0) -> dict:
    key = jax.random.key(seed)
    ks = jax.random.split(key, 21)

    def nrm(k, shape):
        return jax.random.normal(k, shape, jnp.float32)

    def w(k, shape, fan_in):
        return nrm(k, shape) * fan_in ** -0.5

    def gain(k, shape):
        return 1.0 + 0.02 * nrm(k, shape)

    F2 = 2 * D_FF
    return {
        'x': nrm(ks[0], (BATCH, SEQ, D_MODEL)),
        'p': nrm(ks[1], (DEPTH, BATCH, SEQ, PLE_DIM)),
        'mix_norm': gain(ks[2], (DEPTH, D_MODEL)),
        'ab_w_in': w(ks[3], (N_EVEN, D_MODEL, AB_IN), D_MODEL),
        'hg_lb_logits': 0.5 * nrm(ks[4], (N_EVEN, HG_QK)),
        'hg_out_norm': gain(ks[5], (N_EVEN, HG_DV)),
        'ab_w_out': w(ks[6], (N_EVEN, AB_OUT, D_MODEL), AB_OUT),
        'c_w_in': w(ks[7], (N_ODD, D_MODEL, C_IN), D_MODEL),
        'q_norm': gain(ks[8], (N_ODD, SW_DIM)),
        'k_norm': gain(ks[9], (N_ODD, SW_DIM)),
        'sinks': 0.5 * nrm(ks[10], (N_ODD, SW_HEADS)),
        'rel_bias': 0.5 * nrm(ks[11], (N_BUCKETS, SW_HEADS)),
        'c_w_out': w(ks[12], (N_ODD, C_OUT, D_MODEL), C_OUT),
        'ffn_norm': gain(ks[13], (DEPTH, D_MODEL)),
        'ffn_up': w(ks[14], (DEPTH, D_MODEL, F2), D_MODEL),
        'ffn_conv': w(ks[15], (DEPTH, CONV_W, F2), CONV_W),
        'ffn_conv_b': 0.02 * nrm(ks[16], (DEPTH, F2)),
        'ffn_down': w(ks[17], (DEPTH, D_FF, D_MODEL), D_FF),
        'ple_norm': gain(ks[18], (DEPTH, D_MODEL)),
        'ple_gate': w(ks[19], (DEPTH, D_MODEL, D_MODEL), D_MODEL),
        'ple_proj': w(ks[20], (DEPTH, PLE_DIM, D_MODEL), PLE_DIM),
    }

def first_block(x, p, mix_norm, ab_w_in, hg_lb_logits, hg_out_norm, ab_w_out, c_w_in, q_norm, k_norm,
              sinks, rel_bias, c_w_out, ffn_norm, ffn_up, ffn_conv, ffn_conv_b, ffn_down,
              ple_norm, ple_gate, ple_proj):
    lb_cum = jnp.cumsum(jax.nn.softmax(hg_lb_logits.astype(jnp.float32), axis=0), axis=0)
    lower_bounds = lb_cum - lb_cum[0]
    h = x
    for i in range(DEPTH):
        j = i // 2
        hn = rmsnorm(h, mix_norm[i])
        if i % 2 == 0:
            h = h + mixer_ab(hn, ab_w_in[j], lower_bounds[j], hg_out_norm[j], ab_w_out[j])
        else:
            h = h + mixer_c(hn, c_w_in[j], q_norm[j], k_norm[j], sinks[j], rel_bias, c_w_out[j])
        h = h + conv_glu_ffn(rmsnorm(h, ffn_norm[i]), ffn_up[i], ffn_conv[i], ffn_conv_b[i], ffn_down[i])
        gate = jax.nn.sigmoid(rmsnorm(h, ple_norm[i]) @ ple_gate[i])
        h = h + gate * (p[i] @ ple_proj[i])
    return h


DEPTH_2 = 1

HEAD_DIM = 128
MOBA_HEADS = 6
MOBA_BLOCK = 256
MOBA_TOPK = 3
MOBA_QCHUNK = 32
GMLP_GROUPS = 6
GMLP_GROUP_DIM = 128
GMLP_CHUNK = 128
XATTN_HEADS = 4
MEM_LEN = 256
ROPE_THETA = 500000.0
ROT_DIM = HEAD_DIM // 4

A_WIDTH = MOBA_HEADS * HEAD_DIM
B_WIDTH = GMLP_GROUPS * GMLP_GROUP_DIM
C_WIDTH = XATTN_HEADS * HEAD_DIM
IN_SPLITS = (A_WIDTH, A_WIDTH, A_WIDTH, A_WIDTH, B_WIDTH, B_WIDTH, B_WIDTH, C_WIDTH, C_WIDTH, D_MODEL, D_MODEL, D_MODEL)
IN_WIDTH = 4 * A_WIDTH + 3 * B_WIDTH + 2 * C_WIDTH + 3 * D_MODEL


def rms_norm(x, g):
    xf = x.astype(jnp.float32)
    y = xf * lax.rsqrt(jnp.mean(xf * xf, axis=-1, keepdims=True) + EPS)
    return (y * g.astype(jnp.float32)).astype(x.dtype)

def layer_norm(x, g):
    xf = x.astype(jnp.float32)
    mu = jnp.mean(xf, axis=-1, keepdims=True)
    var = jnp.mean(jnp.square(xf - mu), axis=-1, keepdims=True)
    return ((xf - mu) * lax.rsqrt(var + EPS) * g.astype(jnp.float32)).astype(x.dtype)

def split_cols(t, widths):
    offs, acc = [], 0
    for w in widths[:-1]:
        acc += w
        offs.append(acc)
    return jnp.split(t, offs, axis=-1)

def partial_rope(x, pos):
    half = ROT_DIM // 2
    inv_freq = ROPE_THETA ** (-jnp.arange(0, ROT_DIM, 2, dtype=jnp.float32) / ROT_DIM)
    ang = pos.astype(jnp.float32)[:, None] * inv_freq[None, :]
    cos = jnp.cos(ang)[None, :, None, :].astype(x.dtype)
    sin = jnp.sin(ang)[None, :, None, :].astype(x.dtype)
    x1, x2, rest = x[..., :half], x[..., half:ROT_DIM], x[..., ROT_DIM:]
    return jnp.concatenate([x1 * cos - x2 * sin, x2 * cos + x1 * sin, rest], axis=-1)

def moba_attention(q, k, v):
    B, S, H, dh = q.shape
    n_blocks = -(-S // MOBA_BLOCK)
    k_sel_n = min(MOBA_TOPK, n_blocks)
    pad = n_blocks * MOBA_BLOCK - S
    scale = HEAD_DIM ** -0.5
    qh = jnp.transpose(q, (0, 2, 1, 3))
    kh = jnp.pad(jnp.transpose(k, (0, 2, 1, 3)), ((0, 0), (0, 0), (0, pad), (0, 0)))
    vh = jnp.pad(jnp.transpose(v, (0, 2, 1, 3)), ((0, 0), (0, 0), (0, pad), (0, 0)))
    k_blk = kh.reshape(B, H, n_blocks, MOBA_BLOCK, dh)
    v_blk = vh.reshape(B, H, n_blocks, MOBA_BLOCK, dh)
    k_mean = jnp.mean(k_blk.astype(jnp.float32), axis=3)
    b_ix = jnp.arange(B)[:, None, None, None]
    h_ix = jnp.arange(H)[None, :, None, None]
    blk_ids = jnp.arange(n_blocks)

    def chunk_fn(c):
        start = c * MOBA_QCHUNK
        qc = lax.dynamic_slice_in_dim(qh, start, MOBA_QCHUNK, axis=2)
        pos_q = start + jnp.arange(MOBA_QCHUNK)
        own = start // MOBA_BLOCK
        bs = jnp.einsum('bhqd,bhnd->bhqn', qc.astype(jnp.float32), k_mean)
        bs = jnp.where((blk_ids < own)[None, None, None, :], bs, -jnp.inf)
        _, sel_idx = lax.top_k(bs, k_sel_n)
        sel_valid = sel_idx < own
        k_sel = k_blk[b_ix, h_ix, sel_idx]
        v_sel = v_blk[b_ix, h_ix, sel_idx]
        lg_sel = jnp.einsum('bhqd,bhqkpd->bhqkp', qc, k_sel).astype(jnp.float32) * scale
        lg_sel = jnp.where(sel_valid[..., None], lg_sel, -jnp.inf)
        lg_sel = lg_sel.reshape(B, H, MOBA_QCHUNK, k_sel_n * MOBA_BLOCK)
        k_own = lax.dynamic_index_in_dim(k_blk, own, axis=2, keepdims=False)
        v_own = lax.dynamic_index_in_dim(v_blk, own, axis=2, keepdims=False)
        key_pos = own * MOBA_BLOCK + jnp.arange(MOBA_BLOCK)
        causal = key_pos[None, :] <= pos_q[:, None]
        lg_own = jnp.einsum('bhqd,bhpd->bhqp', qc, k_own).astype(jnp.float32) * scale
        lg_own = jnp.where(causal[None, None], lg_own, -jnp.inf)
        p = jax.nn.softmax(jnp.concatenate([lg_sel, lg_own], axis=-1), axis=-1).astype(v.dtype)
        p_sel = p[..., :k_sel_n * MOBA_BLOCK].reshape(B, H, MOBA_QCHUNK, k_sel_n, MOBA_BLOCK)
        p_own = p[..., k_sel_n * MOBA_BLOCK:]
        return (jnp.einsum('bhqkp,bhqkpd->bhqd', p_sel, v_sel)
                + jnp.einsum('bhqp,bhpd->bhqd', p_own, v_own))

    out = lax.map(chunk_fn, jnp.arange(S // MOBA_QCHUNK))
    return jnp.transpose(out, (1, 0, 3, 2, 4)).reshape(B, S, H * dh)

def gmlp_spatial_gate(u, v, ln_g, w_spatial, b_spatial):
    B, S, _ = v.shape
    vn = layer_norm(v, ln_g).reshape(B, S // GMLP_CHUNK, GMLP_CHUNK, GMLP_GROUPS, GMLP_GROUP_DIM)
    w_causal = jnp.tril(w_spatial)
    mixed = jnp.einsum('gts,bnsgd->bntgd', w_causal, vn) + jnp.transpose(b_spatial)[None, None, :, :, None]
    return u * mixed.reshape(B, S, B_WIDTH)

def memory_cross_attention(q, mem_n, w_mem_kv):
    B, S, _ = q.shape
    M = mem_n.shape[1]
    mk, mv = jnp.split(mem_n @ w_mem_kv, 2, axis=-1)
    qh = q.reshape(B, S, XATTN_HEADS, HEAD_DIM)
    kh = mk.reshape(B, M, XATTN_HEADS, HEAD_DIM)
    vh = mv.reshape(B, M, XATTN_HEADS, HEAD_DIM)
    lg = jnp.einsum('bshd,bmhd->bhsm', qh, kh).astype(jnp.float32) * (HEAD_DIM ** -0.5)
    p = jax.nn.softmax(lg, axis=-1).astype(q.dtype)
    return jnp.einsum('bhsm,bmhd->bshd', p, vh).reshape(B, S, C_WIDTH)

def second_inputs(seed: int = 0) -> dict:
    key = jax.random.key(seed)
    ks = jax.random.split(key, 16)
    f32 = jnp.float32

    def nrm(k, shape, fan_in):
        return jax.random.normal(k, shape, f32) * (fan_in ** -0.5)

    def gain(k, shape):
        return 1.0 + 0.1 * jax.random.normal(k, shape, f32)

    return {
        "x": jax.random.normal(ks[0], (BATCH, SEQ, D_MODEL), f32),
        "mem": jax.random.normal(ks[1], (BATCH, MEM_LEN, D_MODEL), f32),
        "norm_g": gain(ks[2], (DEPTH_2, D_MODEL)),
        "mem_norm_g": gain(ks[3], (DEPTH_2, D_MODEL)),
        "final_norm_g": gain(ks[4], (D_MODEL,)),
        "w_in": nrm(ks[5], (DEPTH_2, D_MODEL, IN_WIDTH), D_MODEL),
        "w_mem_kv": nrm(ks[6], (DEPTH_2, D_MODEL, 2 * C_WIDTH), D_MODEL),
        "gmlp_ln_g": gain(ks[7], (DEPTH_2, B_WIDTH)),
        "w_spatial": nrm(ks[8], (DEPTH_2, GMLP_GROUPS, GMLP_CHUNK, GMLP_CHUNK), GMLP_CHUNK),
        "b_spatial": gain(ks[9], (DEPTH_2, GMLP_GROUPS, GMLP_CHUNK)),
        "w_branch_a": nrm(ks[10], (DEPTH_2, A_WIDTH, D_MODEL), A_WIDTH),
        "w_branch_b": nrm(ks[11], (DEPTH_2, B_WIDTH, D_MODEL), B_WIDTH),
        "w_branch_c": nrm(ks[12], (DEPTH_2, C_WIDTH, D_MODEL), C_WIDTH),
        "w_out": nrm(ks[13], (DEPTH_2, D_MODEL, D_MODEL), D_MODEL),
    }

def second_block(x, mem, norm_g, mem_norm_g, final_norm_g, w_in, w_mem_kv, gmlp_ln_g,
              w_spatial, b_spatial, w_branch_a, w_branch_b, w_branch_c, w_out):
    B, S, _ = x.shape
    pos = jnp.arange(S)
    for layer in range(DEPTH_2):
        h = rms_norm(x, norm_g[layer])
        (qa, ka, va, ga, ub, vb, gb, qc, gc, ma, mb, mc) = split_cols(h @ w_in[layer], IN_SPLITS)
        qa = partial_rope(qa.reshape(B, S, MOBA_HEADS, HEAD_DIM), pos)
        ka = partial_rope(ka.reshape(B, S, MOBA_HEADS, HEAD_DIM), pos)
        va = va.reshape(B, S, MOBA_HEADS, HEAD_DIM)
        out_a = moba_attention(qa, ka, va) * jax.nn.silu(ga)
        out_b = gmlp_spatial_gate(ub, vb, gmlp_ln_g[layer], w_spatial[layer], b_spatial[layer]) * jax.nn.silu(gb)
        mem_n = rms_norm(mem, mem_norm_g[layer])
        out_c = memory_cross_attention(qc, mem_n, w_mem_kv[layer]) * jax.nn.silu(gc)
        y = (jax.nn.sigmoid(ma) * (out_a @ w_branch_a[layer])
             + jax.nn.sigmoid(mb) * (out_b @ w_branch_b[layer])
             + jax.nn.sigmoid(mc) * (out_c @ w_branch_c[layer]))
        x = x + y @ w_out[layer]
    return rms_norm(x, final_norm_g)


def setup_inputs(seed=0):
    out = dict(first_inputs(seed))
    for name, value in second_inputs(seed + 1).items():
        if name != "x":
            out[name + "_2"] = value
    return out


def reference(
    x, p, mix_norm, ab_w_in, hg_lb_logits, hg_out_norm, ab_w_out, c_w_in, q_norm, k_norm, sinks,
    rel_bias, c_w_out, ffn_norm, ffn_up, ffn_conv, ffn_conv_b, ffn_down, ple_norm, ple_gate,
    ple_proj, mem_2, norm_g_2, mem_norm_g_2, final_norm_g_2, w_in_2, w_mem_kv_2, gmlp_ln_g_2,
    w_spatial_2, b_spatial_2, w_branch_a_2, w_branch_b_2, w_branch_c_2, w_out_2,
):
    x = first_block(
        x, p, mix_norm, ab_w_in, hg_lb_logits, hg_out_norm, ab_w_out, c_w_in, q_norm, k_norm,
        sinks, rel_bias, c_w_out, ffn_norm, ffn_up, ffn_conv, ffn_conv_b, ffn_down, ple_norm,
        ple_gate, ple_proj,
    )
    return second_block(
        x, mem_2, norm_g_2, mem_norm_g_2, final_norm_g_2, w_in_2, w_mem_kv_2, gmlp_ln_g_2,
        w_spatial_2, b_spatial_2, w_branch_a_2, w_branch_b_2, w_branch_c_2, w_out_2,
    )


_drawn_inputs = setup_inputs


def setup_inputs(seed=0):
    import zlib

    import numpy as np

    out = dict(_drawn_inputs(seed))
    spreads = {}
    factors = {'mix_norm': 3.328,
     'hg_out_norm': 5.853,
     'q_norm': 8.0,
     'k_norm': 8.0,
     'sinks': 42.628,
     'ffn_norm': 3.145,
     'ffn_conv_b': 3.272,
     'ple_norm': 33.513,
     'mem_2': 2.82,
     'mem_norm_g_2': 8.0,
     'w_mem_kv_2': 2.687,
     'gmlp_ln_g_2': 35.056,
     'b_spatial_2': 24.656,
     'w_branch_c_2': 2.719,
     'w_branch_a_2': 8.0}
    for name, (base, spread) in spreads.items():
        noise = np.random.default_rng([zlib.crc32(name.encode()), seed]).standard_normal(out[name].shape)
        drawn = base * np.exp(spread * noise) if base else spread * noise
        out[name] = __import__('jax').numpy.asarray(drawn.astype(out[name].dtype))
    for name, factor in factors.items():
        out[name] = (out[name] * factor).astype(out[name].dtype)
    return out
```

```python
from contextlib import ExitStack

import numpy as np

import concourse.bass as bass
from concourse import mybir

ALU = mybir.AluOpType
ACT = mybir.ActivationFunctionType
AX = mybir.AxisListType
F32 = mybir.dt.float32
F32R = mybir.dt.float32r
I32 = mybir.dt.int32

P = 128
T = 256
TT = T // P
D = 1024
KT = D // P
EPS = 1e-6
NEG = -1e30
SB_HEADS, SB_DIM = 8, 64
HG_HEADS, HG_CHUNK = 4, 64
SW_HEADS, SW_KV, SW_DIM, WINDOW = 16, 4, 64, 128
BUCKETS, MAX_DISTANCE = 32, 128
D_FF = 2816
FT = D_FF // P
MOBA_HEADS, X_HEADS, GROUPS, HEAD = 6, 4, 6, 128
ROT = HEAD // 4
LEVELS = [64, 32, 16, 8, 4, 2, 1, 0]
RAW, RING = 3, 3
MAGIC = float(0x5F3759DF)



def shape_constants():
    i = np.arange(P)
    s, t = i[:, None], i[None, :]
    levels = []
    for half in LEVELS:
        if half:
            levels.append((s // (2 * half) == t // (2 * half)) & (s % (2 * half) < half) & (t % (2 * half) >= half))
        else:
            levels.append(s == t)
    dist = 127 - i
    exact = BUCKETS // 2
    large = exact + (np.log(np.maximum(dist, exact) / exact) / np.log(MAX_DISTANCE / exact) * (BUCKETS - exact)).astype(np.int32)
    bucket = np.where(dist < exact, dist, np.minimum(large, BUCKETS - 1))
    inv_freq = np.float32(500000.0) ** (-np.arange(0, ROT, 2, dtype=np.float32) / np.float32(ROT))
    ang = (np.arange(T, dtype=np.float32)[:, None] * inv_freq[None, :]).astype(np.float32)
    return {
        "c_ident": np.eye(P, dtype=np.float32),
        "c_tri": (s >= t).astype(np.float32),
        "c_levels": np.stack(levels, 1).astype(np.float32).reshape(P, -1),
        "c_reset": np.tile((np.arange(HG_HEADS * T) % HG_CHUNK != 0).astype(np.float32), (P, 1)),
        "c_causal": np.where(np.arange(T)[None, :] - P <= s, 0.0, NEG).astype(np.float32),
        "c_bucket": (bucket[None, :] == np.arange(BUCKETS)[:, None]).astype(np.float32),
        "c_rope": np.stack([np.cos(ang), np.sin(ang)], 1).reshape(TT, P, 2, ROT // 2).transpose(1, 0, 2, 3).reshape(P, -1).astype(np.float32).copy(),
    }


VEC = {}
VEC_LOADS = []


def _vectors():
    at = 0
    for name, layer, n in [("mix_norm", 0, 8), ("mix_norm", 1, 8), ("ffn_norm", 0, 8), ("ffn_norm", 1, 8),
                           ("ple_norm", 0, 8), ("ple_norm", 1, 8), ("norm_g_2", 0, 8), ("mem_norm_g_2", 0, 8),
                           ("hg_out_norm", 0, 1), ("hg_lb_logits", 0, 4), ("gmlp_ln_g_2", 0, 6)]:
        VEC[name, layer] = at
        VEC_LOADS.append((name, (layer,), at, n))
        at += n
    for name in ("q_norm", "k_norm"):
        VEC[name, 0] = at
        VEC_LOADS.append((name, (0,), at, 1))
        at += 1
    at = P
    for layer in range(2):
        VEC["ffn_conv_b", layer] = at + 2 * FT * layer
        VEC_LOADS.append(("ffn_conv_b", (layer,), at + 2 * FT * layer, 2 * FT))
    for n, (layer, tap) in enumerate([(a, b) for a in range(2) for b in range(3)]):
        at = P * (2 + n // 2) + 2 * FT * (n % 2)
        VEC["ffn_conv", layer, tap] = at
        VEC_LOADS.append(("ffn_conv", (layer, tap), at, 2 * FT))


_vectors()
VEC_ROWS = [77, 4 * FT, 4 * FT, 4 * FT, 4 * FT]


class Events:

    def __init__(self, known, make):
        self.known, self.make = known, make
        self.sems, self.count, self.said, self.links = {}, {}, {}, 0

    def sem(self, name):
        if name not in self.sems:
            self.sems[name] = self.make(name)
        return self.sems[name]

    def mark(self, name, *events, by=1):
        self.count[name] = self.count.get(name, 0) + by
        for e in events:
            self.said[e] = (name, self.count[name])
        return self.sem(name), by

    def at(self, event):
        name, value = self.known[event] if self.known else ("first_pass", 1)
        return self.sem(name), value

    def chained(self, *events):
        self.links += 1
        return self.mark("vector_chain", ("link", self.links), *events)

    def chain(self):
        return self.at(("link", self.links))


def panels_of():
    out = []

    def cols(stage, name, at, n, kind, idx=()):
        for i in range(n):
            out.append((stage, i, name, kind, (idx, at + 256 * i)))

    def rows(stage, name, n, kind, idx=()):
        for i in range(n):
            out.append((stage, i, name, kind, (idx, 256 * i)))

    for stage, at, kind in (("qb", 1536, "F"), ("fb", 2048, "F"), ("ib", 2560, "T"), ("gb", 3072, "T"),
                            ("qa", 0, "F"), ("ka", 512, "F"), ("va", 1024, "T")):
        cols(stage, "ab_w_in", at, 2, kind, (0,))
    cols("wo0", "ab_w_out", 0, 4, "T", (0,))
    for layer in range(2):
        for i in range(FT):
            out.append((f"up{layer}", i, "ffn_up", "F", ((layer,), i * P)))
        rows(f"down{layer}", "ffn_down", FT // 2, "BT", (layer,))
        rows(f"pp{layer}", "ple_proj", 1, "BT", (layer,))
        cols(f"gate{layer}", "ple_gate", 0, 4, "T", (layer,))
        if layer == 0:
            cols("qs", "c_w_in", 0, 4, "T", (0,))
            cols("ks", "c_w_in", 1024, 1, "T", (0,))
            cols("vs", "c_w_in", 1280, 1, "T", (0,))
            cols("wo1", "c_w_out", 0, 4, "T", (0,))
    cols("mk", "w_mem_kv_2", 0, 2, "F", (0,))
    cols("mv", "w_mem_kv_2", 512, 2, "T", (0,))
    for stage, at, n, kind in (("qc", 5376, 2, "F"), ("gc", 5888, 2, "F"), ("qka", 0, 6, "T"), ("va2", 1536, 3, "T"),
                               ("ga", 2304, 3, "F"), ("vb", 3840, 3, "T"), ("gb2", 4608, 3, "F"), ("ub", 3072, 3, "F")):
        cols(stage, "w_in_2", at, n, kind, (0,))
    for b, at, n in (("c", 8448, 2), ("b", 7424, 3), ("a", 6400, 3)):
        cols("m" + b, "w_in_2", at, 4, "F", (0,))
        rows("br" + b, f"w_branch_{b}_2", n, "BF", (0,))
    cols("wo2", "w_out_2", 0, 4, "T", (0,))
    return out


PANELS = panels_of()
FIRST = {}
for _n, _p in enumerate(PANELS):
    FIRST.setdefault(_p[0], _n)


def last_of(stage):
    return max(n for n, p in enumerate(PANELS) if p[0] == stage)


def schedule():
    out = []

    def gemm(*stages):
        for s in stages:
            out.extend(("panel", n) for n, p in enumerate(PANELS) if p[0] == s)

    def norm(k):
        out.extend([("stats", k), ("turn", k)])

    out.append(("setup",))
    norm("mix0")
    gemm("qb", "fb")
    out.append(("hg_decay",))
    gemm("ib", "gb")
    out.append(("hg_level", -1))
    out.append(("hg_level", 0))
    gemm("qa")
    out.append(("hg_level", 1))
    out.append(("hg_level", 2))
    out.append(("hg_level", 3))
    gemm("ka")
    out.append(("hg_level", 4))
    out.append(("hg_level", 5))
    gemm("va")
    out.append(("hg_level", 6))
    out.append(("hg_level", 7))
    for i in range(SB_HEADS // 2):
        out.append(("sb_scores", i))
    out.append(("sb_log",))
    out.append(("hg_out",))
    out.append(("hg_turn",))
    for i in range(SB_HEADS // 2):
        out.append(("sb_weights", i))
    for i in range(SB_HEADS // 2):
        out.append(("sb_out", i))
    gemm("wo0")
    for layer in range(2):
        norm(f"ffn{layer}")
        if layer == 0:
            out.append(("bias",))
        gemm(f"up{layer}")
        out.append(("up_tail", layer))
        out.append(("ple_input", layer))
        gemm(f"down{layer}")
        gemm(f"pp{layer}")
        if layer == 1:
            out.append(("stats", "mem"))
        norm(f"ple{layer}")
        gemm(f"gate{layer}")
        if layer == 0:
            norm("mix1")
            gemm("qs", "ks", "vs")
            out.append(("sw_norm",))
            for g in range(SW_KV):
                out.append(("sw_logits", g))
                out.append(("sw_weights", g))
                out.append(("sw_out", g))
            gemm("wo1")
    out.append(("turn", "mem"))
    out.append(("stats", "blk2"))
    gemm("mk", "mv")
    out.append(("turn", "blk2"))
    gemm("qc", "gc")
    out.append(("x_logits", 0))
    gemm("qka")
    out.extend([("x_weights", 0), ("x_logits", 1), ("x_out", 0), ("rope",)])
    gemm("va2")
    out.extend([("x_weights", 1), ("x_out", 1), ("rope_turn",), ("spatial",), ("a_logits", 0)])
    gemm("ga")
    out.extend([("a_weights", 0), ("a_logits", 1), ("a_out", 0)])
    gemm("vb")
    out.extend([("a_weights", 1), ("a_logits", 2), ("a_out", 1), ("layer_norm",)])
    gemm("gb2")
    out.extend([("a_weights", 2), ("a_out", 2)])
    gemm("ub")
    out.append(("mixed",))
    for b in "cba":
        gemm("m" + b, "br" + b)
        out.append(("branch_end", b))
    out.append(("y_split",))
    gemm("wo2")
    out.append(("stats", "final"))
    return out


SCHEDULE = schedule()


def block_program(nc, io, out_ap, known):
    with ExitStack() as ctx:
        events = Events(known, lambda name: ctx.enter_context(nc.semaphore(name)))
        mark, at, chained, chain = events.mark, events.at, events.chained, events.chain
        top = [16512]

        def fixed(name, shape, dt=F32):
            n = 4 * int(np.prod(shape[1:]))
            n = (n + 31) // 32 * 32
            t = nc.alloc_sbuf_tensor_at(name, shape, dt, offset=top[0])
            top[0] += n
            return t

        raw = [fixed(f"w_raw{i}", [P, 2048]) for i in range(RAW)]
        whi = [fixed(f"w_hi{i}", [P, 2048], F32R) for i in range(RING)]
        wlo = [fixed(f"w_lo{i}", [P, 2048], F32R) for i in range(RING)]
        XH, XL = (fixed(n, [P, KT, T], F32R) for n in ("x_hi", "x_lo"))
        h = fixed("h", [P, TT, D])
        xn = fixed("xn", [P, TT, D])
        ident = fixed("ident", [P, P])
        tri = fixed("tri", [P, P])
        vecs = fixed("vecs", [P, 5, P])
        small = fixed("small", [P, 320])
        g_at = top[0]
        GH, GL = (fixed(n, [P, FT, T], F32R) for n in ("g_hi", "g_lo"))
        t_at = top[0]
        end = nc.sbuf_usable_end

        class Region:

            def __init__(self, at, end):
                self.at, self.end = at, end

            def __call__(self, name, shape, dt=F32):
                n = 4 * int(np.prod(shape[1:]))
                t = nc.alloc_sbuf_tensor_at(name, shape, dt, offset=self.at)
                self.at += n
                assert self.at <= self.end, (name, self.at - self.end)
                return t

        r, g = Region(t_at, end), Region(g_at, t_at)
        qaT, kaT = r("qaT", [P, 4, T]), r("kaT", [P, 4, T])
        va, ib, gbs = r("va", [P, TT, 512]), r("ib", [P, TT, 512]), r("gbs", [P, TT, 512])
        qf, kk, bdec = r("qf", [P, HG_HEADS, T]), r("kk", [P, HG_HEADS, T]), r("bdec", [P, HG_HEADS, T])
        ex, prod = r("ex", [P, HG_HEADS, T]), r("prod", [P, len(LEVELS), P])
        masks = r("masks", [P, len(LEVELS), P])
        zs, sp_ = g("zs", [P, SB_HEADS, 384]), g("sp_", [P, SB_HEADS, 384])
        reset, sc, on = g("reset", [P, HG_HEADS * T]), g("sc", [P, HG_HEADS, 384]), g("on", [P, TT, HG_HEADS, P])
        exb = g("exb", [P, HG_HEADS, T])
        xs_buf = [r(f"xs{i}", [P, HG_HEADS, T]) for i in range(2)]
        ones = g("ones", [P, P])
        prod4 = prod[:, :, :].rearrange("p (t a) c -> p t (a c)", t=TT)

        def blocks_of(buf, h0):
            return buf[:, h0:h0 + 2, :].rearrange("p h (a c) -> p h a c", a=3)[:, :, 0:3:2, :]

        def blocks_of_prod(j):
            return prod[:, 4 * j:4 * j + 4, :].rearrange("p (h t) c -> p h t c", h=2)

        r = Region(t_at, end)
        cc = [r(f"cc{i}", [P, 2, T]) for i in range(3)]
        sgate = [r(f"sgate{i}", [P, T]) for i in range(2)]
        gf = [r(f"gf{i}", [P, T]) for i in range(2)]
        praw = r("praw", [P, TT, 256])
        PTH, PTL = r("pt_hi", [P, 2, T], F32R), r("pt_lo", [P, 2, T], F32R)
        gate = [r(f"gate{i}", [P, TT, 256]) for i in range(2)]
        vsw = r("vsw", [P, TT, 256])
        bias = r("bias", [P, SW_HEADS, T])
        brow = r("brow", [16, 3 * P])
        relb, buck = r("relb", [32, 16]), r("buck", [32, P])
        r, g = Region(t_at, t_at + 4 * 4096), Region(g_at, t_at)
        qsT, le_s = r("qsT", [P, 8, T]), r("le_s", [P, 4, 2, T])
        qk, sq = g("qk", [P, TT, 1280]), g("sq", [P, TT, 1280])
        qkn = g("qkn", [P, TT, 24, SW_DIM])
        wT_s = g("wT_s", [P, 4, 384])
        ksT = g("ksT", [P, SW_KV, T])
        qF = nc.alloc_sbuf_tensor_at("qF", [P, MOBA_HEADS, T], F32, offset=g_at + 4 * T * 16)
        kF = nc.alloc_sbuf_tensor_at("kF", [P, MOBA_HEADS, T], F32, offset=g_at + 4 * T * (FT + 16))
        mem = nc.alloc_sbuf_tensor_at("mem", [P, TT, D], F32, offset=g_at)
        mem_junk = nc.alloc_sbuf_tensor_at("mem_junk", [P, D], F32, offset=g_at + 4 * TT * D)
        r = Region(t_at, end)
        qkm = r("qkm", [P, TT, 1536])
        qc, gc = r("qc", [P, X_HEADS, T]), r("gc", [P, X_HEADS, T])
        mk, mv = r("mk", [P, X_HEADS, T]), r("mv", [P, TT, 512])
        le, wT = r("le", [P, 2, 2, T]), r("wT", [P, 2, 2, T])
        va2, vb = r("va2", [P, TT, 768]), r("vb", [P, TT, 768])
        wsp, bsp = r("wsp", [P, GROUPS, P]), r("bsp", [P, GROUPS, P])
        causal = r("causal", [P, T])
        r = Region(t_at, t_at + 4 * 3072)
        ubs, ga = r("ubs", [P, GROUPS, T]), r("ga", [P, MOBA_HEADS, T])
        r = Region(t_at + 4 * 3072, end)
        msig = [r(f"msig{i}", [P, KT, T]) for i in range(2)]
        gfin, result = r("gfin", [P, D]), r("result", [P, TT, D])
        xflat = xn[:, :, :].rearrange("p a b -> p (a b)")
        y = xflat.rearrange("p (k t) -> p k t", k=KT)
        rtmp = xflat[:, 0:768].rearrange("p (f e j) -> p f e j", f=4, e=12)
        wsp_raw = xflat[:, 1024:1792].rearrange("p (g s) -> p g s", g=GROUPS)
        mixt = xflat[:, 0:1536].rearrange("p (g t) -> p g t", g=GROUPS)

        bank = [ctx.enter_context(nc.psum_tensor(f"bank{i}", [P, 512], F32)) for i in range(8)]
        BW = 3 * P
        scratch = nc.dram_tensor("bias_rows", [SW_HEADS, P, BW], F32, kind="Internal").ap()

        small_at = [64]

        def col(n):
            small_at[0] += n
            assert small_at[0] <= 320
            return small[:, small_at[0] - n:small_at[0]]

        rope = small[:, 0:64].rearrange("p (t c f) -> p t c f", t=TT, c=2)
        NORMS = ["mix0", "ffn0", "ple0", "mix1", "ffn1", "mem", "ple1", "blk2", "final"]
        ssq, mean_sq, rstd = ({k: col(TT) for k in NORMS} for _ in range(3))
        minus_half = col(TT)
        lb, oml, lb_tmp = col(HG_HEADS), col(HG_HEADS), col(HG_HEADS)
        q_gain, sinks = col(1), col(SW_HEADS)
        hg_ss, hg_rs, hg_tmp = col(8), col(8), col(8)
        s_max, s_neg, s_sum, s_exp = col(8), col(8), col(8), col(8)
        ln_sum, ln_neg, ln_ss, ln_rs = col(TT), col(TT), col(TT), col(TT)
        sw_ss, sw_rs, sw_tmp = col(40), col(40), qkn[:, 0, 23, 0:40]

        vflat = vecs[:, :, :].rearrange("p a b -> p (a b)")

        def vec(name, layer, *more):
            return lambda i: vflat[:, VEC[(name, layer, *more)] + i:VEC[(name, layer, *more)] + i + 1]

        GAIN = {"mix0": vec("mix_norm", 0), "mix1": vec("mix_norm", 1), "ffn0": vec("ffn_norm", 0), "ffn1": vec("ffn_norm", 1),
                "ple0": vec("ple_norm", 0), "ple1": vec("ple_norm", 1), "blk2": vec("norm_g_2", 0), "mem": vec("mem_norm_g_2", 0)}

        def plain(ap):
            return ap.bitcast(F32)

        def two(b):
            return bank[b][:, :].rearrange("p (a c) -> p a c", a=2)

        def pb(n):
            return 4 + n % 4

        READY = {"mix0": ("loaded", "x"), "ffn0": ("ev", last_of("wo0")), "ple0": ("h", "down0", 1), "mix1": ("ev", last_of("gate0")),
                 "ffn1": ("ev", last_of("wo1")), "ple1": ("h", "down1", 1), "blk2": ("ev", last_of("gate1")),
                 "mem": ("loaded", "mem"), "final": ("ev", last_of("wo2"))}
        XUSED = {"ffn0": ("pe", last_of("wo0")), "ple0": ("pe", last_of("up0")), "mix1": ("pe", last_of("gate0")),
                 "ffn1": ("pe", last_of("wo1")), "ple1": ("pe", last_of("up1")), "mem": ("pe", last_of("gate1")),
                 "blk2": ("pe", last_of("mv"))}
        XIN = {}
        for s in ("qb", "fb", "ib", "gb", "qa", "ka", "va"):
            XIN[s] = (XH, XL, 0, [("xl", "mix0", 3)])
        XIN["wo0"] = (XH, XL, 0, [("xl", "sb", 3), ("xl", "hg", 1)])
        XIN["wo1"] = (XH, XL, 0, [("xl", "sw", 7)])
        for l in range(2):
            XIN[f"up{l}"] = (XH, XL, 0, [("xl", f"ffn{l}", 3)])
            XIN[f"down{l}"] = (GH, GL, 0, [("gl", l, FT - 1)])
            XIN[f"pp{l}"] = (PTH, PTL, 0, [("ptl", l)])
            XIN[f"gate{l}"] = (XH, XL, 0, [("xl", f"ple{l}", 3)])
        for s in ("qs", "ks", "vs"):
            XIN[s] = (XH, XL, 0, [("xl", "mix1", 3)])
        for s in ("mk", "mv"):
            XIN[s] = (XH, XL, 0, [("xl", "mem", 3)])
        for s in ("qc", "gc", "qka", "va2", "ga", "vb", "gb2", "ub", "mc", "mb", "ma"):
            XIN[s] = (XH, XL, 0, [("xl", "blk2", 3)])
        OUT_AT = {"a": 0, "b": MOBA_HEADS, "c": MOBA_HEADS + GROUPS}
        XIN["brc"] = (GH, GL, OUT_AT["c"], [("ol", "c", X_HEADS - 1)])
        XIN["brb"] = (GH, GL, OUT_AT["b"], [("ol", "b", GROUPS - 1)])
        XIN["bra"] = (GH, GL, OUT_AT["a"], [("ol", "a", MOBA_HEADS - 1)])
        XIN["wo2"] = (XH, XL, 0, [("xl", "y", 3)])

        block = ctx.enter_context(nc.Block())

        @block.sync
        def _(sp):
            def load(dst, src, name):
                sp.dma_start(dst, src).then_inc(*mark(f"load_{name}", ("loaded", name), by=16))

            load(h[:, :, :], io["x"][0].rearrange("(t p) d -> p t d", p=P), "x")
            load(ident[:, :], io["c_ident"], "ident")

            def panel(n):
                stage, i, name, kind, (idx, where) = PANELS[n]
                w = io[name]
                for j in idx:
                    w = w[j]
                slot = n % RAW
                if n >= RAW:
                    sp.wait_ge(*at(("lo", n - RAW)))
                if kind in ("BT", "BF"):
                    src = w[where:where + 256, :].rearrange("(k p) n -> p k n", p=P)
                    sp.dma_start(raw[slot][:, :].rearrange("p (k n) -> p k n", k=2), src).then_inc(*mark(f"panel_loaded{slot}", ("raw", n), by=16))
                elif stage.startswith("up"):
                    dst = raw[slot][:, :].rearrange("p (k c n) -> p k c n", k=KT, c=2)
                    for c in range(2):
                        a = where + c * D_FF
                        sp.dma_start(dst[:, :, c, :], w[:, a:a + P].rearrange("(k p) n -> p k n", p=P)).then_inc(*mark(f"panel_loaded{slot}", ("raw", n), by=16))
                else:
                    src = w[:, where:where + 256].rearrange("(k p) n -> p k n", p=P)
                    sp.dma_start(raw[slot][:, :].rearrange("p (k n) -> p k n", k=KT), src).then_inc(*mark(f"panel_loaded{slot}", ("raw", n), by=16))

            for n in range(len(PANELS)):
                panel(n)
                if n == 2:
                    load(masks[:, :, :].rearrange("p a b -> p (a b)"), io["c_levels"], "levels")
                    load(reset[:, :], io["c_reset"], "reset")
                    load(tri[:, :], io["c_tri"], "tri")
            for tok in range(TT):
                sp.wait_ge(*at(("result", tok)))
                sp.dma_start(out_ap[0].rearrange("(t p) d -> p t d", p=P)[:, tok, :], result[:, tok, :]).then_inc(*mark("stored", ("stored", tok), by=16))
            sp.wait_ge(*at(("stored", 1)))

        @block.gpsimd
        def _(pool):
            def load(dst, src, name):
                pool.dma_start(dst, src).then_inc(*mark(f"load_{name}", ("loaded", name), by=16))

            def rows(name, pre):
                a = io[name]
                for j in pre:
                    a = a[j]
                return a

            def earlier_only(buf, hd, name, event):
                v = buf[:, hd, :].rearrange("p (a c) -> p a c", a=3)[:, 0:3:2, :]
                pool.affine_select(out=v, in_=v, compare_op=ALU.is_gt, fill=0.0, base=0, pattern=[[0, 2], [1, P]], channel_multiplier=-1).then_inc(*mark(name, event))

            vrow = xn[:, 0, 0:640].rearrange("p (g c) -> p g c", g=5)
            for name, pre, r0, n in VEC_LOADS:
                src, g, q = rows(name, pre), r0 // P, r0 % P
                if name in ("q_norm", "k_norm"):
                    for k in range(2):
                        load(vrow[q:q + 1, g, 64 * k:64 * k + 64], src.rearrange("(a c) -> a c", a=1), "vectors")
                else:
                    load(vrow[q:q + n, g, :], src.rearrange("(a c) -> a c", c=P), "vectors")
            pool.memset(minus_half, -0.5).then_inc(*mark("pool_const", ("half",)))
            pool.memset(ones[:, :], 1.0).then_inc(*mark("pool_const", ("ones",)))
            for step in SCHEDULE:
                kind, args = step[0], step[1:]
                if kind == "stats":
                    k = args[0]
                    pool.wait_ge(*at(("half",)))
                    pool.wait_ge(*at(("ms", k)))
                    pool.tensor_tensor(rstd[k], mean_sq[k], minus_half, ALU.pow).then_inc(*mark("rstd", ("rstd", k)))
                elif kind == "hg_level":
                    li = args[0]
                    if li >= 1:
                        for j in range(2):
                            a = blocks_of(sc, 2 * j)
                            pool.wait_ge(*at(("prod", li, j)))
                            pool.tensor_tensor(a, a, blocks_of_prod(j), ALU.add).then_inc(*mark("scores_summed", ("sc", li, j)))
                elif kind == "sb_log":
                    for hd in range(SB_HEADS):
                        pool.wait_ge(*at(("splus", hd // 2)))
                        earlier_only(sp_, hd, "softplus_masked", ("spm", hd // 2))
                elif kind == "sb_weights":
                    i = args[0]
                    pool.wait_ge(*at(("w", i)))
                    for r in range(2):
                        earlier_only(zs, 2 * i + r, "weights_masked", ("wm", i))
                elif kind == "bias":
                    pool.wait_ge(*at(("ev", last_of("wo0"))))
                    load(relb[:, :], io["rel_bias"], "rel")
                    load(buck[:, :], io["c_bucket"], "buck")
                    load(sinks, bass.AP(tensor=io["sinks"].tensor, offset=0, ap=[[0, P], [1, SW_HEADS]]), "sinks")
                    pool.memset(brow[:, :], NEG).then_inc(*mark("bias_row_clear", ("brow0",)))
                    pool.wait_ge(*at(("brow",)))
                    load(scratch, brow[:, :].rearrange("h (a c) -> h a c", a=1).to_broadcast([SW_HEADS, P, BW]), "bias_rows")
                    pool.wait_ge(*at(("loaded", "bias_rows")))
                    load(bias[:, :, :], bass.AP(tensor=scratch.tensor, offset=P - 1, ap=[[BW - 1, P], [P * BW, SW_HEADS], [1, T]]), "bias")
                elif kind == "ple_input":
                    l = args[0]
                    if l == 1:
                        pool.wait_ge(*at(("pt", 0, 1)))
                    pool.dma_start(praw[:, :, :], io["p"][l, 0].rearrange("(t p) d -> p t d", p=P)).then_inc(*mark("load_p", ("loaded", "p", l), by=16))
                    if l == 1:
                        pool.wait_ge(*at(("pe", last_of("down1"))))
                        load(mem[:, :, :], io["mem_2"][0].rearrange("(t p) d -> p t d", p=P), "mem")
                elif kind == "turn" and args[0] == "blk2":
                    pool.wait_ge(*at(("tr", "blk2", 3)))
                    pool.wait_ge(*at(("ev", last_of("gate1"))))
                    load(wsp_raw, io["w_spatial_2"][0].rearrange("g t s -> t g s"), "wsp")
                    load(bsp[:, :, :].rearrange("p g t -> p (g t)"),
                         bass.AP(tensor=io["b_spatial_2"].tensor, offset=0, ap=[[0, P], [1, GROUPS * P]]), "bsp")
                    load(causal[:, :], io["c_causal"], "causal")
                    load(small[:, 0:64], io["c_rope"], "rope")
                    pool.wait_ge(*at(("loaded", "wsp")))
                    pool.affine_select(out=wsp_raw, in_=wsp_raw, compare_op=ALU.is_ge, fill=0.0, base=0, pattern=[[0, GROUPS], [-1, P]], channel_multiplier=1).then_inc(*mark("spatial_masked", ("wspm",)))
                elif kind == "y_split":
                    pool.wait_ge(*at(("yb", "a", 3)))
                    load(gfin[:, :], bass.AP(tensor=io["final_norm_g_2"].tensor, offset=0, ap=[[0, P], [1, D]]), "gfin")

        @block.tensor
        def _(pe):
            reader = {}

            def claim(b, event):
                if b in reader:
                    pe.wait_ge(*at(reader[b]))
                reader[b] = event

            def panel(n):
                stage, i, name, kind, _where = PANELS[n]
                xh, xl, k0, needs = XIN[stage]
                wh, wl = whi[n % RING], wlo[n % RING]
                pe.wait_ge(*at(("lo", n)))
                for before in needs:
                    pe.wait_ge(*at(before))
                if kind == "T":
                    b = pb(n)
                    claim(b, ("ev", n) if not stage.startswith("gate") else ("a", n))
                    wv = [w[:, :].rearrange("p (k n) -> p k n", k=KT) for w in (wh, wl)]
                    for t in range(TT):
                        for k in range(KT):
                            for m, (x, w) in enumerate(((xh, 0), (xh, 1), (xl, 0))):
                                mm = pe.matmul(bank[b][:, t * 256:t * 256 + 256], x[:, k, t * P:(t + 1) * P], wv[w][:, k, :],
                                               start=(k == 0 and m == 0), stop=(k == KT - 1 and m == 2))
                elif kind == "F":
                    b = pb(n)
                    claim(b, ("ev", n))
                    wv = [w[:, :].rearrange("p (k n) -> p k n", k=KT) for w in (wh, wl)]
                    for c in range(2):
                        for k in range(KT):
                            for m, (x, w) in enumerate(((xh, 0), (xl, 0), (xh, 1))):
                                mm = pe.matmul(bank[b][:, c * 256:c * 256 + 256], wv[w][:, k, c * P:(c + 1) * P], x[:, k, :],
                                               start=(k == 0 and m == 0), stop=(k == KT - 1 and m == 2))
                elif kind == "BT":
                    last = n == last_of(stage)
                    if i == 0:
                        for b in range(4):
                            claim(b, ("h", stage, b // 2) if stage.startswith("down") else ("ev", last_of(f"gate{stage[-1]}")))
                    wv = [w[:, :].rearrange("p (k n) -> p k n", k=2) for w in (wh, wl)]
                    for t in range(TT):
                        for k in range(2):
                            for m, (x, w) in enumerate(((xh, 0), (xh, 1), (xl, 0))):
                                for half in range(2):
                                    mm = pe.matmul(bank[2 * t + half][:, :], x[:, 2 * i + k, t * P:(t + 1) * P],
                                                   wv[w][:, k, half * 512:half * 512 + 512],
                                                   start=(i == 0 and k == 0 and m == 0), stop=(last and k == 1 and m == 2))
                        if last and t == 0:
                            mm.then_inc(*mark("product", ("tok0", stage)))
                else:
                    last = n == last_of(stage)
                    if i == 0:
                        for b in range(4):
                            claim(b, ("yb", stage[-1], b))
                    wv = [w[:, :].rearrange("p (k n) -> p k n", k=2) for w in (wh, wl)]
                    for f in range(KT):
                        for k in range(2):
                            for m, (x, w) in enumerate(((xh, 0), (xl, 0), (xh, 1))):
                                mm = pe.matmul(bank[f // 2][:, (f % 2) * 256:(f % 2) * 256 + 256],
                                               wv[w][:, k, f * P:(f + 1) * P], x[:, k0 + 2 * i + k, :],
                                               start=(i == 0 and k == 0 and m == 0 and f % 2 == 0),
                                               stop=(last and k == 1 and m == 2), skip_group_check=True)
                mm.then_inc(*mark("product", ("pe", n)))

            def turn(k):
                src = mem if k == "mem" else xn
                pe.wait_ge(*at(("loaded", "ident")))
                pe.wait_ge(*at(("xn", k, 0)))
                pe.wait_ge(*at(("xn", k, 1)))
                for j in range(4):
                    claim(4 + j, ("xl", k, j))
                    for q in range(2):
                        for t in range(TT):
                            kt = 2 * j + q
                            mm = pe.transpose(bank[4 + j][:, q * 256 + t * P:q * 256 + (t + 1) * P],
                                              src[:, t, kt * P:(kt + 1) * P], ident[:, :])
                    mm.then_inc(*mark("turned", ("tr", k, j)))

            def three_blocks(b, src, width):
                pe.transpose(bank[b][:, 0:P], src[:, 0, 0:P], ident[:, :])
                pe.transpose(bank[b][:, P:2 * P], src[:, 1, 0:P], ident[:, :])
                return pe.transpose(bank[b][:, 2 * P:3 * P], src[:, 1, P:2 * P], ident[:, :])

            def weigh(dst, v0, v1, w):
                pe.matmul(dst(0), v0, w[:, 0:2 * P], start=True, stop=False)
                return pe.matmul(dst(P), v1, w[:, 2 * P:3 * P], start=False, stop=True)

            for step in SCHEDULE:
                kind, args = step[0], step[1:]
                if kind == "panel":
                    panel(args[0])
                elif kind == "setup":
                    pe.wait_ge(*at(("loaded", "ident")))
                    pe.wait_ge(*at(("loaded", "vectors")))
                    for g in range(5):
                        b, c, n = (4, g * P, VEC_ROWS[g]) if g < 4 else (5, 0, VEC_ROWS[g])
                        if c == 0:
                            claim(b, ("vec", 3 if g == 0 else 4))
                        mm = pe.transpose(bank[b][:, c:c + n], xn[0:n, 0, g * P:(g + 1) * P], ident[0:n, 0:n])
                        if g >= 3:
                            mm.then_inc(*mark("turned", ("tr", "vec", g)))
                elif kind == "turn":
                    turn(args[0])
                elif kind == "hg_level":
                    li = args[0]
                    if li < 0:
                        pe.wait_ge(*at(("xs", li)))
                        claim(0, ("sc", -1, 0))
                        for hd in range(HG_HEADS):
                            X = xs_buf[1]
                            mm = pe.matmul(bank[0][:, hd * P:(hd + 1) * P], X[:, hd, 0:P], X[:, hd, P:T], start=True, stop=True)
                        mm.then_inc(*mark("scores", ("ps", -1, 0)))
                    else:
                        if LEVELS[li]:
                            pe.wait_ge(*at(("xs", li)))
                            A = B = xs_buf[li % 2]
                        else:
                            pe.wait_ge(*at(("kk",)))
                            A, B = kk, qf
                        for j in range(2):
                            b = (2 * li + j + 2) % 4
                            claim(b, ("prod", li, j))
                            for q in range(2):
                                for t in range(TT):
                                    hd = 2 * j + q
                                    mm = pe.matmul(bank[b][:, (2 * q + t) * P:(2 * q + t + 1) * P],
                                                   A[:, hd, t * P:(t + 1) * P], B[:, hd, t * P:(t + 1) * P], start=True, stop=True)
                            mm.then_inc(*mark("scores", ("ps", li, j)))
                elif kind == "hg_out":
                    pe.wait_ge(*at(("sc", len(LEVELS) - 1, 1)))
                    pe.wait_ge(*at(("sc", -1, 0)))
                    pe.wait_ge(*at(("ev", last_of("ib"))))
                    for t in range(TT):
                        claim(t, ("on", t))
                        for hd in range(HG_HEADS):
                            o, v = bank[t][:, hd * P:(hd + 1) * P], ib[:, :, hd * P:(hd + 1) * P]
                            if t == 0:
                                mm = pe.matmul(o, sc[:, hd, 0:P], v[:, 0, :], start=True, stop=True)
                            else:
                                pe.matmul(o, sc[:, hd, P:2 * P], v[:, 0, :], start=True, stop=False)
                                mm = pe.matmul(o, sc[:, hd, 2 * P:3 * P], v[:, 1, :], start=False, stop=True)
                        mm.then_inc(*mark("weighted", ("hgo", t)))
                elif kind == "hg_turn":
                    pe.wait_ge(*at(("gated", 0)))
                    pe.wait_ge(*at(("gated", 1)))
                    for j in range(2):
                        claim(2 + j, ("xl", "hg", j))
                        for q in range(2):
                            for t in range(TT):
                                mm = pe.transpose(bank[2 + j][:, q * 256 + t * P:q * 256 + (t + 1) * P], on[:, t, 2 * j + q, :], ident[:, :])
                        mm.then_inc(*mark("turned", ("tr", "hg", j)))
                elif kind == "sb_scores":
                    i = args[0]
                    pe.wait_ge(*at(("ev", last_of("qa"))))
                    pe.wait_ge(*at(("ev", last_of("ka"))))
                    for r in range(2):
                        hd = 2 * i + r
                        b, q = 4 + hd % 4, slice(64 * r, 64 * r + 64)
                        claim(b, ("z", hd))
                        pe.matmul(bank[b][:, 0:T], kaT[q, i, 0:P], qaT[q, i, :], start=True, stop=True)
                        mm = pe.matmul(bank[b][:, T:T + P], kaT[q, i, P:T], qaT[q, i, P:T], start=True, stop=True)
                        mm.then_inc(*mark("scores", ("sbz", hd)))
                elif kind == "sb_weights":
                    i = args[0]
                    pe.wait_ge(*at(("spm", i)))
                    pe.wait_ge(*at(("loaded", "tri")))
                    pe.wait_ge(*at(("ones",)))
                    for r in range(2):
                        hd = 2 * i + r
                        b, a = 4 + hd % 4, sp_[:, hd, :]
                        claim(b, ("d", hd))
                        pe.matmul(bank[b][:, 0:T], tri[:, :], a[:, 0:T], start=True, stop=False)
                        pe.matmul(bank[b][:, P:T], ones[:, :], a[:, T:T + P], start=False, stop=True)
                        mm = pe.matmul(bank[b][:, T:T + P], tri[:, :], a[:, T:T + P], start=True, stop=True)
                        mm.then_inc(*mark("weighted", ("sbr", hd)))
                elif kind == "sb_out":
                    i = args[0]
                    b = 4 + i
                    pe.wait_ge(*at(("wm", i)))
                    pe.wait_ge(*at(("ev", last_of("va"))))
                    claim(b, ("xl", "sb", i))
                    for r in range(2):
                        hd = 2 * i + r
                        mm = weigh(lambda c: bank[b][64 * r:64 * r + 64, c:T], va[:, 0, hd * 64:hd * 64 + 64],
                                   va[:, 1, hd * 64:hd * 64 + 64], zs[:, hd, :])
                    mm.then_inc(*mark("weighted", ("sbo", i)))
                elif kind == "ple_input":
                    l = args[0]
                    pe.wait_ge(*at(("loaded", "p", l)))
                    claim(4, ("ptl", l))
                    for q in range(2):
                        for t in range(TT):
                            mm = pe.transpose(bank[4][:, q * 256 + t * P:q * 256 + (t + 1) * P], praw[:, t, q * P:(q + 1) * P], ident[:, :])
                    mm.then_inc(*mark("turned", ("pt", l, 1)))
                elif kind == "bias":
                    pe.wait_ge(*at(("loaded", "rel")))
                    pe.wait_ge(*at(("loaded", "buck")))
                    claim(0, ("brow",))
                    pe.matmul(bank[0][0:16, 0:P], relb[:, :], buck[:, :], start=True, stop=True).then_inc(*mark("weighted", ("brp",)))
                elif kind == "sw_norm":
                    for j in range(6):
                        if j % 4 == 0 or j == 4:
                            pe.wait_ge(*at(("qkn", 0)))
                            pe.wait_ge(*at(("qkn", 1)))
                        b = 4 + j % 4
                        claim(b, ("qsT", j))
                        for q in range(2):
                            for t in range(TT):
                                mm = pe.transpose(bank[b][:, q * 256 + t * P:q * 256 + (t + 1) * P],
                                                  qkn[:, t, 4 * j + 2 * q:4 * j + 2 * q + 2, :].rearrange("p a d -> p (a d)"), ident[:, :])
                        mm.then_inc(*mark("turned", ("tr", "sw", j)))
                elif kind == "sw_logits":
                    g = args[0]
                    pe.wait_ge(*at(("qsT", 5)))
                    for j in range(4):
                        hd = 4 * g + j
                        q = slice(64 * (hd % 2), 64 * (hd % 2) + 64)
                        claim(j, ("swm", g, j))
                        pe.matmul(bank[j][:, 0:P], qsT[q, hd // 2, 0:P], ksT[q, g, 0:P], start=True, stop=True)
                        mm = pe.matmul(bank[j][:, T:2 * T], qsT[q, hd // 2, P:T], ksT[q, g, :], start=True, stop=True)
                        mm.then_inc(*mark("scores", ("swz", g, j)))
                elif kind == "sw_weights":
                    g = args[0]
                    for j in range(4):
                        pe.wait_ge(*at(("swn", g, j)))
                        claim(4 + j, ("swt", g, j))
                        three_blocks(4 + j, le_s[:, j, :, :], T).then_inc(*mark("turned", ("tr", "sww", g, j)))
                elif kind == "sw_out":
                    g = args[0]
                    for q in range(2):
                        pe.wait_ge(*at(("swt", g, 2 * q)))
                        pe.wait_ge(*at(("swt", g, 2 * q + 1)))
                        pe.wait_ge(*at(("ev", last_of("vs"))))
                        claim(q, ("xl", "sw", 2 * g + q))
                        for r in range(2):
                            mm = weigh(lambda c: bank[q][64 * r:64 * r + 64, c:T], vsw[:, 0, 64 * g:64 * g + 64],
                                       vsw[:, 1, 64 * g:64 * g + 64], wT_s[:, 2 * q + r, :])
                        mm.then_inc(*mark("weighted", ("swo", 2 * g + q)))
                elif kind == "x_logits":
                    g = args[0]
                    pe.wait_ge(*at(("ev", last_of("mk"))))
                    pe.wait_ge(*at(("ev", last_of("qc"))))
                    for j in range(2):
                        hd = 2 * g + j
                        claim(j, ("e", "x", hd))
                        for t in range(TT):
                            mm = pe.matmul(bank[j][:, t * T:(t + 1) * T], qc[:, hd, t * P:(t + 1) * P], mk[:, hd, :], start=True, stop=True)
                        mm.then_inc(*mark("scores", ("xz", hd)))
                elif kind == "x_weights":
                    g = args[0]
                    for j in range(2):
                        hd = 2 * g + j
                        pe.wait_ge(*at(("n", "x", hd)))
                        claim(2 + j, ("wT", "x", hd))
                        for m in range(2):
                            for t in range(TT):
                                mm = pe.transpose(bank[2 + j][:, m * T + t * P:m * T + (t + 1) * P], le[:, j, t, m * P:(m + 1) * P], ident[:, :])
                        mm.then_inc(*mark("turned", ("trw", "x", hd)))
                elif kind == "x_out":
                    g = args[0]
                    for j in range(2):
                        hd = 2 * g + j
                        pe.wait_ge(*at(("wT", "x", hd)))
                        pe.wait_ge(*at(("ev", last_of("mv"))))
                        claim(j, ("og", "c", hd))
                        for m in range(2):
                            mm = pe.matmul(bank[j][:, 0:T], mv[:, m, hd * P:(hd + 1) * P], wT[:, j, m, :], start=(m == 0), stop=(m == 1))
                        mm.then_inc(*mark("weighted", ("oz", "c", hd)))
                elif kind == "rope_turn":
                    pe.wait_ge(*at(("roped",)))
                    for j in range(6):
                        b = 2 + j % 2
                        claim(b, ("qkF", j))
                        for q in range(2):
                            for t in range(TT):
                                c = (2 * j + q) * P
                                mm = pe.transpose(bank[b][:, q * T + t * P:q * T + (t + 1) * P], qkm[:, t, c:c + P], ident[:, :])
                        mm.then_inc(*mark("turned", ("tr", "rope", j)))
                elif kind == "spatial":
                    pe.wait_ge(*at(("wspm",)))
                    for j in range(2):
                        claim(2 + j, ("wspT", j))
                        for q in range(3):
                            mm = pe.transpose(bank[2 + j][:, q * P:(q + 1) * P], wsp_raw[:, 3 * j + q, :], ident[:, :])
                        mm.then_inc(*mark("turned", ("tr", "wsp", j)))
                elif kind == "a_logits":
                    g = args[0]
                    pe.wait_ge(*at(("qkF", 4)))
                    pe.wait_ge(*at(("qkF", 5)))
                    for j in range(2):
                        hd = 2 * g + j
                        claim(j, ("am", hd))
                        pe.matmul(bank[j][:, 0:P], qF[:, hd, 0:P], kF[:, hd, 0:P], start=True, stop=True)
                        mm = pe.matmul(bank[j][:, T:2 * T], qF[:, hd, P:T], kF[:, hd, :], start=True, stop=True)
                        mm.then_inc(*mark("scores", ("az", hd)))
                elif kind == "a_weights":
                    g = args[0]
                    for j in range(2):
                        hd = 2 * g + j
                        pe.wait_ge(*at(("n", "a", hd)))
                        claim(2 + j, ("wT", "a", hd))
                        three_blocks(2 + j, le[:, j, :, :], T).then_inc(*mark("turned", ("trw", "a", hd)))
                elif kind == "a_out":
                    g = args[0]
                    for j in range(2):
                        hd = 2 * g + j
                        pe.wait_ge(*at(("wT", "a", hd)))
                        pe.wait_ge(*at(("ev", last_of("va2"))))
                        claim(j, ("og", "a", hd))
                        w = wT[:, j, :, :].rearrange("p a b -> p (a b)")
                        mm = weigh(lambda c: bank[j][:, c:T], va2[:, 0, hd * P:(hd + 1) * P], va2[:, 1, hd * P:(hd + 1) * P], w)
                        mm.then_inc(*mark("weighted", ("oz", "a", hd)))
                elif kind == "mixed":
                    pe.wait_ge(*at(("vn", 0)))
                    pe.wait_ge(*at(("vn", 1)))
                    pe.wait_ge(*at(("wspT", 0)))
                    pe.wait_ge(*at(("wspT", 1)))
                    for j in range(3):
                        claim(j, ("mixg", 2 * j + 1))
                        for q in range(2):
                            g = 2 * j + q
                            for t in range(TT):
                                mm = pe.matmul(bank[j][:, q * T + t * P:q * T + (t + 1) * P], vb[:, t, g * P:(g + 1) * P], wsp[:, g, :], start=True, stop=True)
                        mm.then_inc(*mark("weighted", ("mixp", j)))

        @block.scalar
        def _(act):
            def split(n):
                if n < len(PANELS):
                    act.wait_ge(*at(("raw", n)))
                    if n >= RING:
                        act.wait_ge(*at(("pe", n - RING)))
                    act.activation(whi[n % RING][:, :], raw[n % RAW][:, :], ACT.Copy).then_inc(*mark("weights_hi", ("hi", n)))

            def parts(src, gain, dst, event, *first):
                for before in first:
                    act.wait_ge(*at(before))
                if gain is None:
                    act.activation(dst, src, ACT.Copy).then_inc(*mark("input_hi", event))
                else:
                    act.activation(dst, src, ACT.Copy, scale=gain).then_inc(*mark("input_hi", event))

            def ffn_gate(l, i):
                act.wait_ge(*at(("conv", l, i)))
                if l > 0 or i >= 2:
                    act.wait_ge(*at(("gf", l, i - 2) if i >= 2 else ("gf", l - 1, FT - 2 + i)))
                act.activation(sgate[i % 2][:, :], cc[i % 3][:, 0, :], ACT.Silu).then_inc(*mark("gate_done", ("sg", l, i)))

            def ffn_hi(l, i):
                act.wait_ge(*at(("gf", l, i)))
                act.activation(GH[:, i, :], gf[i % 2][:, :], ACT.Copy).then_inc(*mark("gated_hi", ("gh", l, i)))

            def panel(n):
                stage, i, name, kind, _where = PANELS[n]
                b = pb(n)
                c2, cT = slice(2 * i, 2 * i + 2), slice(256 * i, 256 * i + 256)
                ev = ("ev", n)
                if not (stage[:2] in ("wo", "br", "do", "pp") or stage == "ub"):
                    act.wait_ge(*at(("pe", n)))
                if stage == "qb":
                    act.activation(qf[:, c2, :], two(b), ACT.Silu).then_inc(*mark("projected", ev))
                elif stage == "fb":
                    act.activation(bdec[:, c2, :], two(b), ACT.Sigmoid).then_inc(*mark("projected", ("sig", i)))
                    act.activation(kk[:, c2, :], two(b), ACT.Sigmoid, scale=-1.0).then_inc(*mark("projected", ev))
                elif stage == "ib":
                    act.activation(ib[:, :, cT], two(b), ACT.Copy).then_inc(*mark("projected", ev))
                elif stage == "gb":
                    act.activation(gbs[:, :, cT], two(b), ACT.Silu).then_inc(*mark("projected", ev))
                elif stage == "qa":
                    act.activation(qaT[:, c2, :], two(b), ACT.Copy, scale=SB_DIM ** -0.5).then_inc(*mark("projected", ev))
                elif stage == "ka":
                    act.activation(kaT[:, c2, :], two(b), ACT.Copy).then_inc(*mark("projected", ev))
                elif stage == "va":
                    act.activation(va[:, :, cT], two(b), ACT.Copy).then_inc(*mark("projected", ev))
                elif stage.startswith("up"):
                    l = int(stage[-1])
                    if l > 0 or i >= 3:
                        act.wait_ge(*at(("gf", l, i - 3) if i >= 3 else ("gf", l - 1, FT - 1)))
                    for c in range(2):
                        j = c * FT + i
                        act.activation(cc[i % 3][:, c, :], two(b)[:, c, :], ACT.Identity, scale=vec("ffn_conv", l, 2)(j), bias=vec("ffn_conv_b", l)(j)).then_inc(*mark("projected", ("a", n)))
                elif stage.startswith("gate"):
                    if i >= 2:
                        act.wait_ge(*at(("ev", n - 2)))
                    elif stage == "gate1":
                        act.wait_ge(*at(("ev", last_of("gate0"))))
                    act.activation(gate[i % 2][:, :, :], two(b), ACT.Sigmoid).then_inc(*mark("projected", ("a", n)))
                elif stage in ("qs", "ks"):
                    a = 256 * (n - FIRST["qs"])
                    act.activation(qk[:, :, a:a + 256], two(b), ACT.Copy).then_inc(*mark("projected", ev))
                elif stage == "vs":
                    act.activation(vsw[:, :, :], two(b), ACT.Copy).then_inc(*mark("projected", ev))
                elif stage == "mk":
                    act.activation(mk[:, c2, :], two(b), ACT.Copy).then_inc(*mark("projected", ev))
                elif stage == "mv":
                    act.activation(mv[:, :, cT], two(b), ACT.Copy).then_inc(*mark("projected", ev))
                elif stage == "qc":
                    act.activation(qc[:, c2, :], two(b), ACT.Copy).then_inc(*mark("projected", ev))
                elif stage == "gc":
                    act.activation(gc[:, c2, :], two(b), ACT.Silu).then_inc(*mark("projected", ev))
                elif stage == "qka":
                    act.activation(qkm[:, :, cT], two(b), ACT.Copy).then_inc(*mark("projected", ev))
                elif stage == "va2":
                    act.activation(va2[:, :, cT], two(b), ACT.Copy).then_inc(*mark("projected", ev))
                elif stage == "ga":
                    if i == 0:
                        act.wait_ge(*at(("tr", "rope", 5)))
                    act.activation(ga[:, c2, :], two(b), ACT.Silu).then_inc(*mark("projected", ev))
                elif stage == "vb":
                    act.activation(vb[:, :, cT], two(b), ACT.Copy).then_inc(*mark("projected", ev))
                elif stage == "gb2":
                    act.activation(ubs[:, c2, :], two(b), ACT.Silu).then_inc(*mark("projected", ev))
                elif stage in ("ma", "mb", "mc"):
                    m = msig[stage == "mb"]
                    if stage == "ma" and i == 0:
                        act.wait_ge(*at(("yb", "c", 3)))
                    act.activation(m[:, c2, :], two(b), ACT.Sigmoid).then_inc(*mark("projected", ev))
                split(n + RING)
                if stage.startswith("up"):
                    if i >= 1:
                        ffn_gate(l, i - 1)
                    if i >= 2:
                        ffn_hi(l, i - 2)

            def soft(tag, hd, j, scale):
                act.wait_ge(*at(("neg", tag, hd)))
                for t in range(TT):
                    c = 2 * j + t
                    if tag == "x":
                        src, dst = bank[j][:, t * T:(t + 1) * T], le[:, j, t, :]
                    else:
                        w = slice(0, P) if t == 0 else slice(0, T)
                        src = dst = le[:, j, t, w]
                    act.activation(dst, src, ACT.Exp, scale=scale, bias=s_neg[:, c:c + 1], accum_out=s_sum[:, c:c + 1]).then_inc(*mark("exponentials", ("e", tag, hd)))

            for n in range(RING):
                split(n)
            for step in SCHEDULE:
                kind, args = step[0], step[1:]
                if kind == "panel":
                    panel(args[0])
                elif kind == "setup":
                    for g in range(5):
                        b, c, n = (4, g * P, VEC_ROWS[g]) if g < 4 else (5, 0, VEC_ROWS[g])
                        act.wait_ge(*at(("tr", "vec", max(g, 3))))
                        act.activation(vecs[:, g, 0:n], bank[b][:, c:c + n], ACT.Copy).then_inc(*mark("vectors", ("vec", g)))
                    act.wait_ge(*at(("lb0",)))
                    act.activation(lb_tmp, lb_tmp, ACT.Exp).then_inc(*mark("vectors", ("lbe",)))
                elif kind == "stats":
                    k = args[0]
                    act.wait_ge(*at(READY[k]))
                    src = mem if k == "mem" else h
                    if k == "mix0":
                        act.wait_ge(*at(("tr", "vec", 4)))
                    elif k != "mem":
                        prev = {"ffn0": "mix0", "ple0": "ffn0", "mix1": "ple0", "ffn1": "mix1", "ple1": "ffn1", "blk2": "ple1"}.get(k)
                        if prev:
                            act.wait_ge(*at(("tr", prev, 3)))
                        else:
                            act.wait_ge(*at(("xl", "y", 3)))
                    if k == "mem":
                        act.wait_ge(*at(("pe", last_of("down1"))))
                    for t in range(TT):
                        junk = mem_junk[:, :] if k == "mem" else xn[:, t, :]
                        if k == "mem" and t == 1:
                            act.wait_ge(*at(("sq", k, 0)))
                        act.activation(junk, src[:, t, :], ACT.Square, accum_out=ssq[k][:, t:t + 1]).then_inc(*mark("squared", ("sq", k, t)))
                    act.wait_ge(*at(("rstd", k)))
                    if k == "final":
                        continue
                    dst = mem if k == "mem" else xn
                    act.activation(dst[:, 1, :], src[:, 1, :], ACT.Copy, scale=rstd[k][:, 1:2]).then_inc(*mark("normalized", ("xn", k, 1)))
                elif kind == "turn":
                    k = args[0]
                    if k in XUSED:
                        act.wait_ge(*at(XUSED[k]))
                    act.wait_ge(*at(("vec", 4)))
                    for j in range(4):
                        act.wait_ge(*at(("tr", k, j)))
                        for q in range(2):
                            kt = 2 * j + q
                            act.activation(XH[:, kt, :], two(4 + j)[:, q, :], ACT.Copy, scale=GAIN[k](kt)).then_inc(*mark("input_hi", ("xh", k, j)))
                elif kind == "hg_decay":
                    act.wait_ge(*at(("f",)))
                    act.activation(ex[:, :, :], bdec[:, :, :], ACT.Ln).then_inc(*mark("levels", ("logf",)))
                elif kind == "hg_level":
                    li = args[0]
                    if li < 0 or LEVELS[li]:
                        e = ex if li % 2 == 0 else exb
                        act.wait_ge(*at(("dd", li)))
                        act.activation(e[:, :, :], e[:, :, :], ACT.Exp).then_inc(*mark("levels", ("ex", li)))
                elif kind == "sb_scores":
                    i = args[0]
                    if i == 0:
                        act.wait_ge(*at(("loaded", "reset")))
                    for r in range(2):
                        hd = 2 * i + r
                        b = 4 + hd % 4
                        act.wait_ge(*at(("sbz", hd)))
                        act.activation(sp_[:, hd, :], bank[b][:, 0:384], ACT.Abs).then_inc(*mark("sb_scores", ("az0", hd)))
                        act.activation(zs[:, hd, :], bank[b][:, 0:384], ACT.Copy).then_inc(*mark("sb_scores", ("z", hd)))
                elif kind == "sb_log":
                    for i in range(4):
                        c = slice(2 * i, 2 * i + 2)
                        act.wait_ge(*at(("z", 2 * i + 1)))
                        act.activation(sp_[:, c, :], sp_[:, c, :], ACT.Exp, scale=-1.0).then_inc(*mark("sb_logs", ("sbe", i)))
                    for i in range(4):
                        c = slice(2 * i, 2 * i + 2)
                        act.wait_ge(*at(("sbe", i)))
                        act.activation(sp_[:, c, :], sp_[:, c, :], ACT.Ln, bias=1.0).then_inc(*mark("sb_logs", ("sbl", i)))
                elif kind == "hg_out":
                    for t in range(TT):
                        act.wait_ge(*at(("hgo", t)))
                        if t == 0:
                            act.wait_ge(*at(("sc", len(LEVELS) - 1, 1)))
                        act.activation(prod4[:, t, :], bank[t][:, :], ACT.Square).then_inc(*mark("squared", ("hgsq", t)))
                elif kind == "hg_turn":
                    for j in range(2):
                        parts(two(2 + j), vec("hg_out_norm", 0)(0), XH[:, 4 + 2 * j:6 + 2 * j, :], ("xh", "hg", j),
                              ("tr", "hg", j), ("pe", last_of("va")))
                elif kind == "sb_weights":
                    i = args[0]
                    act.wait_ge(*at(("d", 2 * i + 1)))
                    c = slice(2 * i, 2 * i + 2)
                    act.activation(zs[:, c, :], zs[:, c, :], ACT.Exp).then_inc(*mark("sb_weights", ("w", i)))
                elif kind == "sb_out":
                    i = args[0]
                    parts(bank[4 + i][:, 0:T], None, XH[:, i, :], ("xh", "sb", i), ("sbo", i), ("pe", last_of("va")))
                elif kind == "up_tail":
                    l = args[0]
                    ffn_gate(l, FT - 1)
                    ffn_hi(l, FT - 2)
                    ffn_hi(l, FT - 1)
                elif kind == "ple_input":
                    l = args[0]
                    if l == 1:
                        act.wait_ge(*at(("pe", last_of("pp0"))))
                    parts(two(4), None, PTH[:, :, :], ("pth", l), ("pt", l, 1))
                elif kind == "sw_norm":
                    for t in range(TT):
                        act.wait_ge(*at(("ev", last_of("ks"))))
                        act.activation(sq[:, t, :], qk[:, t, :], ACT.Square).then_inc(*mark("squared", ("swsq", t)))
                    for j in range(6):
                        act.wait_ge(*at(("tr", "sw", j)))
                        if j < 4:
                            act.activation(qsT[:, 2 * j:2 * j + 2, :], two(4 + j % 4), ACT.Copy, scale=q_gain).then_inc(*mark("sw_turned", ("qsT", j)))
                        else:
                            act.activation(ksT[:, 2 * j - 8:2 * j - 6, :], two(4 + j % 4), ACT.Copy, scale=vec("k_norm", 0)(0)).then_inc(*mark("sw_turned", ("qsT", j)))
                elif kind == "sw_logits":
                    g = args[0]
                    act.wait_ge(*at(("swneg", g)))
                    for j in range(4):
                        for t in range(TT):
                            c = 2 * j + t
                            v = le_s[:, j, t, 0:P if t == 0 else T]
                            act.activation(v, v, ACT.Exp, bias=s_neg[:, c:c + 1], accum_out=s_sum[:, c:c + 1]).then_inc(*mark("exponentials", ("swe", g, j)))
                    act.activation(s_exp, s_exp, ACT.Exp).then_inc(*mark("exponentials", ("swx", g)))
                elif kind == "sw_weights":
                    g = args[0]
                    for j in (0, 2):
                        act.wait_ge(*at(("tr", "sww", g, j)))
                        if g:
                            act.wait_ge(*at(("swo", 2 * g - 1)))
                        act.activation(wT_s[:, j, :], bank[4 + j][:, 0:384], ACT.Copy).then_inc(*mark("turned_copied", ("swt", g, j)))
                elif kind == "sw_out":
                    g = args[0]
                    for q in range(2):
                        parts(bank[q][:, 0:T], None, XH[:, 2 * g + q, :], ("xh", "sw", 2 * g + q), ("swo", 2 * g + q), ("pe", last_of("vs")))
                elif kind == "x_logits":
                    g = args[0]
                    for j in range(2):
                        soft("x", 2 * g + j, j, HEAD ** -0.5)
                elif kind == "a_logits":
                    g = args[0]
                    for j in range(2):
                        soft("a", 2 * g + j, j, HEAD ** -0.5)
                elif kind in ("x_weights", "a_weights"):
                    tag, g = kind[0], args[0]
                    hd = 2 * g
                    act.wait_ge(*at(("trw", tag, hd)))
                    if tag == "x" and g:
                        act.wait_ge(*at(("oz", "c", hd - 1)))
                    elif tag == "a":
                        act.wait_ge(*at(("oz", "a", hd - 1) if g else ("oz", "c", X_HEADS - 1)))
                    n = 2 * T if tag == "x" else 384
                    act.activation(wT[:, 0, :, :].rearrange("p a b -> p (a b)")[:, 0:n], bank[2][:, 0:n], ACT.Copy).then_inc(*mark("turned_copied", ("wT", tag, hd)))
                elif kind in ("x_out", "a_out"):
                    b, g = ("c" if kind[0] == "x" else "a"), args[0]
                    src = gc if b == "c" else ga
                    for j in range(2):
                        hd = 2 * g + j
                        act.wait_ge(*at(("og", b, hd)))
                        act.wait_ge(*at(("xn", "mem", 1)))
                        act.wait_ge(*at(("pe", last_of("down1"))))
                        act.activation(GH[:, OUT_AT[b] + hd, :], src[:, hd, :], ACT.Copy).then_inc(*mark("gated_hi", ("oh", b, hd)))
                elif kind == "rope_turn":
                    for j in (0, 2, 4):
                        act.wait_ge(*at(("tr", "rope", j)))
                        dst = qF if j < 3 else kF
                        act.activation(dst[:, (2 * j) % 6:(2 * j) % 6 + 2, :], two(2), ACT.Copy).then_inc(*mark("turned_copied", ("qkF", j)))
                elif kind == "spatial":
                    for j in range(2):
                        act.wait_ge(*at(("tr", "wsp", j)))
                        act.activation(wsp[:, 3 * j:3 * j + 3, :].rearrange("p g t -> p (g t)"), bank[2 + j][:, 0:384], ACT.Copy).then_inc(*mark("turned_copied", ("wspT", j)))
                elif kind == "layer_norm":
                    act.wait_ge(*at(("roped",)))
                    act.wait_ge(*at(("tr", "wsp", 1)))
                    for t in range(TT):
                        act.wait_ge(*at(("lnm",)))
                        act.activation(xn[:, t, 0:768], vb[:, t, :], ACT.Square, bias=ln_neg[:, t:t + 1], accum_out=ln_ss[:, t:t + 1]).then_inc(*mark("squared", ("lnsq", t)))
                elif kind == "mixed":
                    for g in range(GROUPS):
                        act.wait_ge(*at(("og", "b", g)))
                        act.activation(GH[:, OUT_AT["b"] + g, :], ubs[:, g, :], ACT.Copy).then_inc(*mark("gated_hi", ("oh", "b", g)))
                elif kind == "y_split":
                    for j in range(4):
                        parts(y[:, 2 * j:2 * j + 2, :], None, XH[:, 2 * j:2 * j + 2, :], ("xh", "y", j), ("yb", "a", j), ("pe", last_of("ma")))

        @block.vector
        def _(dve):
            def split(n):
                if n < len(PANELS):
                    dve.wait_ge(*at(("hi", n)))
                    dve.tensor_tensor(wlo[n % RING][:, :], raw[n % RAW][:, :], plain(whi[n % RING][:, :]), ALU.subtract).then_inc(*mark("weights_lo", ("lo", n)))

            def rest(src, gain, hi, lo, name, event, *first):
                for before in first:
                    dve.wait_ge(*at(before))
                if gain is None:
                    return dve.tensor_tensor(lo, src, plain(hi), ALU.subtract).then_inc(*mark(name, event))
                return dve.scalar_tensor_tensor(lo, src, gain, plain(hi), ALU.mult, ALU.subtract).then_inc(*mark(name, event))

            def inverse_root(x, out, tmp):
                dve.tensor_scalar(tmp.bitcast(I32), x.bitcast(I32), 1, None, ALU.logical_shift_right).then_inc(*chained())
                dve.wait_ge(*chain())
                dve.tensor_scalar(out.bitcast(I32), tmp.bitcast(I32), -1.0, MAGIC, ALU.mult, ALU.add).then_inc(*chained())
                dve.wait_ge(*chain())
                for _ in range(3):
                    dve.tensor_tensor(tmp, out, out, ALU.mult).then_inc(*chained())
                    dve.wait_ge(*chain())
                    dve.scalar_tensor_tensor(tmp, x, -0.5, tmp, ALU.mult, ALU.mult).then_inc(*chained())
                    dve.wait_ge(*chain())
                    dve.scalar_tensor_tensor(out, tmp, 1.5, out, ALU.add, ALU.mult).then_inc(*chained())
                    dve.wait_ge(*chain())

            def hg_level(li):
                if li < 0 or LEVELS[li]:
                    e = ex if li % 2 == 0 else exb
                    X = xs_buf[li % 2]
                    half = LEVELS[li] if li >= 0 else P
                    if li >= 1 or li == 0:
                        for before in ([("xs", li - 2)] if li >= 1 else []):
                            dve.wait_ge(*at(before))
                    if half >= HG_CHUNK:
                        ends = [bdec[:, :, HG_CHUNK * (c + 1) - 1:HG_CHUNK * (c + 1)].to_broadcast([P, HG_HEADS, HG_CHUNK]) for c in range(4)]
                        part = lambda x, c: x[:, :, HG_CHUNK * c:HG_CHUNK * (c + 1)]
                        left = (0, 1) if half == P else (0, 2)
                        for c in range(4):
                            if c in left:
                                dve.tensor_tensor(part(e, c), ends[c], part(bdec, c), ALU.subtract).then_inc(*mark("exponents", ("dd_left", li), ("dd", li)))
                            elif half == P and c == 3:
                                dve.tensor_tensor(part(e, c), ends[2], part(bdec, c), ALU.add).then_inc(*mark("exponents", ("dd", li)))
                            else:
                                dve.tensor_copy(part(e, c), part(bdec, c)).then_inc(*mark("exponents", ("dd", li)))
                        if half == P:
                            dve.wait_ge(*at(("dd_left", li)))
                            dve.tensor_tensor(part(e, 0), part(e, 0), ends[1], ALU.add).then_inc(*mark("exponents", ("dd", li)))
                    else:
                        halves = lambda x: x[:, :, :].rearrange("p h (n c) -> p (h n) c", c=2 * half)
                        mid = halves(bdec)[:, :, half - 1:half].to_broadcast([P, HG_HEADS * T // (2 * half), half])
                        l, r = halves(bdec)[:, :, 0:half], halves(bdec)[:, :, half:2 * half]
                        dve.tensor_tensor(halves(e)[:, :, 0:half], mid, l, ALU.subtract).then_inc(*mark("exponents", ("dd0", li)))
                        dve.tensor_tensor(halves(e)[:, :, half:2 * half], r, mid, ALU.subtract).then_inc(*mark("exponents", ("dd", li)))
                    dve.wait_ge(*at(("ex", li)))
                    if li >= 1:
                        dve.wait_ge(*at(("ps", li - 2, 1 if li >= 2 else 0)))
                    halves = lambda x: x[:, :, :].rearrange("p h (n c) -> p (h n) c", c=2 * half)
                    dve.tensor_tensor(halves(X)[:, :, 0:half], halves(e)[:, :, 0:half], halves(kk)[:, :, 0:half], ALU.mult).then_inc(*mark("decayed", ("xs0", li)))
                    dve.tensor_tensor(halves(X)[:, :, half:2 * half], halves(e)[:, :, half:2 * half], halves(qf)[:, :, half:2 * half], ALU.mult).then_inc(*mark("decayed", ("xs", li)))
                if li < 0:
                    dve.wait_ge(*at(("ps", li, 0)))
                    dve.tensor_copy(sc[:, :, P:2 * P], bank[0][:, :].rearrange("p (h c) -> p h c", h=HG_HEADS)).then_inc(*mark("cross_scores", ("sc", -1, 0)))
                    return
                dve.wait_ge(*at(("loaded", "levels")))
                for j in range(2):
                    b = (2 * li + j + 2) % 4
                    dve.wait_ge(*at(("ps", li, j)))
                    for before in ([("sc", li - 1, j)] if li >= 2 else []):
                        dve.wait_ge(*at(before))
                    out = blocks_of(sc, 2 * j) if li == 0 else blocks_of_prod(j)
                    mask = masks[:, li, :].rearrange("p (a b c) -> p a b c", a=1, b=1).to_broadcast([P, 2, 2, P])
                    events = [("prod", li, j)] + ([("sc", 0, j)] if li == 0 else [])
                    dve.tensor_tensor(out, bank[b][:, :].rearrange("p (h t c) -> p h t c", h=2, t=2), mask, ALU.mult).then_inc(*mark("masked_scores", *events))

            def ffn_mul(l, i):
                dve.wait_ge(*at(("sg", l, i)))
                if i >= 2:
                    dve.wait_ge(*at(("gl", l, i - 2)))
                elif l:
                    dve.wait_ge(*at(("gl", l - 1, FT - 2 + i)))
                dve.tensor_tensor(gf[i % 2][:, :], sgate[i % 2][:, :], cc[i % 3][:, 1, :], ALU.mult).then_inc(*mark("gated", ("gf", l, i)))

            def ffn_lo(l, i):
                rest(gf[i % 2][:, :], None, GH[:, i, :], GL[:, i, :], "gated_lo", ("gl", l, i), ("gh", l, i))

            def panel(n):
                stage, i, name, kind, _where = PANELS[n]
                b = pb(n)
                c2, cT = slice(2 * i, 2 * i + 2), slice(256 * i, 256 * i + 256)
                ev = ("ev", n)
                if stage.startswith("wo"):
                    dve.wait_ge(*at(("pe", n)))
                    dve.tensor_tensor(h[:, :, cT], two(b), h[:, :, cT], ALU.add).then_inc(*mark("residual", ev))
                elif stage.startswith("up"):
                    l = int(stage[-1])
                    dve.wait_ge(*at(("a", n)))
                    for tap in (1, 0):
                        d = 2 - tap
                        for c in range(2):
                            v = cc[i % 3][:, c, d:T]
                            if tap == 0:
                                dve.wait_ge(*at(("tap", n, c)))
                            dve.scalar_tensor_tensor(v, two(b)[:, c, 0:T - d], vec("ffn_conv", l, tap)(c * FT + i), v, ALU.mult, ALU.add).then_inc(*mark("convolved", *([("tap", n, c)] if tap else [("conv", l, i), ev])))
                elif stage.startswith("gate"):
                    dve.wait_ge(*at(("a", n)))
                    dve.wait_ge(*at(("pe", last_of("pp" + stage[-1]))))
                    g = gate[i % 2]
                    for t in range(TT):
                        dve.tensor_tensor(g[:, t, :], g[:, t, :], bank[2 * t + i // 2][:, (i % 2) * 256:(i % 2) * 256 + 256], ALU.mult).then_inc(*mark("ple", ("ple", n, t)))
                    dve.wait_ge(*at(("ple", n, 1)))
                    dve.tensor_tensor(h[:, :, cT], g[:, :, :], h[:, :, cT], ALU.add).then_inc(*mark("residual", ev))
                elif stage == "ub":
                    dve.wait_ge(*at(("pe", n)))
                    dve.wait_ge(*at(("ev", n - 3)))
                    dve.tensor_tensor(ubs[:, c2, :], two(b), ubs[:, c2, :], ALU.mult).then_inc(*mark("residual", ev))
                split(n + RING)
                if stage.startswith("up"):
                    if i >= 1:
                        ffn_mul(l, i - 1)
                    if i >= 2:
                        ffn_lo(l, i - 2)
                if stage.startswith("down") and n == last_of(stage):
                    for t in range(TT):
                        dve.wait_ge(*at(("tok0", stage) if t == 0 else ("pe", n)))
                        for half in range(2):
                            a = h[:, t, half * 512:half * 512 + 512]
                            dve.tensor_tensor(a, bank[2 * t + half][:, :], a, ALU.add).then_inc(*mark("residual", ("h", stage, t)))

            def soften(tag, hd, j):
                dve.wait_ge(*at(("e", tag, hd)))
                c = slice(2 * j, 2 * j + 2)
                dve.reciprocal(s_sum[:, c], s_sum[:, c]).then_inc(*chained())
                dve.wait_ge(*chain())
                for t in range(TT):
                    v = le[:, j, t, 0:P if (t == 0 and tag == "a") else T]
                    dve.tensor_scalar(v, v, s_sum[:, 2 * j + t:2 * j + t + 1], None, ALU.mult).then_inc(*mark("softmax", ("n", tag, hd)))

            for n in range(RING):
                split(n)
            for step in SCHEDULE:
                kind, args = step[0], step[1:]
                if kind == "panel":
                    panel(args[0])
                elif kind == "setup":
                    dve.wait_ge(*at(("vec", 0)))
                    a = VEC["hg_lb_logits", 0]
                    dve.tensor_tensor(lb_tmp, vflat[:, a:a + 4], vflat[:, a:a + 4], ALU.subtract).then_inc(*chained(("lb0",)))
                    dve.wait_ge(*chain())
                    dve.wait_ge(*at(("lbe",)))
                    dve.reciprocal(lb, lb_tmp).then_inc(*chained())
                    dve.wait_ge(*chain())
                    dve.tensor_tensor(lb_tmp, lb, lb_tmp, ALU.mult).then_inc(*chained())
                    dve.wait_ge(*chain())
                    dve.tensor_tensor(lb, lb_tmp, lb_tmp, ALU.subtract).then_inc(*chained())
                    dve.wait_ge(*chain())
                    dve.tensor_scalar(oml, lb, -1.0, 1.0, ALU.mult, ALU.add).then_inc(*chained())
                    dve.wait_ge(*chain())
                    dve.tensor_scalar(q_gain, vec("q_norm", 0)(0), SW_DIM ** -0.5, None, ALU.mult).then_inc(*chained(("q_gain",)))
                    dve.wait_ge(*chain())
                elif kind == "stats":
                    k = args[0]
                    dve.wait_ge(*at(("sq", k, 1)))
                    dve.tensor_scalar(mean_sq[k], ssq[k], 1.0 / D, EPS, ALU.mult, ALU.add).then_inc(*mark("mean_square", ("ms", k)))
                    dve.wait_ge(*at(("rstd", k)))
                    if k == "final":
                        for t in range(TT):
                            dve.wait_ge(*at(("loaded", "gfin")))
                            dve.scalar_tensor_tensor(result[:, t, :], h[:, t, :], rstd[k][:, t:t + 1], gfin[:, :], ALU.mult, ALU.mult).then_inc(*mark("result", ("result", t)))
                    else:
                        src, dst = (mem, mem) if k == "mem" else (h, xn)
                        dve.tensor_scalar(dst[:, 0, :], src[:, 0, :], rstd[k][:, 0:1], None, ALU.mult).then_inc(*mark("normalized0", ("xn", k, 0)))
                elif kind == "turn":
                    k = args[0]
                    for j in range(4):
                        for q in range(2):
                            kt = 2 * j + q
                            rest(two(4 + j)[:, q, :], GAIN[k](kt), XH[:, kt, :], XL[:, kt, :], "input_lo", ("xl", k, j), ("xh", k, j))
                elif kind == "hg_decay":
                    dve.wait_ge(*at(("ev", last_of("fb"))))
                    for hd in range(HG_HEADS):
                        dve.tensor_scalar(bdec[:, hd, :], bdec[:, hd, :], oml[:, hd:hd + 1], lb[:, hd:hd + 1], ALU.mult, ALU.add).then_inc(*mark("decay", ("f0",)))
                        dve.tensor_scalar(kk[:, hd, :], kk[:, hd, :], oml[:, hd:hd + 1], None, ALU.mult).then_inc(*mark("decay", ("kk",)))
                    dve.wait_ge(*at(("f0",)))
                    dve.tensor_scalar(bdec[:, :, :], bdec[:, :, :], 2.0 ** -64, None, ALU.max).then_inc(*mark("decay", ("f",)))
                    dve.wait_ge(*at(("logf",)))
                    dve.wait_ge(*at(("loaded", "reset")))
                    flat = lambda x: x[:, :, :].rearrange("p a b -> p (a b)")
                    dve.tensor_tensor_scan(flat(bdec), reset[:, :], flat(ex), 0.0, ALU.mult, ALU.add).then_inc(*mark("decay", ("b",)))
                    dve.wait_ge(*at(("b",)))
                    dve.wait_ge(*at(("kk",)))
                elif kind == "hg_level":
                    hg_level(args[0])
                elif kind == "sb_log":
                    for i in range(4):
                        c = slice(2 * i, 2 * i + 2)
                        dve.wait_ge(*at(("sbl", i)))
                        fl = lambda x: x[:, c, :].rearrange("p a b -> p (a b)")
                        dve.scalar_tensor_tensor(fl(sp_), fl(zs), 0.0, fl(sp_), ALU.max, ALU.add).then_inc(*mark("softplus", ("splus", i)))
                elif kind == "hg_out":
                    for t in range(TT):
                        dve.wait_ge(*at(("hgsq", t)))
                        dve.tensor_reduce(hg_ss[:, 4 * t:4 * t + 4], prod4[:, t, :].rearrange("p (h v) -> p h v", h=4), AX.X, ALU.add).then_inc(*chained())
                        dve.wait_ge(*chain())
                    dve.tensor_scalar(hg_ss, hg_ss, 1.0 / P, EPS, ALU.mult, ALU.add).then_inc(*chained())
                    dve.wait_ge(*chain())
                    inverse_root(hg_ss, hg_rs, hg_tmp)
                    for t in range(TT):
                        r4 = hg_rs[:, 4 * t:4 * t + 4].rearrange("p (h a) -> p h a", a=1).to_broadcast([P, 4, P])
                        dve.tensor_tensor(on[:, t, :, :], bank[t][:, :].rearrange("p (h v) -> p h v", h=4), r4, ALU.mult).then_inc(*chained(("on", t)))
                        dve.wait_ge(*chain())
                        o = on[:, t, :, :].rearrange("p h v -> p (h v)")
                        dve.tensor_tensor(o, o, gbs[:, t, :], ALU.mult).then_inc(*mark("hg_gated", ("gated", t)))
                elif kind == "hg_turn":
                    for j in range(2):
                        dve.wait_ge(*at(("xh", "hg", j)))
                        fl = lambda x: x.rearrange("p a b -> p (a b)")
                        dve.scalar_tensor_tensor(fl(XL[:, 4 + 2 * j:6 + 2 * j, :]), bank[2 + j][:, :], vec("hg_out_norm", 0)(0), plain(fl(XH[:, 4 + 2 * j:6 + 2 * j, :])), ALU.mult, ALU.subtract).then_inc(*mark("input_lo", ("xl", "hg", j)))
                elif kind == "sb_weights":
                    i = args[0]
                    for r in range(2):
                        hd = 2 * i + r
                        dve.wait_ge(*at(("sbr", hd)))
                        dve.tensor_tensor(zs[:, hd, :], zs[:, hd, :], bank[4 + hd % 4][:, 0:384], ALU.subtract).then_inc(*mark("sb_exponents", ("d", hd)))
                elif kind == "sb_out":
                    i = args[0]
                    rest(bank[4 + i][:, 0:T], None, XH[:, i, :], XL[:, i, :], "input_lo", ("xl", "sb", i), ("xh", "sb", i))
                elif kind == "up_tail":
                    l = args[0]
                    ffn_mul(l, FT - 1)
                    ffn_lo(l, FT - 2)
                    ffn_lo(l, FT - 1)
                elif kind == "ple_input":
                    l = args[0]
                    rest(two(4), None, PTH[:, :, :], PTL[:, :, :], "input_lo", ("ptl", l), ("pth", l))
                elif kind == "bias":
                    dve.wait_ge(*at(("brp",)))
                    dve.wait_ge(*at(("brow0",)))
                    dve.tensor_copy(brow[:, P:2 * P], bank[0][0:16, 0:P]).then_inc(*mark("bias_row", ("brow",)))
                elif kind == "sw_norm":
                    for t in range(TT):
                        dve.wait_ge(*at(("swsq", t)))
                        dve.tensor_reduce(sw_ss[:, 20 * t:20 * t + 20], sq[:, t, :].rearrange("p (h d) -> p h d", d=SW_DIM), AX.X, ALU.add).then_inc(*chained())
                        dve.wait_ge(*chain())
                    dve.tensor_scalar(sw_ss, sw_ss, 1.0 / SW_DIM, EPS, ALU.mult, ALU.add).then_inc(*chained())
                    dve.wait_ge(*chain())
                    inverse_root(sw_ss, sw_rs, sw_tmp)
                    for t in range(TT):
                        r = sw_rs[:, 20 * t:20 * t + 20]
                        src = qk[:, t, :].rearrange("p (h d) -> p h d", d=SW_DIM)
                        dve.tensor_tensor(qkn[:, t, 0:16, :], src[:, 0:16, :], r[:, 0:16].rearrange("p (h a) -> p h a", a=1).to_broadcast([P, 16, SW_DIM]), ALU.mult).then_inc(*mark("sw_normed", ("qkn0",)))
                        for two_ in range(2):
                            dst = qkn[:, t, 16:24, :].rearrange("p (g a) d -> p g a d", a=2)[:, :, two_, :]
                            dve.tensor_tensor(dst, src[:, 16:20, :], r[:, 16:20].rearrange("p (h a) -> p h a", a=1).to_broadcast([P, 4, SW_DIM]), ALU.mult).then_inc(*mark("sw_normed", ("qkn", t)))
                elif kind == "sw_logits":
                    g = args[0]
                    dve.wait_ge(*at(("loaded", "bias")))
                    dve.wait_ge(*at(("loaded", "sinks")))
                    for j in range(4):
                        hd = 4 * g + j
                        dve.wait_ge(*at(("swz", g, j)))
                        if g:
                            dve.wait_ge(*at(("tr", "sww", g - 1, j)))
                            dve.wait_ge(*at(("swn", g - 1, 3)))
                        for t in range(TT):
                            w = P if t == 0 else T
                            dve.tensor_tensor_reduce(le_s[:, j, t, 0:w], bank[j][:, t * T:t * T + w], bias[:, hd, T - w:T], 1.0, -3.0e38, ALU.add, ALU.max, s_max[:, 2 * j + t:2 * j + t + 1]).then_inc(*mark("logits", ("swm", g, j)))
                    dve.wait_ge(*at(("swm", g, 3)))
                    sk = sinks[:, 4 * g:4 * g + 4].rearrange("p (h a) -> p h a", a=1).to_broadcast([P, 4, 2])
                    v = lambda x: x.rearrange("p (h a) -> p h a", a=2)
                    dve.tensor_tensor(v(s_max), v(s_max), sk, ALU.max).then_inc(*chained())
                    dve.wait_ge(*chain())
                    dve.tensor_scalar(s_neg, s_max, -1.0, None, ALU.mult).then_inc(*chained())
                    dve.wait_ge(*chain())
                    dve.tensor_tensor(v(s_exp), v(s_neg), sk, ALU.add).then_inc(*chained(("swneg", g)))
                    dve.wait_ge(*chain())
                    dve.wait_ge(*at(("swx", g)))
                    dve.tensor_tensor(s_sum, s_sum, s_exp, ALU.add).then_inc(*chained())
                    dve.wait_ge(*chain())
                    dve.reciprocal(s_sum, s_sum).then_inc(*chained())
                    dve.wait_ge(*chain())
                    for j in range(4):
                        for t in range(TT):
                            a = le_s[:, j, t, 0:P if t == 0 else T]
                            dve.tensor_scalar(a, a, s_sum[:, 2 * j + t:2 * j + t + 1], None, ALU.mult).then_inc(*mark("softmax", ("swn", g, j)))
                elif kind == "sw_weights":
                    g = args[0]
                    for j in (1, 3):
                        dve.wait_ge(*at(("tr", "sww", g, j)))
                        if g:
                            dve.wait_ge(*at(("swo", 2 * g - 1)))
                        dve.tensor_copy(wT_s[:, j, :], bank[4 + j][:, 0:384]).then_inc(*mark("turned_copied2", ("swt", g, j)))
                elif kind == "sw_out":
                    g = args[0]
                    for q in range(2):
                        i = 2 * g + q
                        rest(bank[q][:, 0:T], None, XH[:, i, :], XL[:, i, :], "input_lo", ("xl", "sw", i), ("xh", "sw", i))
                elif kind == "x_logits":
                    g = args[0]
                    for j in range(2):
                        hd = 2 * g + j
                        dve.wait_ge(*at(("xz", hd)))
                        if g:
                            dve.wait_ge(*at(("n", "x", 2 * g - 1)))
                            dve.wait_ge(*at(("trw", "x", hd - 2)))
                        c = slice(2 * j, 2 * j + 2)
                        dve.tensor_reduce(s_max[:, c], two(j), AX.X, ALU.max).then_inc(*chained())
                        dve.wait_ge(*chain())
                        dve.tensor_scalar(s_neg[:, c], s_max[:, c], -HEAD ** -0.5, None, ALU.mult).then_inc(*chained(("neg", "x", hd)))
                        dve.wait_ge(*chain())
                    for j in range(2):
                        soften("x", 2 * g + j, j)
                elif kind == "a_logits":
                    g = args[0]
                    dve.wait_ge(*at(("loaded", "causal")))
                    for j in range(2):
                        hd = 2 * g + j
                        dve.wait_ge(*at(("az", hd)))
                        dve.wait_ge(*at(("trw", "a", hd - 2) if g else ("trw", "x", 2 + j)))
                        for t in range(TT):
                            w = P if t == 0 else T
                            dve.tensor_tensor_reduce(le[:, j, t, 0:w], bank[j][:, t * T:t * T + w], causal[:, T - w:T], 1.0, -3.0e38, ALU.add, ALU.max, s_max[:, 2 * j + t:2 * j + t + 1]).then_inc(*mark("logits", ("am", hd)))
                        dve.wait_ge(*at(("am", hd)))
                        dve.tensor_scalar(s_neg[:, 2 * j:2 * j + 2], s_max[:, 2 * j:2 * j + 2], -HEAD ** -0.5, None, ALU.mult).then_inc(*chained(("neg", "a", hd)))
                        dve.wait_ge(*chain())
                    for j in range(2):
                        soften("a", 2 * g + j, j)
                elif kind in ("x_weights", "a_weights"):
                    tag, g = kind[0], args[0]
                    hd = 2 * g + 1
                    dve.wait_ge(*at(("trw", tag, hd)))
                    if tag == "x" and g:
                        dve.wait_ge(*at(("oz", "c", hd - 2)))
                    elif tag == "a":
                        dve.wait_ge(*at(("oz", "a", hd - 2) if g else ("oz", "c", X_HEADS - 1)))
                    n = 2 * T if tag == "x" else 384
                    dve.tensor_copy(wT[:, 1, :, :].rearrange("p a b -> p (a b)")[:, 0:n], bank[3][:, 0:n]).then_inc(*mark("turned_copied2", ("wT", tag, hd)))
                elif kind in ("x_out", "a_out"):
                    b, g = ("c" if kind[0] == "x" else "a"), args[0]
                    src = gc if b == "c" else ga
                    dve.wait_ge(*at(("ev", last_of("gc" if b == "c" else "ga"))))
                    for j in range(2):
                        hd = 2 * g + j
                        dve.wait_ge(*at(("oz", b, hd)))
                        dve.tensor_tensor(src[:, hd, :], bank[j][:, 0:T], src[:, hd, :], ALU.mult).then_inc(*mark("gated", ("og", b, hd)))
                    for j in range(2):
                        hd = 2 * g + j
                        rest(src[:, hd, :], None, GH[:, OUT_AT[b] + hd, :], GL[:, OUT_AT[b] + hd, :], "gated_lo", ("ol", b, hd), ("oh", b, hd))
                elif kind == "rope":
                    dve.wait_ge(*at(("ev", last_of("qka"))))
                    dve.wait_ge(*at(("loaded", "rope")))
                    dve.wait_ge(*at(("tr", "blk2", 3)))
                    for t in range(TT):
                        q = qkm[:, t, :].rearrange("p (e d) -> p e d", d=HEAD)
                        x1, x2 = q[:, :, 0:16], q[:, :, 16:32]
                        cos, sin = (rope[:, t, c, :].rearrange("p (a f) -> p a f", a=1).to_broadcast([P, 12, 16]) for c in range(2))
                        if t:
                            dve.wait_ge(*at(("roped0",)))
                        for f, (a, m) in enumerate(((x1, cos), (x2, sin), (x2, cos), (x1, sin))):
                            dve.tensor_tensor(rtmp[:, f, :, :], a, m, ALU.mult).then_inc(*mark("rope", ("rope_m", t)))
                        dve.wait_ge(*at(("rope_m", t)))
                        dve.tensor_tensor(x1, rtmp[:, 0, :, :], rtmp[:, 1, :, :], ALU.subtract).then_inc(*mark("rope", ("rope_s", t)))
                        dve.tensor_tensor(x2, rtmp[:, 2, :, :], rtmp[:, 3, :, :], ALU.add).then_inc(*mark("rope", ("roped",) if t else ("roped0",)))
                elif kind == "rope_turn":
                    for j in (1, 3, 5):
                        dve.wait_ge(*at(("tr", "rope", j)))
                        dst = qF if j < 3 else kF
                        dve.tensor_copy(dst[:, (2 * j) % 6:(2 * j) % 6 + 2, :], two(3)).then_inc(*mark("turned_copied2", ("qkF", j)))
                elif kind == "layer_norm":
                    dve.wait_ge(*at(("ev", last_of("vb"))))
                    for t in range(TT):
                        dve.tensor_reduce(ln_sum[:, t:t + 1], vb[:, t, :], AX.X, ALU.add).then_inc(*chained())
                        dve.wait_ge(*chain())
                    dve.tensor_scalar(ln_neg, ln_sum, -1.0 / 768, None, ALU.mult).then_inc(*chained(("lnm",)))
                    dve.wait_ge(*chain())
                    dve.wait_ge(*at(("lnsq", 1)))
                    dve.tensor_scalar(ln_ss, ln_ss, 1.0 / 768, EPS, ALU.mult, ALU.add).then_inc(*chained())
                    dve.wait_ge(*chain())
                    inverse_root(ln_ss, ln_rs, ln_sum)
                    for t in range(TT):
                        dve.tensor_scalar(vb[:, t, :], vb[:, t, :], ln_neg[:, t:t + 1], ln_rs[:, t:t + 1], ALU.add, ALU.mult).then_inc(*mark("layer_normed", ("vn", t)))
                elif kind == "mixed":
                    dve.wait_ge(*at(("ev", last_of("ub"))))
                    dve.wait_ge(*at(("loaded", "bsp")))
                    for g in range(GROUPS):
                        dve.wait_ge(*at(("mixp", g // 2)))
                        tb = lambda x: x.rearrange("p (t c) -> p t c", t=TT)
                        bb = bsp[:, g, :].rearrange("p (a c) -> p a c", a=1).to_broadcast([P, TT, P])
                        dve.scalar_tensor_tensor(tb(mixt[:, g, :]), tb(two(g // 2)[:, g % 2, :]), vec("gmlp_ln_g_2", 0)(g), bb, ALU.mult, ALU.add).then_inc(*mark("mixed", ("mixg", g)))
                    for g in range(GROUPS):
                        dve.wait_ge(*at(("mixg", g)))
                        dve.tensor_tensor(ubs[:, g, :], mixt[:, g, :], ubs[:, g, :], ALU.mult).then_inc(*mark("gated", ("og", "b", g)))
                    for g in range(GROUPS):
                        rest(ubs[:, g, :], None, GH[:, OUT_AT["b"] + g, :], GL[:, OUT_AT["b"] + g, :], "gated_lo", ("ol", "b", g), ("oh", "b", g))
                elif kind == "branch_end":
                    b = args[0]
                    m = msig[b == "b"]
                    dve.wait_ge(*at(("pe", last_of("br" + b))))
                    dve.wait_ge(*at(("ev", last_of("m" + b))))
                    dve.wait_ge(*at(("og", "b", GROUPS - 1)))
                    for j in range(4):
                        c = slice(2 * j, 2 * j + 2)
                        if b == "c":
                            dve.tensor_tensor(y[:, c, :], two(j), m[:, c, :], ALU.mult).then_inc(*mark("branch_sum", ("yb", b, j)))
                        else:
                            dve.tensor_tensor(m[:, c, :], two(j), m[:, c, :], ALU.mult).then_inc(*chained())
                            dve.wait_ge(*chain())
                            dve.tensor_tensor(y[:, c, :], y[:, c, :], m[:, c, :], ALU.add).then_inc(*mark("branch_sum", ("yb", b, j)))
                elif kind == "y_split":
                    for j in range(4):
                        c = slice(2 * j, 2 * j + 2)
                        rest(y[:, c, :], None, XH[:, c, :], XL[:, c, :], "input_lo", ("xl", "y", j), ("xh", "y", j))

    return events


_INS = ["x", "p", "mix_norm", "ab_w_in", "hg_lb_logits", "hg_out_norm", "ab_w_out", "c_w_in", "q_norm", "k_norm", "sinks", "rel_bias",
        "c_w_out", "ffn_norm", "ffn_up", "ffn_conv", "ffn_conv_b", "ffn_down", "ple_norm", "ple_gate", "ple_proj", "mem_2", "norm_g_2",
        "mem_norm_g_2", "final_norm_g_2", "w_in_2", "w_mem_kv_2", "gmlp_ln_g_2", "w_spatial_2", "b_spatial_2", "w_branch_a_2",
        "w_branch_b_2", "w_branch_c_2", "w_out_2"]


def kernel(**inputs):
    import concourse.bacc as bacc
    from concourse.bass_utils import run_bass_kernel_spmd

    arrays = {f"in_{n}": np.ascontiguousarray(inputs[n]) for n in _INS}
    arrays.update(shape_constants())

    def build(known):
        nc = bacc.Bacc("TRN2", target_bir_lowering=False, num_devices=1)
        io = {}
        for name, a in arrays.items():
            io[name.removeprefix("in_")] = nc.dram_tensor(name, a.shape, mybir.dt.from_np(a.dtype), kind="ExternalInput").ap()
        out = nc.dram_tensor("out_dram", (1, T, D), F32, kind="ExternalOutput").ap()
        return nc, block_program(nc, io, out, known)

    said = build({})[1].said
    nc = build(said)[0]
    r = run_bass_kernel_spmd(nc, [arrays], core_ids=[0])
    return r.results[0]["out_dram"]
```

```python
from contextlib import ExitStack

import numpy as np

import concourse.bass as bass
from concourse import mybir

ALU = mybir.AluOpType
ACT = mybir.ActivationFunctionType
AX = mybir.AxisListType
F32 = mybir.dt.float32
F32R = mybir.dt.float32r
I32 = mybir.dt.int32

P = 128
T = 256
TT = T // P
D = 1024
KT = D // P
EPS = 1e-6
NEG = -1e30
SB_HEADS, SB_DIM = 8, 64
HG_HEADS, HG_CHUNK = 4, 64
SW_HEADS, SW_KV, SW_DIM, WINDOW = 16, 4, 64, 128
BUCKETS, MAX_DISTANCE = 32, 128
D_FF = 2816
FT = D_FF // P
MOBA_HEADS, X_HEADS, GROUPS, HEAD = 6, 4, 6, 128
ROT = HEAD // 4
LEVELS = [64, 32, 16, 8, 4, 2, 1, 0]
RAW, RING = 3, 3
MAGIC = float(0x5F3759DF)



def shape_constants():
    i = np.arange(P)
    s, t = i[:, None], i[None, :]
    levels = []
    for half in LEVELS:
        if half:
            levels.append((s // (2 * half) == t // (2 * half)) & (s % (2 * half) < half) & (t % (2 * half) >= half))
        else:
            levels.append(s == t)
    dist = 127 - i
    exact = BUCKETS // 2
    large = exact + (np.log(np.maximum(dist, exact) / exact) / np.log(MAX_DISTANCE / exact) * (BUCKETS - exact)).astype(np.int32)
    bucket = np.where(dist < exact, dist, np.minimum(large, BUCKETS - 1))
    inv_freq = np.float32(500000.0) ** (-np.arange(0, ROT, 2, dtype=np.float32) / np.float32(ROT))
    ang = (np.arange(T, dtype=np.float32)[:, None] * inv_freq[None, :]).astype(np.float32)
    return {
        "c_ident": np.eye(P, dtype=np.float32),
        "c_tri": (s >= t).astype(np.float32),
        "c_levels": np.stack(levels, 1).astype(np.float32).reshape(P, -1),
        "c_reset": np.tile((np.arange(HG_HEADS * T) % HG_CHUNK != 0).astype(np.float32), (P, 1)),
        "c_causal": np.where(np.arange(T)[None, :] - P <= s, 0.0, NEG).astype(np.float32),
        "c_bucket": (bucket[None, :] == np.arange(BUCKETS)[:, None]).astype(np.float32),
        "c_rope": np.stack([np.cos(ang), np.sin(ang)], 1).reshape(TT, P, 2, ROT // 2).transpose(1, 0, 2, 3).reshape(P, -1).astype(np.float32).copy(),
    }


VEC = {}
VEC_LOADS = []


def _vectors():
    at = 0
    for name, layer, n in [("mix_norm", 0, 8), ("mix_norm", 1, 8), ("ffn_norm", 0, 8), ("ffn_norm", 1, 8),
                           ("ple_norm", 0, 8), ("ple_norm", 1, 8), ("norm_g_2", 0, 8), ("mem_norm_g_2", 0, 8),
                           ("hg_out_norm", 0, 1), ("hg_lb_logits", 0, 4), ("gmlp_ln_g_2", 0, 6)]:
        VEC[name, layer] = at
        VEC_LOADS.append((name, (layer,), at, n))
        at += n
    for name in ("q_norm", "k_norm"):
        VEC[name, 0] = at
        VEC_LOADS.append((name, (0,), at, 1))
        at += 1
    at = P
    for layer in range(2):
        VEC["ffn_conv_b", layer] = at + 2 * FT * layer
        VEC_LOADS.append(("ffn_conv_b", (layer,), at + 2 * FT * layer, 2 * FT))
    for n, (layer, tap) in enumerate([(a, b) for a in range(2) for b in range(3)]):
        at = P * (2 + n // 2) + 2 * FT * (n % 2)
        VEC["ffn_conv", layer, tap] = at
        VEC_LOADS.append(("ffn_conv", (layer, tap), at, 2 * FT))


_vectors()
VEC_ROWS = [77, 4 * FT, 4 * FT, 4 * FT, 4 * FT]


class Events:

    def __init__(self, known, make):
        self.known, self.make = known, make
        self.sems, self.count, self.said, self.links = {}, {}, {}, 0

    def sem(self, name):
        if name not in self.sems:
            self.sems[name] = self.make(name)
        return self.sems[name]

    def mark(self, name, *events, by=1):
        self.count[name] = self.count.get(name, 0) + by
        for e in events:
            self.said[e] = (name, self.count[name])
        return self.sem(name), by

    def at(self, event):
        name, value = self.known[event] if self.known else ("first_pass", 1)
        return self.sem(name), value

    def chained(self, *events):
        self.links += 1
        return self.mark("vector_chain", ("link", self.links), *events)

    def chain(self):
        return self.at(("link", self.links))


def panels_of():
    out = []

    def cols(stage, name, at, n, kind, idx=()):
        for i in range(n):
            out.append((stage, i, name, kind, (idx, at + 256 * i)))

    def rows(stage, name, n, kind, idx=()):
        for i in range(n):
            out.append((stage, i, name, kind, (idx, 256 * i)))

    for stage, at, kind in (("qb", 1536, "F"), ("gb", 3072, "T"), ("fb", 2048, "F"), ("qa", 0, "F"), ("ka", 512, "F"),
                            ("ib", 2560, "T"), ("va", 1024, "T")):
        cols(stage, "ab_w_in", at, 2, kind, (0,))
    cols("wo0", "ab_w_out", 0, 4, "T", (0,))
    for layer in range(2):
        for i in range(FT):
            out.append((f"up{layer}", i, "ffn_up", "F", ((layer,), i * P)))
        rows(f"down{layer}", "ffn_down", FT // 2, "BT", (layer,))
        rows(f"pp{layer}", "ple_proj", 1, "BT", (layer,))
        cols(f"gate{layer}", "ple_gate", 0, 4, "T", (layer,))
        if layer == 0:
            cols("qs", "c_w_in", 0, 4, "T", (0,))
            cols("ks", "c_w_in", 1024, 1, "T", (0,))
            cols("vs", "c_w_in", 1280, 1, "T", (0,))
            cols("wo1", "c_w_out", 0, 4, "T", (0,))
    cols("mk", "w_mem_kv_2", 0, 2, "F", (0,))
    cols("mv", "w_mem_kv_2", 512, 2, "T", (0,))
    for stage, at, n, kind in (("qc", 5376, 2, "F"), ("gc", 5888, 2, "F"), ("qka", 0, 6, "T"), ("va2", 1536, 3, "T"),
                               ("ga", 2304, 3, "F"), ("vb", 3840, 3, "T"), ("gb2", 4608, 3, "F"), ("ub", 3072, 3, "F")):
        cols(stage, "w_in_2", at, n, kind, (0,))
    for b, at, n in (("c", 8448, 2), ("b", 7424, 3), ("a", 6400, 3)):
        cols("m" + b, "w_in_2", at, 4, "F", (0,))
        rows("br" + b, f"w_branch_{b}_2", n, "BF", (0,))
    cols("wo2", "w_out_2", 0, 4, "T", (0,))
    return out


PANELS = panels_of()
FIRST = {}
for _n, _p in enumerate(PANELS):
    FIRST.setdefault(_p[0], _n)


def last_of(stage):
    return max(n for n, p in enumerate(PANELS) if p[0] == stage)


TURNED_LATER = ("blk2", "final")


def schedule():
    out = []

    def gemm(*stages):
        for s in stages:
            out.extend(("panel", n) for n, p in enumerate(PANELS) if p[0] == s)

    def producer(stage, k):
        first = FIRST[stage]
        for j in range(4):
            out.append(("panel", first + j))
            if k and j < 3:
                out.append(("square", k, j))
            if k in TURNED_LATER:
                continue
            if k and j:
                out.append(("turn", k, j - 1))
        if k and k not in TURNED_LATER:
            out.append(("turn_last", k))
        if k:
            out.extend([("square", k, 3), ("stats", k)])

    out.extend([("setup", 0), ("turn", "mix0", 0), ("turn", "mix0", 1), ("turn", "mix0", 2), ("split", 0), ("turn_last", "mix0")])
    out.extend(("square", "mix0", j) for j in range(4))
    out.extend([("stats", "mix0"), ("split", 1), ("split", 2)])
    gemm("qb")
    out.append(("setup", 1))
    gemm("gb", "fb")
    first = FIRST["qa"]
    out.extend([("hg_decay",), ("hg_level", -1), ("panel", first), ("panel", first + 1), ("hg_level", 0), ("panel", first + 2)])
    for n, li in enumerate(range(-1, 4)):
        out.append(("hg_scores", li))
        if n:
            out.append(("sb_scores", n - 1))
        out.extend([("hg_mask", li), ("hg_level", li + 2)])
        out.append(("panel", first + 3 + n))
    out.extend([("hg_scores", 4), ("hg_mask", 4), ("hg_level", 6), ("hg_scores", 5), ("hg_mask", 5), ("sb_log",)])
    out.extend([("hg_scores", 6), ("hg_scores", 7), ("hg_mask", 6), ("hg_mask", 7)])
    out.extend([("sb_weights", 0), ("sb_weights", 1), ("hg_out",), ("sb_weights", 2), ("sb_weights", 3)])
    for i in range(SB_HEADS // 2):
        out.append(("sb_out", i))
    out.append(("hg_turn",))
    producer("wo0", "ffn0")
    for layer in range(2):
        out.append(("ffn_loads", layer))
        gemm(f"up{layer}")
        out.extend([("up_tail", layer), ("ple_input", layer)])
        if layer == 0:
            out.append(("bias",))
        gemm(f"down{layer}")
        gemm(f"pp{layer}")
        k = f"ple{layer}"
        out.extend([("turn", k, 0), ("turn", k, 1), ("turn", k, 2), ("turn_last", k)])
        out.extend(("square", k, j) for j in range(4))
        out.append(("stats", k))
        if layer == 0:
            producer("gate0", "mix1")
            gemm("qs", "ks", "vs")
            out.append(("sw_norm",))
            for g in range(SW_KV):
                out.append(("sw_logits", g))
                out.append(("sw_weights", g))
                out.append(("sw_out", g))
            producer("wo1", "ffn1")
    producer("gate1", "blk2")
    at = out.index(("panel", FIRST["gate1"] + 2))
    out[at:at] = [("stats", "mem")]
    out.extend(("turn", "mem", j) for j in range(4))
    for n, stage in enumerate(("mk", "mk", "mv", "mv")):
        out.extend([("panel", FIRST["mk"] + n), ("turn", "blk2", n)])
    gemm("qc", "gc")
    out.append(("x_logits", 0))
    gemm("qka")
    out.extend([("x_weights", 0), ("x_logits", 1), ("x_out", 0), ("rope",)])
    gemm("va2")
    out.extend([("x_weights", 1), ("x_out", 1), ("rope_turn",), ("spatial",), ("a_logits", 0)])
    gemm("ga")
    out.extend([("a_weights", 0), ("a_logits", 1), ("a_out", 0)])
    gemm("vb")
    out.extend([("a_weights", 1), ("a_logits", 2), ("a_out", 1), ("layer_norm",)])
    gemm("gb2")
    out.extend([("a_weights", 2), ("a_out", 2)])
    gemm("ub")
    out.append(("mixed",))
    for b in "cba":
        gemm("m" + b, "br" + b)
        out.append(("branch_end", b))
    out.append(("y_split",))
    producer("wo2", "final")
    return out


LATE_TURN = {FIRST["qb"]: "mix0", FIRST["up0"]: "ffn0", FIRST["gate0"]: "ple0", FIRST["qs"]: "mix1", FIRST["up1"]: "ffn1",
             FIRST["gate1"]: "ple1"}
ROWS_AFTER = {FIRST["qb"]: "mix0", FIRST["up0"]: "ffn0", FIRST["up1"]: "ffn1", FIRST["mv"]: "blk2"}
SCHEDULE = schedule()


def block_program(nc, io, out_ap, known):
    with ExitStack() as ctx:
        events = Events(known, lambda name: ctx.enter_context(nc.semaphore(name)))
        mark, at, chained, chain = events.mark, events.at, events.chained, events.chain
        top = [16512]

        def fixed(name, shape, dt=F32):
            n = 4 * int(np.prod(shape[1:]))
            n = (n + 31) // 32 * 32
            t = nc.alloc_sbuf_tensor_at(name, shape, dt, offset=top[0])
            top[0] += n
            return t

        raw = [fixed(f"w_raw{i}", [P, 2048]) for i in range(RAW)]
        whi = [fixed(f"w_hi{i}", [P, 2048], F32R) for i in range(RING)]
        wlo = [fixed(f"w_lo{i}", [P, 2048], F32R) for i in range(RING)]
        XH, XL = (fixed(n, [P, KT, T], F32R) for n in ("x_hi", "x_lo"))
        h = fixed("h", [P, TT, D])
        xn_at = top[0]
        xn = fixed("xn", [P, TT, D])
        ident = fixed("ident", [P, P])
        tri = fixed("tri", [P, P])
        vecs = fixed("vecs", [P, 5, P])
        small = fixed("small", [P, 320])
        g_at = top[0]
        GH, GL = (fixed(n, [P, FT, T], F32R) for n in ("g_hi", "g_lo"))
        t_at = top[0]
        end = nc.sbuf_usable_end

        class Region:

            def __init__(self, at, end):
                self.at, self.end = at, end

            def __call__(self, name, shape, dt=F32):
                n = 4 * int(np.prod(shape[1:]))
                t = nc.alloc_sbuf_tensor_at(name, shape, dt, offset=self.at)
                self.at += n
                assert self.at <= self.end, (name, self.at - self.end)
                return t

        r, g = Region(t_at, end), Region(g_at, t_at)
        qaT, kaT = r("qaT", [P, 4, T]), r("kaT", [P, 4, T])
        va, ib, gbs = r("va", [P, TT, 512]), r("ib", [P, TT, 512]), r("gbs", [P, TT, 512])
        qf, kk, bdec = r("qf", [P, HG_HEADS, T]), r("kk", [P, HG_HEADS, T]), r("bdec", [P, HG_HEADS, T])
        ex, prod = r("ex", [P, HG_HEADS, T]), r("prod", [P, len(LEVELS), P])
        masks = r("masks", [P, len(LEVELS), P])
        zs, sp_ = g("zs", [P, SB_HEADS, 384]), g("sp_", [P, SB_HEADS, 384])
        reset, sc, on = g("reset", [P, HG_HEADS * T]), g("sc", [P, HG_HEADS, 384]), g("on", [P, TT, HG_HEADS, P])
        exb = g("exb", [P, HG_HEADS, T])
        xs_buf = [r(f"xs{i}", [P, HG_HEADS, T]) for i in range(2)]
        ones = g("ones", [P, P])
        prod4 = prod[:, :, :].rearrange("p (t a) c -> p t (a c)", t=TT)

        def blocks_of(buf, h0):
            return buf[:, h0:h0 + 2, :].rearrange("p h (a c) -> p h a c", a=3)[:, :, 0:3:2, :]

        def blocks_of_prod(j):
            return prod[:, 4 * j:4 * j + 4, :].rearrange("p (h t) c -> p h t c", h=2)

        r = Region(t_at, end)
        cc = [r(f"cc{i}", [P, 2, T]) for i in range(3)]
        sgate = [r(f"sgate{i}", [P, T]) for i in range(2)]
        gf = [r(f"gf{i}", [P, T]) for i in range(2)]
        praw = r("praw", [P, TT, 256])
        PTH, PTL = r("pt_hi", [P, 2, T], F32R), r("pt_lo", [P, 2, T], F32R)
        gate = [r(f"gate{i}", [P, TT, 256]) for i in range(2)]
        ub_ = [r(f"conv_in{i}", [P, 2, T]) for i in range(2)]
        vsw = r("vsw", [P, TT, 256])
        bias = r("bias", [P, SW_HEADS, T])
        brow = r("brow", [16, 3 * P])
        relb, buck = r("relb", [32, 16]), r("buck", [32, P])
        YL = r("y_lo", [P, KT, T], F32R)
        YH = nc.alloc_sbuf_tensor_at("y_hi", [P, KT, T], F32R, offset=xn_at)
        row_early = r("row_early", [P, T])
        junk = [cc[t][:, 0, :] for t in range(TT)]
        r, g = Region(t_at, t_at + 4 * 4096), Region(g_at, t_at)
        qsT, le_s = r("qsT", [P, 8, T]), r("le_s", [P, 4, 2, T])
        qk, sq = g("qk", [P, TT, 1280]), g("sq", [P, TT, 1280])
        qkn = g("qkn", [P, TT, 24, SW_DIM])
        wT_s = g("wT_s", [P, 4, 384])
        ksT = g("ksT", [P, SW_KV, T])
        qF = nc.alloc_sbuf_tensor_at("qF", [P, MOBA_HEADS, T], F32, offset=g_at + 4 * T * 16)
        kF = nc.alloc_sbuf_tensor_at("kF", [P, MOBA_HEADS, T], F32, offset=g_at + 4 * T * (FT + 16))
        mem = nc.alloc_sbuf_tensor_at("mem", [P, TT, D], F32, offset=g_at)
        mem_junk = nc.alloc_sbuf_tensor_at("mem_junk", [P, D], F32, offset=g_at + 4 * TT * D)
        r = Region(t_at, end)
        qkm = r("qkm", [P, TT, 1536])
        qc, gc = r("qc", [P, X_HEADS, T]), r("gc", [P, X_HEADS, T])
        mk, mv = r("mk", [P, X_HEADS, T]), r("mv", [P, TT, 512])
        le, wT = r("le", [P, 2, 2, T]), r("wT", [P, 2, 2, T])
        va2, vb = r("va2", [P, TT, 768]), r("vb", [P, TT, 768])
        wsp, bsp = r("wsp", [P, GROUPS, P]), r("bsp", [P, GROUPS, P])
        causal = r("causal", [P, T])
        r = Region(t_at, t_at + 4 * 3072)
        ubs, ga = r("ubs", [P, GROUPS, T]), r("ga", [P, MOBA_HEADS, T])
        r = Region(t_at + 4 * 3072, end)
        msig = [r(f"msig{i}", [P, KT, T]) for i in range(2)]
        gfin, result = r("gfin", [P, D]), r("result", [P, TT, D])
        xflat = xn[:, :, :].rearrange("p a b -> p (a b)")
        y = xflat.rearrange("p (k t) -> p k t", k=KT)
        rtmp = xflat[:, 0:768].rearrange("p (f e j) -> p f e j", f=4, e=12)
        wsp_raw = xflat[:, 1024:1792].rearrange("p (g s) -> p g s", g=GROUPS)
        mixt = xflat[:, 0:1536].rearrange("p (g t) -> p g t", g=GROUPS)

        bank = [ctx.enter_context(nc.psum_tensor(f"bank{i}", [P, 512], F32)) for i in range(8)]
        BW = 3 * P
        scratch = nc.dram_tensor("bias_rows", [SW_HEADS, P, BW], F32, kind="Internal").ap()

        small_at = [64]

        def col(n):
            small_at[0] += n
            assert small_at[0] <= 320
            return small[:, small_at[0] - n:small_at[0]]

        rope = small[:, 0:64].rearrange("p (t c f) -> p t c f", t=TT, c=2)
        NORMS = ["mix0", "ffn0", "ple0", "mix1", "ffn1", "mem", "ple1", "blk2", "final"]
        ssq = {k: col(4 * TT) for k in NORMS}
        rstd = {k: col(TT) for k in NORMS}
        minus_half = col(TT)
        lb, oml, lb_tmp = col(HG_HEADS), col(HG_HEADS), col(HG_HEADS)
        q_gain, sinks = col(1), col(SW_HEADS)
        s_max, s_neg, s_sum, s_exp = col(8), col(8), col(8), col(8)
        ln_sum, ln_neg, ln_ss, ln_rs = col(TT), col(TT), col(TT), col(TT)
        sw_ss, sw_rs, sw_tmp = col(40), col(40), qkn[:, 0, 23, 0:40]
        hg_ss, hg_rs, hg_tmp = sw_ss[:, 0:8], sw_ss[:, 8:16], sw_ss[:, 16:24]

        vflat = vecs[:, :, :].rearrange("p a b -> p (a b)")

        def vec(name, layer, *more):
            return lambda i: vflat[:, VEC[(name, layer, *more)] + i:VEC[(name, layer, *more)] + i + 1]

        GAIN = {"mix0": vec("mix_norm", 0), "mix1": vec("mix_norm", 1), "ffn0": vec("ffn_norm", 0), "ffn1": vec("ffn_norm", 1),
                "ple0": vec("ple_norm", 0), "ple1": vec("ple_norm", 1), "blk2": vec("norm_g_2", 0), "mem": vec("mem_norm_g_2", 0)}

        ROWS = {k: row_early[:, :] for k in ("mix0", "ffn0", "ffn1")}
        ROWS["blk2"] = vflat[:, P:P + T]

        def row2(k):
            return ROWS[k].rearrange("p (a t) -> p a t", a=1).to_broadcast([P, 2, T])

        def plain(ap):
            return ap.bitcast(F32)

        def two(b):
            return bank[b][:, :].rearrange("p (a c) -> p a c", a=2)

        def pb(n):
            return n % 2 if PANELS[n][0].startswith("gate") else 4 + n % 4

        def ppb(l, t, half):
            return 4 + (FIRST["qs" if l == 0 else "mk"] + 2 * half + t) % 4

        def turn_bank(k, j):
            return 2 + j % 2 if k in ("mix1", "mem") else j

        def columns_ready(k, j):
            stage = {"ffn0": "wo0", "mix1": "gate0", "ffn1": "wo1", "blk2": "gate1", "final": "wo2"}.get(k)
            if stage:
                return "ev", FIRST[stage] + j
            return ("loaded", "x") if k == "mix0" else ("h", "down" + k[-1], 1)

        DEST = {k: (XH, XL) for k in ("mix0", "ple0", "ple1", "blk2")}
        DEST.update({k: (YH, YL) for k in ("ffn0", "mix1", "ffn1", "mem")})
        XUSED = {"ffn0": ("tr", "vec", 4), "ple0": ("pe", last_of("wo0")), "mix1": ("pe", last_of("up0")),
                 "ffn1": ("pe", last_of("vs")), "ple1": ("pe", last_of("wo1")), "mem": ("pe", last_of("up1")),
                 "blk2": ("pe", last_of("gate1"))}
        XIN = {}

        def normed(k):
            return (*DEST[k], 0, {2 * j: [("xl", k, j)] for j in range(4)})

        for s in ("qb", "gb", "fb", "qa", "ka", "ib", "va"):
            XIN[s] = normed("mix0")
        XIN["wo0"] = (XH, XL, 0, {**{k: [("xl", "sb", k)] for k in range(4)}, 4: [("xl", "hg", 0)], 6: [("xl", "hg", 1)]})
        XIN["wo1"] = (XH, XL, 0, {k: [("xl", "sw", k)] for k in range(8)})
        for l in range(2):
            XIN[f"up{l}"] = normed(f"ffn{l}")
            XIN[f"down{l}"] = (GH, GL, 0, {})
            XIN[f"pp{l}"] = (PTH, PTL, 0, {0: [("ptl", l)]})
            XIN[f"gate{l}"] = normed(f"ple{l}")
        for s in ("qs", "ks", "vs"):
            XIN[s] = normed("mix1")
        for s in ("mk", "mv"):
            XIN[s] = normed("mem")
        for s in ("qc", "gc", "qka", "va2", "ga", "vb", "gb2", "ub", "mc", "mb", "ma"):
            XIN[s] = normed("blk2")
        OUT_AT = {"a": 0, "b": MOBA_HEADS, "c": MOBA_HEADS + GROUPS}
        XIN["brc"] = (GH, GL, OUT_AT["c"], {0: [("ol", "c", X_HEADS - 1)]})
        XIN["brb"] = (GH, GL, OUT_AT["b"], {0: [("ol", "b", GROUPS - 1)]})
        XIN["bra"] = (GH, GL, OUT_AT["a"], {0: [("ol", "a", MOBA_HEADS - 1)]})
        XIN["wo2"] = (XH, XL, 0, {2 * j: [("xl", "y", j)] for j in range(4)})
        NORM_OF = {s: "mix0" for s in ("qb", "gb", "fb", "qa", "ka", "ib", "va")}
        NORM_OF.update({s: "mix1" for s in ("qs", "ks", "vs")})
        NORM_OF.update({"up0": "ffn0", "up1": "ffn1", "gate0": "ple0", "gate1": "ple1"})
        NORM_OF.update({s: "blk2" for s in ("qc", "gc", "qka", "va2", "ga", "vb", "gb2", "ub", "mc", "mb", "ma")})

        block = ctx.enter_context(nc.Block())

        @block.sync
        def _(sp):
            def load(dst, src, name):
                sp.dma_start(dst, src).then_inc(*mark(f"load_{name}", ("loaded", name), by=16))

            load(h[:, :, :], io["x"][0].rearrange("(t p) d -> p t d", p=P), "x")
            load(ident[:, :], io["c_ident"], "ident")

            def panel(n):
                stage, i, name, kind, (idx, where) = PANELS[n]
                w = io[name]
                for j in idx:
                    w = w[j]
                slot = n % RAW
                if n >= RAW:
                    sp.wait_ge(*at(("lo", n - RAW)))
                if kind in ("BT", "BF"):
                    src = w[where:where + 256, :].rearrange("(k p) n -> p k n", p=P)
                    sp.dma_start(raw[slot][:, :].rearrange("p (k n) -> p k n", k=2), src).then_inc(*mark(f"panel_loaded{slot}", ("raw", n), by=16))
                elif stage.startswith("up"):
                    dst = raw[slot][:, :].rearrange("p (k c n) -> p k c n", k=KT, c=2)
                    for c in range(2):
                        a = where + c * D_FF
                        sp.dma_start(dst[:, :, c, :], w[:, a:a + P].rearrange("(k p) n -> p k n", p=P)).then_inc(*mark(f"panel_loaded{slot}", ("raw", n), by=16))
                else:
                    src = w[:, where:where + 256].rearrange("(k p) n -> p k n", p=P)
                    sp.dma_start(raw[slot][:, :].rearrange("p (k n) -> p k n", k=KT), src).then_inc(*mark(f"panel_loaded{slot}", ("raw", n), by=16))

            for n in range(len(PANELS)):
                panel(n)
                if n == 3:
                    load(masks[:, :, :].rearrange("p a b -> p (a b)"), io["c_levels"], "levels")
                    load(reset[:, :], io["c_reset"], "reset")
                    load(tri[:, :], io["c_tri"], "tri")
            for tok in range(TT):
                sp.wait_ge(*at(("result", tok)))
                sp.dma_start(out_ap[0].rearrange("(t p) d -> p t d", p=P)[:, tok, :], result[:, tok, :]).then_inc(*mark("stored", ("stored", tok), by=16))
            sp.wait_ge(*at(("stored", 1)))

        @block.gpsimd
        def _(pool):
            def load(dst, src, name):
                pool.dma_start(dst, src).then_inc(*mark(f"load_{name}", ("loaded", name), by=16))

            def rows(name, pre):
                a = io[name]
                for j in pre:
                    a = a[j]
                return a

            def earlier_only(buf, hd, name, event):
                v = buf[:, hd, :].rearrange("p (a c) -> p a c", a=3)[:, 0:3:2, :]
                pool.affine_select(out=v, in_=v, compare_op=ALU.is_gt, fill=0.0, base=0, pattern=[[0, 2], [1, P]], channel_multiplier=-1).then_inc(*mark(name, event))

            def ffn_mul(l, i):
                pool.wait_ge(*at(("sg", l, i)))
                if i >= 2:
                    pool.wait_ge(*at(("gl", l, i - 2)))
                elif l:
                    pool.wait_ge(*at(("gl", l - 1, FT - 2 + i)))
                pool.tensor_tensor(gf[i % 2][:, :], sgate[i % 2][:, :], cc[i % 3][:, 1, :], ALU.mult).then_inc(*mark("gated", ("gf", l, i)))

            vrow = xn[:, 0, 0:640].rearrange("p (g c) -> p g c", g=5)
            for name, pre, r0, n in VEC_LOADS:
                src, g, q = rows(name, pre), r0 // P, r0 % P
                if g:
                    load(vrow[q:q + n, g, :], src.rearrange("(a c) -> a c", c=P), "vectors")
            pool.memset(minus_half, -0.5).then_inc(*mark("pool_const", ("half",)))
            pool.memset(ones[:, :], 1.0).then_inc(*mark("pool_const", ("ones",)))
            for step in SCHEDULE:
                kind, args = step[0], step[1:]
                if kind == "stats":
                    k = args[0]
                    pool.wait_ge(*at(("half",)))
                    pool.wait_ge(*at(("ms", k)))
                    pool.tensor_tensor(rstd[k], rstd[k], minus_half, ALU.pow).then_inc(*mark("rstd", ("rstd", k)))
                elif kind == "panel" and PANELS[args[0]][0].startswith("up"):
                    stage, i = PANELS[args[0]][:2]
                    if i >= 2:
                        ffn_mul(int(stage[-1]), i - 2)
                elif kind == "up_tail":
                    ffn_mul(args[0], FT - 2)
                    ffn_mul(args[0], FT - 1)
                elif kind == "hg_mask":
                    li = args[0]
                    if li >= 1:
                        for j in range(2):
                            a = blocks_of(sc, 2 * j)
                            pool.wait_ge(*at(("prod", li, j)))
                            pool.tensor_tensor(a, a, blocks_of_prod(j), ALU.add).then_inc(*mark("scores_summed", ("sc", li, j)))
                elif kind == "sb_log":
                    for hd in range(SB_HEADS):
                        pool.wait_ge(*at(("splus", hd // 2)))
                        earlier_only(sp_, hd, "softplus_masked", ("spm", hd // 2))
                elif kind == "sb_weights":
                    i = args[0]
                    pool.wait_ge(*at(("w", i)))
                    for r in range(2):
                        earlier_only(zs, 2 * i + r, "weights_masked", ("wm", i))
                elif kind == "ffn_loads":
                    l = args[0]
                    if l == 1:
                        pool.wait_ge(*at(("pt", 0, 1)))
                    else:
                        pool.wait_ge(*at(("ev", last_of("wo0"))))
                    load(praw[:, :, :], io["p"][l, 0].rearrange("(t p) d -> p t d", p=P), f"p{l}")
                    if l == 0:
                        load(relb[:, :], io["rel_bias"], "rel")
                        load(buck[:, :], io["c_bucket"], "buck")
                        load(sinks, bass.AP(tensor=io["sinks"].tensor, offset=0, ap=[[0, P], [1, SW_HEADS]]), "sinks")
                        pool.memset(brow[:, :], NEG).then_inc(*mark("bias_row_clear", ("brow0",)))
                elif kind == "bias":
                    pool.wait_ge(*at(("brow",)))
                    load(scratch, brow[:, :].rearrange("h (a c) -> h a c", a=1).to_broadcast([SW_HEADS, P, BW]), "bias_rows")
                    pool.wait_ge(*at(("loaded", "bias_rows")))
                    load(bias[:, :, :], bass.AP(tensor=scratch.tensor, offset=P - 1, ap=[[BW - 1, P], [P * BW, SW_HEADS], [1, T]]), "bias")
                elif kind == "ple_input" and args[0] == 1:
                    pool.wait_ge(*at(("pe", last_of("down1"))))
                    load(mem[:, :, :], io["mem_2"][0].rearrange("(t p) d -> p t d", p=P), "mem")
                elif kind == "turn" and args == ("blk2", 3):
                    pool.wait_ge(*at(("pe", last_of("mv"))))
                    pool.wait_ge(*at(("ev", last_of("gate1"))))
                    load(wsp_raw, io["w_spatial_2"][0].rearrange("g t s -> t g s"), "wsp")
                    load(bsp[:, :, :].rearrange("p g t -> p (g t)"),
                         bass.AP(tensor=io["b_spatial_2"].tensor, offset=0, ap=[[0, P], [1, GROUPS * P]]), "bsp")
                    load(causal[:, :], io["c_causal"], "causal")
                    load(small[:, 0:64], io["c_rope"], "rope")
                    pool.wait_ge(*at(("loaded", "wsp")))
                    pool.affine_select(out=wsp_raw, in_=wsp_raw, compare_op=ALU.is_ge, fill=0.0, base=0, pattern=[[0, GROUPS], [-1, P]], channel_multiplier=1).then_inc(*mark("spatial_masked", ("wspm",)))
                elif kind == "y_split":
                    pool.wait_ge(*at(("yb", "a", 3)))
                    load(gfin[:, :], bass.AP(tensor=io["final_norm_g_2"].tensor, offset=0, ap=[[0, P], [1, D]]), "gfin")

        @block.tensor
        def _(pe):
            reader = {}

            def claim(b, event):
                if b in reader:
                    pe.wait_ge(*at(reader[b]))
                reader[b] = event

            def panel(n):
                stage, i, name, kind, _where = PANELS[n]
                xh, xl, k0, needs = XIN[stage]
                wh, wl = whi[n % RING], wlo[n % RING]
                pe.wait_ge(*at(("lo", n)))

                def input_ready(k):
                    if k == 6 and n in LATE_TURN:
                        turn(LATE_TURN[n], 3)
                    for before in needs.get(k, ()):
                        pe.wait_ge(*at(before))
                if kind == "T":
                    b = pb(n)
                    claim(b, ("ev", n) if not stage.startswith("gate") else ("a", n))
                    wv = [w[:, :].rearrange("p (k n) -> p k n", k=KT) for w in (wh, wl)]
                    for t in range(TT):
                        for k in range(KT):
                            if t == 0 and i == 0:
                                input_ready(k)
                            for m, (x, w) in enumerate(((xh, 0), (xh, 1), (xl, 0))):
                                mm = pe.matmul(bank[b][:, t * 256:t * 256 + 256], x[:, k, t * P:(t + 1) * P], wv[w][:, k, :],
                                               start=(k == 0 and m == 0), stop=(k == KT - 1 and m == 2))
                elif kind == "F":
                    b = pb(n)
                    claim(b, ("ev", n))
                    wv = [w[:, :].rearrange("p (k n) -> p k n", k=KT) for w in (wh, wl)]
                    for c in range(2):
                        for k in range(KT):
                            if c == 0 and i == 0:
                                input_ready(k)
                            for m, (x, w) in enumerate(((xh, 0), (xl, 0), (xh, 1))):
                                mm = pe.matmul(bank[b][:, c * 256:c * 256 + 256], wv[w][:, k, c * P:(c + 1) * P], x[:, k, :],
                                               start=(k == 0 and m == 0), stop=(k == KT - 1 and m == 2))
                elif kind == "BT":
                    last, l, down = n == last_of(stage), int(stage[-1]), stage.startswith("down")
                    if down:
                        pe.wait_ge(*at(("gl", l, 2 * i + 1)))
                    else:
                        input_ready(0)
                    out_bank = lambda t, half: 2 * t + half if down else ppb(l, t, half)
                    if i == 0:
                        for t in range(TT):
                            for half in range(2):
                                claim(out_bank(t, half), ("h", stage, t) if down else ("ev", FIRST[f"gate{l}"] + 2 * half + 1))
                    wv = [w[:, :].rearrange("p (k n) -> p k n", k=2) for w in (wh, wl)]
                    for t in range(TT):
                        for k in range(2):
                            for m, (x, w) in enumerate(((xh, 0), (xh, 1), (xl, 0))):
                                for half in range(2):
                                    mm = pe.matmul(bank[out_bank(t, half)][:, :], x[:, 2 * i + k, t * P:(t + 1) * P],
                                                   wv[w][:, k, half * 512:half * 512 + 512],
                                                   start=(i == 0 and k == 0 and m == 0), stop=(last and k == 1 and m == 2))
                        if last and t == 0:
                            mm.then_inc(*mark("product", ("tok0", stage)))
                else:
                    last = n == last_of(stage)
                    if i == 0:
                        input_ready(0)
                        for b in range(4):
                            claim(b, ("yb", stage[-1], b))
                    wv = [w[:, :].rearrange("p (k n) -> p k n", k=2) for w in (wh, wl)]
                    for f in range(KT):
                        for k in range(2):
                            for m, (x, w) in enumerate(((xh, 0), (xl, 0), (xh, 1))):
                                mm = pe.matmul(bank[f // 2][:, (f % 2) * 256:(f % 2) * 256 + 256],
                                               wv[w][:, k, f * P:(f + 1) * P], x[:, k0 + 2 * i + k, :],
                                               start=(i == 0 and k == 0 and m == 0 and f % 2 == 0),
                                               stop=(last and k == 1 and m == 2), skip_group_check=True)
                mm.then_inc(*mark("product", ("pe", n)))
                if n in ROWS_AFTER:
                    k = ROWS_AFTER[n]
                    pe.wait_ge(*at(("rstd", k)))
                    claim(0, ("rows", k))
                    for t in range(TT):
                        mm = pe.transpose(bank[0][:, t * P:(t + 1) * P], rstd[k][:, t:t + 1].to_broadcast([P, P]), ident[:, :])
                    mm.then_inc(*mark("turned", ("tr", "rows", k)))

            def turn(k, j):
                src = mem if k == "mem" else h
                pe.wait_ge(*at(("loaded", "ident")))
                if k == "mem":
                    pe.wait_ge(*at(("xn", k, 0)))
                    pe.wait_ge(*at(("xn", k, 1)))
                else:
                    pe.wait_ge(*at(columns_ready(k, j)))
                b = turn_bank(k, j)
                claim(b, ("xl", k, j))
                for q in range(2):
                    for t in range(TT):
                        kt = 2 * j + q
                        mm = pe.transpose(bank[b][:, q * 256 + t * P:q * 256 + (t + 1) * P], src[:, t, kt * P:(kt + 1) * P], ident[:, :])
                mm.then_inc(*mark("turned", ("tr", k, j)))

            def three_blocks(b, src, width):
                pe.transpose(bank[b][:, 0:P], src[:, 0, 0:P], ident[:, :])
                pe.transpose(bank[b][:, P:2 * P], src[:, 1, 0:P], ident[:, :])
                return pe.transpose(bank[b][:, 2 * P:3 * P], src[:, 1, P:2 * P], ident[:, :])

            def weigh(dst, v0, v1, w):
                pe.matmul(dst(0), v0, w[:, 0:2 * P], start=True, stop=False)
                return pe.matmul(dst(P), v1, w[:, 2 * P:3 * P], start=False, stop=True)

            for step in SCHEDULE:
                kind, args = step[0], step[1:]
                if kind == "panel":
                    panel(args[0])
                elif kind == "setup":
                    pe.wait_ge(*at(("loaded", "ident")))
                    pe.wait_ge(*at(("loaded", "vectors" if args[0] else "vectors0")))
                    for g in ((1, 2, 3, 4) if args[0] else (0,)):
                        claim(4 + g % 4, ("vec", g))
                        mm = pe.transpose(bank[4 + g % 4][:, 0:VEC_ROWS[g]], xn[0:VEC_ROWS[g], 0, g * P:(g + 1) * P], ident[0:VEC_ROWS[g], 0:VEC_ROWS[g]])
                        mm.then_inc(*mark("turned", ("tr", "vec", g)))
                elif kind == "turn":
                    turn(*args)
                elif kind == "hg_scores":
                    li = args[0]
                    if li < 0:
                        pe.wait_ge(*at(("xs", li)))
                        claim(0, ("sc", -1, 0))
                        for hd in range(HG_HEADS):
                            X = xs_buf[1]
                            mm = pe.matmul(bank[0][:, hd * P:(hd + 1) * P], X[:, hd, 0:P], X[:, hd, P:T], start=True, stop=True)
                        mm.then_inc(*mark("scores", ("ps", -1, 0)))
                    else:
                        if LEVELS[li]:
                            pe.wait_ge(*at(("xs", li)))
                            A = B = xs_buf[li % 2]
                        else:
                            pe.wait_ge(*at(("kk",)))
                            A, B = kk, qf
                        for j in range(2):
                            b = (2 * li + j + 2) % 4
                            claim(b, ("prod", li, j))
                            for q in range(2):
                                for t in range(TT):
                                    hd = 2 * j + q
                                    mm = pe.matmul(bank[b][:, (2 * q + t) * P:(2 * q + t + 1) * P],
                                                   A[:, hd, t * P:(t + 1) * P], B[:, hd, t * P:(t + 1) * P], start=True, stop=True)
                            mm.then_inc(*mark("scores", ("ps", li, j)))
                elif kind == "hg_out":
                    pe.wait_ge(*at(("sc", len(LEVELS) - 1, 1)))
                    pe.wait_ge(*at(("sc", -1, 0)))
                    pe.wait_ge(*at(("ev", last_of("ib"))))
                    for t in range(TT):
                        claim(t, ("on", t))
                        for hd in range(HG_HEADS):
                            o, v = bank[t][:, hd * P:(hd + 1) * P], ib[:, :, hd * P:(hd + 1) * P]
                            if t == 0:
                                mm = pe.matmul(o, sc[:, hd, 0:P], v[:, 0, :], start=True, stop=True)
                            else:
                                pe.matmul(o, sc[:, hd, P:2 * P], v[:, 0, :], start=True, stop=False)
                                mm = pe.matmul(o, sc[:, hd, 2 * P:3 * P], v[:, 1, :], start=False, stop=True)
                        mm.then_inc(*mark("weighted", ("hgo", t)))
                elif kind == "hg_turn":
                    pe.wait_ge(*at(("gated", 0)))
                    pe.wait_ge(*at(("gated", 1)))
                    for j in range(2):
                        claim(2 + j, ("xl", "hg", j))
                        for q in range(2):
                            for t in range(TT):
                                mm = pe.transpose(bank[2 + j][:, q * 256 + t * P:q * 256 + (t + 1) * P], on[:, t, 2 * j + q, :], ident[:, :])
                        mm.then_inc(*mark("turned", ("tr", "hg", j)))
                elif kind == "sb_scores":
                    i = args[0]
                    pe.wait_ge(*at(("ev", last_of("qa"))))
                    pe.wait_ge(*at(("ev", last_of("ka"))))
                    for r in range(2):
                        hd = 2 * i + r
                        b, q = 4 + hd % 4, slice(64 * r, 64 * r + 64)
                        claim(b, ("z", hd))
                        pe.matmul(bank[b][:, 0:T], kaT[q, i, 0:P], qaT[q, i, :], start=True, stop=True)
                        mm = pe.matmul(bank[b][:, T:T + P], kaT[q, i, P:T], qaT[q, i, P:T], start=True, stop=True)
                        mm.then_inc(*mark("scores", ("sbz", hd)))
                elif kind == "sb_weights":
                    i = args[0]
                    pe.wait_ge(*at(("spm", i)))
                    pe.wait_ge(*at(("loaded", "tri")))
                    pe.wait_ge(*at(("ones",)))
                    for r in range(2):
                        hd = 2 * i + r
                        b, a = 4 + hd % 4, sp_[:, hd, :]
                        claim(b, ("d", hd))
                        pe.matmul(bank[b][:, 0:T], tri[:, :], a[:, 0:T], start=True, stop=False)
                        pe.matmul(bank[b][:, P:T], ones[:, :], a[:, T:T + P], start=False, stop=True)
                        mm = pe.matmul(bank[b][:, T:T + P], tri[:, :], a[:, T:T + P], start=True, stop=True)
                        mm.then_inc(*mark("weighted", ("sbr", hd)))
                elif kind == "sb_out":
                    i = args[0]
                    b = 4 + i
                    pe.wait_ge(*at(("wm", i)))
                    pe.wait_ge(*at(("ev", last_of("va"))))
                    claim(b, ("xl", "sb", i))
                    for r in range(2):
                        hd = 2 * i + r
                        mm = weigh(lambda c: bank[b][64 * r:64 * r + 64, c:T], va[:, 0, hd * 64:hd * 64 + 64],
                                   va[:, 1, hd * 64:hd * 64 + 64], zs[:, hd, :])
                    mm.then_inc(*mark("weighted", ("sbo", i)))
                elif kind == "ple_input":
                    l = args[0]
                    pe.wait_ge(*at(("loaded", f"p{l}")))
                    claim(4, ("ptl", l))
                    for q in range(2):
                        for t in range(TT):
                            mm = pe.transpose(bank[4][:, q * 256 + t * P:q * 256 + (t + 1) * P], praw[:, t, q * P:(q + 1) * P], ident[:, :])
                    mm.then_inc(*mark("turned", ("pt", l, 1)))
                elif kind == "bias":
                    pe.wait_ge(*at(("loaded", "rel")))
                    pe.wait_ge(*at(("loaded", "buck")))
                    claim(0, ("brow",))
                    pe.matmul(bank[0][0:16, 0:P], relb[:, :], buck[:, :], start=True, stop=True).then_inc(*mark("weighted", ("brp",)))
                elif kind == "sw_norm":
                    for j in range(6):
                        if j % 4 == 0 or j == 4:
                            pe.wait_ge(*at(("qkn", 0)))
                            pe.wait_ge(*at(("qkn", 1)))
                        b = 4 + j % 4
                        claim(b, ("qsT", j))
                        for q in range(2):
                            for t in range(TT):
                                mm = pe.transpose(bank[b][:, q * 256 + t * P:q * 256 + (t + 1) * P],
                                                  qkn[:, t, 4 * j + 2 * q:4 * j + 2 * q + 2, :].rearrange("p a d -> p (a d)"), ident[:, :])
                        mm.then_inc(*mark("turned", ("tr", "sw", j)))
                elif kind == "sw_logits":
                    g = args[0]
                    pe.wait_ge(*at(("qsT", 5)))
                    for j in range(4):
                        hd = 4 * g + j
                        q = slice(64 * (hd % 2), 64 * (hd % 2) + 64)
                        claim(j, ("swm", g, j))
                        pe.matmul(bank[j][:, 0:P], qsT[q, hd // 2, 0:P], ksT[q, g, 0:P], start=True, stop=True)
                        mm = pe.matmul(bank[j][:, T:2 * T], qsT[q, hd // 2, P:T], ksT[q, g, :], start=True, stop=True)
                        mm.then_inc(*mark("scores", ("swz", g, j)))
                elif kind == "sw_weights":
                    g = args[0]
                    for j in range(4):
                        pe.wait_ge(*at(("swn", g, j)))
                        claim(4 + j, ("swt", g, j))
                        three_blocks(4 + j, le_s[:, j, :, :], T).then_inc(*mark("turned", ("tr", "sww", g, j)))
                elif kind == "sw_out":
                    g = args[0]
                    for q in range(2):
                        pe.wait_ge(*at(("swt", g, 2 * q)))
                        pe.wait_ge(*at(("swt", g, 2 * q + 1)))
                        pe.wait_ge(*at(("ev", last_of("vs"))))
                        claim(q, ("xl", "sw", 2 * g + q))
                        for r in range(2):
                            mm = weigh(lambda c: bank[q][64 * r:64 * r + 64, c:T], vsw[:, 0, 64 * g:64 * g + 64],
                                       vsw[:, 1, 64 * g:64 * g + 64], wT_s[:, 2 * q + r, :])
                        mm.then_inc(*mark("weighted", ("swo", 2 * g + q)))
                elif kind == "x_logits":
                    g = args[0]
                    pe.wait_ge(*at(("ev", last_of("mk"))))
                    pe.wait_ge(*at(("ev", last_of("qc"))))
                    for j in range(2):
                        hd = 2 * g + j
                        claim(j, ("e", "x", hd))
                        for t in range(TT):
                            mm = pe.matmul(bank[j][:, t * T:(t + 1) * T], qc[:, hd, t * P:(t + 1) * P], mk[:, hd, :], start=True, stop=True)
                        mm.then_inc(*mark("scores", ("xz", hd)))
                elif kind == "x_weights":
                    g = args[0]
                    for j in range(2):
                        hd = 2 * g + j
                        pe.wait_ge(*at(("n", "x", hd)))
                        claim(2 + j, ("wT", "x", hd))
                        for m in range(2):
                            for t in range(TT):
                                mm = pe.transpose(bank[2 + j][:, m * T + t * P:m * T + (t + 1) * P], le[:, j, t, m * P:(m + 1) * P], ident[:, :])
                        mm.then_inc(*mark("turned", ("trw", "x", hd)))
                elif kind == "x_out":
                    g = args[0]
                    for j in range(2):
                        hd = 2 * g + j
                        pe.wait_ge(*at(("wT", "x", hd)))
                        pe.wait_ge(*at(("ev", last_of("mv"))))
                        claim(j, ("og", "c", hd))
                        for m in range(2):
                            mm = pe.matmul(bank[j][:, 0:T], mv[:, m, hd * P:(hd + 1) * P], wT[:, j, m, :], start=(m == 0), stop=(m == 1))
                        mm.then_inc(*mark("weighted", ("oz", "c", hd)))
                elif kind == "rope_turn":
                    pe.wait_ge(*at(("roped",)))
                    for j in range(6):
                        b = 2 + j % 2
                        claim(b, ("qkF", j))
                        for q in range(2):
                            for t in range(TT):
                                c = (2 * j + q) * P
                                mm = pe.transpose(bank[b][:, q * T + t * P:q * T + (t + 1) * P], qkm[:, t, c:c + P], ident[:, :])
                        mm.then_inc(*mark("turned", ("tr", "rope", j)))
                elif kind == "spatial":
                    pe.wait_ge(*at(("wspm",)))
                    for j in range(2):
                        claim(2 + j, ("wspT", j))
                        for q in range(3):
                            mm = pe.transpose(bank[2 + j][:, q * P:(q + 1) * P], wsp_raw[:, 3 * j + q, :], ident[:, :])
                        mm.then_inc(*mark("turned", ("tr", "wsp", j)))
                elif kind == "a_logits":
                    g = args[0]
                    pe.wait_ge(*at(("qkF", 4)))
                    pe.wait_ge(*at(("qkF", 5)))
                    for j in range(2):
                        hd = 2 * g + j
                        claim(j, ("am", hd))
                        pe.matmul(bank[j][:, 0:P], qF[:, hd, 0:P], kF[:, hd, 0:P], start=True, stop=True)
                        mm = pe.matmul(bank[j][:, T:2 * T], qF[:, hd, P:T], kF[:, hd, :], start=True, stop=True)
                        mm.then_inc(*mark("scores", ("az", hd)))
                elif kind == "a_weights":
                    g = args[0]
                    for j in range(2):
                        hd = 2 * g + j
                        pe.wait_ge(*at(("n", "a", hd)))
                        claim(2 + j, ("wT", "a", hd))
                        three_blocks(2 + j, le[:, j, :, :], T).then_inc(*mark("turned", ("trw", "a", hd)))
                elif kind == "a_out":
                    g = args[0]
                    for j in range(2):
                        hd = 2 * g + j
                        pe.wait_ge(*at(("wT", "a", hd)))
                        pe.wait_ge(*at(("ev", last_of("va2"))))
                        claim(j, ("og", "a", hd))
                        w = wT[:, j, :, :].rearrange("p a b -> p (a b)")
                        mm = weigh(lambda c: bank[j][:, c:T], va2[:, 0, hd * P:(hd + 1) * P], va2[:, 1, hd * P:(hd + 1) * P], w)
                        mm.then_inc(*mark("weighted", ("oz", "a", hd)))
                elif kind == "mixed":
                    pe.wait_ge(*at(("vn", 0)))
                    pe.wait_ge(*at(("vn", 1)))
                    pe.wait_ge(*at(("wspT", 0)))
                    pe.wait_ge(*at(("wspT", 1)))
                    for j in range(3):
                        claim(j, ("mixg", 2 * j + 1))
                        for q in range(2):
                            g = 2 * j + q
                            for t in range(TT):
                                mm = pe.matmul(bank[j][:, q * T + t * P:q * T + (t + 1) * P], vb[:, t, g * P:(g + 1) * P], wsp[:, g, :], start=True, stop=True)
                        mm.then_inc(*mark("weighted", ("mixp", j)))

        @block.scalar
        def _(act):
            def split(n):
                if n < len(PANELS):
                    act.wait_ge(*at(("raw", n)))
                    if n >= RING:
                        act.wait_ge(*at(("pe", n - RING)))
                    act.activation(whi[n % RING][:, :], raw[n % RAW][:, :], ACT.Copy).then_inc(*mark("weights_hi", ("hi", n)))

            for name, pre, r0, n in VEC_LOADS:
                src, q = io[name], r0 % P
                for j in pre:
                    src = src[j]
                if r0 < P:
                    for k in range(2 if n == 1 and name != "hg_out_norm" else 1):
                        dst = xn[q:q + 1, 0, 64 * k:64 * k + 64] if name in ("q_norm", "k_norm") else xn[q:q + n, 0, 0:P]
                        act.dma_start(dst, src.rearrange("(a c) -> a c", a=n)).then_inc(*mark("load_vectors0", ("loaded", "vectors0"), by=16))

            def parts(src, gain, dst, event, *first):
                for before in first:
                    act.wait_ge(*at(before))
                if gain is None:
                    act.activation(dst, src, ACT.Copy).then_inc(*mark("input_hi", event))
                else:
                    act.activation(dst, src, ACT.Copy, scale=gain).then_inc(*mark("input_hi", event))

            def ffn_gate(l, i):
                act.wait_ge(*at(("conv", l, i)))
                if l > 0 or i >= 2:
                    act.wait_ge(*at(("gf", l, i - 2) if i >= 2 else ("gf", l - 1, FT - 2 + i)))
                act.activation(sgate[i % 2][:, :], cc[i % 3][:, 0, :], ACT.Silu).then_inc(*mark("gate_done", ("sg", l, i)))

            def ffn_hi(l, i):
                act.wait_ge(*at(("gf", l, i)))
                act.activation(GH[:, i, :], gf[i % 2][:, :], ACT.Copy).then_inc(*mark("gated_hi", ("gh", l, i)))

            def panel(n):
                stage, i, name, kind, _where = PANELS[n]
                b = pb(n)
                c2, cT = slice(2 * i, 2 * i + 2), slice(256 * i, 256 * i + 256)
                ev = ("ev", n)
                if not stage.startswith("gate"):
                    split(n + RING)
                if n in ROWS_AFTER:
                    k = ROWS_AFTER[n]
                    act.wait_ge(*at(("tr", "rows", k)))
                    act.activation(ROWS[k], bank[0][:, 0:T], ACT.Copy).then_inc(*mark("rows", ("rows", k)))
                if kind == "T" and stage in NORM_OF:
                    norm = NORM_OF[stage]
                    if stage.startswith("gate"):
                        if i >= 2:
                            act.wait_ge(*at(("ev", n - 2)))
                        elif stage == "gate1":
                            act.wait_ge(*at(("ev", last_of("gate0"))))
                        dst, func, event = gate[i % 2][:, :, :], ACT.Sigmoid, ("a", n)
                    else:
                        func, event = ACT.Silu if stage == "gb" else ACT.Copy, ev
                        a = 1024 if stage == "ks" else 256 * i
                        dst = {"ib": ib, "gb": gbs, "va": va, "qs": qk, "ks": qk, "vs": vsw, "qka": qkm, "va2": va2, "vb": vb}[stage][:, :, a:a + 256]
                    act.wait_ge(*at(("rstd", norm)))
                    act.wait_ge(*at(("pe", n)))
                    for t in range(TT):
                        act.activation(dst[:, t, :], two(b)[:, t, :], func, scale=rstd[norm][:, t:t + 1]).then_inc(*mark("projected", event))
                elif kind == "F" and stage in ("qb", "gc", "ga", "gb2", "mc", "mb", "ma"):
                    dst = {"qb": qf, "gc": gc, "ga": ga, "gb2": ubs, "mc": msig[0], "mb": msig[1], "ma": msig[0]}[stage][:, c2, :]
                    act.wait_ge(*at(("scaled", n)))
                    act.activation(dst, dst, ACT.Sigmoid if stage[0] == "m" else ACT.Silu).then_inc(*mark("projected", ev))
                elif stage == "fb":
                    act.wait_ge(*at(("scaled", n)))
                    act.activation(kk[:, c2, :], bdec[:, c2, :], ACT.Sigmoid, scale=-1.0).then_inc(*mark("projected", ("sig", i)))
                    act.activation(bdec[:, c2, :], bdec[:, c2, :], ACT.Sigmoid).then_inc(*mark("projected", ev))
                elif stage.startswith("up"):
                    l = int(stage[-1])
                    if l > 0 or i >= 3:
                        act.wait_ge(*at(("gf", l, i - 3) if i >= 3 else ("gf", l - 1, FT - 1)))
                    act.wait_ge(*at(("scaled", n)))
                    for c in range(2):
                        j = c * FT + i
                        act.activation(cc[i % 3][:, c, :], ub_[i % 2][:, c, :], ACT.Identity, scale=vec("ffn_conv", l, 2)(j), bias=vec("ffn_conv_b", l)(j)).then_inc(*mark("projected", ("a", n)))
                elif stage == "mk":
                    act.wait_ge(*at(("pe", n)))
                    act.activation(mk[:, c2, :], two(b), ACT.Copy).then_inc(*mark("projected", ev))
                elif stage == "mv":
                    act.wait_ge(*at(("pe", n)))
                    act.activation(mv[:, :, cT], two(b), ACT.Copy).then_inc(*mark("projected", ev))
                if stage.startswith("gate"):
                    split(n + RING)
                if stage.startswith("up"):
                    if i >= 1:
                        ffn_gate(l, i - 1)
                    if i >= 2:
                        ffn_hi(l, i - 2)

            def soft(tag, hd, j, scale):
                act.wait_ge(*at(("neg", tag, hd)))
                for t in range(TT):
                    c = 2 * j + t
                    if tag == "x":
                        src, dst = bank[j][:, t * T:(t + 1) * T], le[:, j, t, :]
                    else:
                        w = slice(0, P) if t == 0 else slice(0, T)
                        src = dst = le[:, j, t, w]
                    act.activation(dst, src, ACT.Exp, scale=scale, bias=s_neg[:, c:c + 1], accum_out=s_sum[:, c:c + 1]).then_inc(*mark("exponentials", ("e", tag, hd)))

            for step in SCHEDULE:
                kind, args = step[0], step[1:]
                if kind == "panel":
                    panel(args[0])
                elif kind == "split":
                    split(args[0])
                elif kind == "setup":
                    for g in ((1, 2, 3, 4) if args[0] else (0,)):
                        act.wait_ge(*at(("tr", "vec", g)))
                        act.activation(vecs[:, g, 0:VEC_ROWS[g]], bank[4 + g % 4][:, 0:VEC_ROWS[g]], ACT.Copy).then_inc(*mark("vectors", ("vec", g)))
                    if args[0]:
                        act.wait_ge(*at(("lb0",)))
                        act.activation(lb_tmp, lb_tmp, ACT.Exp).then_inc(*mark("vectors", ("lbe",)))
                elif kind == "square":
                    k, j = args
                    act.wait_ge(*at(columns_ready(k, j)))
                    if k == "final" and j == 0:
                        act.wait_ge(*at(("xl", "y", 3)))
                    if j:
                        act.wait_ge(*at(("sq", k, j - 1)))
                    for t in range(TT):
                        dst = xn[:, t, 0:256] if k == "final" else junk[t]
                        act.activation(dst, h[:, t, 256 * j:256 * j + 256], ACT.Square, accum_out=ssq[k][:, 4 * t + j:4 * t + j + 1]).then_inc(*mark("squared", ("sq", k, j)))
                elif kind == "stats":
                    k = args[0]
                    if k == "mem":
                        act.wait_ge(*at(("loaded", "mem")))
                        for t in range(TT):
                            for j in range(4):
                                if t or j:
                                    act.wait_ge(*at(("sq", k, 4 * t + j - 1)))
                                act.activation(mem_junk[:, 0:256], mem[:, t, 256 * j:256 * j + 256], ACT.Square, accum_out=ssq[k][:, 4 * t + j:4 * t + j + 1]).then_inc(*mark("squared", ("sq", k, 4 * t + j)))
                        act.wait_ge(*at(("rstd", k)))
                        act.activation(mem[:, 1, :], mem[:, 1, :], ACT.Copy, scale=rstd[k][:, 1:2]).then_inc(*mark("normalized", ("xn", k, 1)))
                    elif k == "final":
                        act.wait_ge(*at(("rstd", k)))
                        act.wait_ge(*at(("hgn", 3)))
                        act.activation(result[:, 1, :], result[:, 1, :], ACT.Copy, scale=rstd[k][:, 1:2]).then_inc(*mark("result1", ("result", 1)))
                elif kind in ("turn", "turn_last"):
                    k, j = args if kind == "turn" else (args[0], 3)
                    if k in XUSED:
                        act.wait_ge(*at(XUSED[k]))
                    act.wait_ge(*at(("vec", 0)))
                    act.wait_ge(*at(("tr", k, j)))
                    for q in range(2):
                        kt = 2 * j + q
                        act.activation(DEST[k][0][:, kt, :], two(turn_bank(k, j))[:, q, :], ACT.Copy, scale=GAIN[k](kt)).then_inc(*mark("input_hi", ("xh", k, j)))
                elif kind == "hg_decay":
                    act.wait_ge(*at(("f",)))
                    act.activation(ex[:, :, :], bdec[:, :, :], ACT.Ln).then_inc(*mark("levels", ("logf",)))
                elif kind == "hg_level":
                    li = args[0]
                    if li < 0 or LEVELS[li]:
                        e = ex if li % 2 == 0 else exb
                        act.wait_ge(*at(("dd", li)))
                        act.activation(e[:, :, :], e[:, :, :], ACT.Exp).then_inc(*mark("levels", ("ex", li)))
                elif kind == "sb_scores":
                    i = args[0]
                    if i == 0:
                        act.wait_ge(*at(("loaded", "reset")))
                    for r in range(2):
                        hd = 2 * i + r
                        b = 4 + hd % 4
                        act.wait_ge(*at(("sbz", hd)))
                        act.activation(sp_[:, hd, :], bank[b][:, 0:384], ACT.Abs).then_inc(*mark("sb_scores", ("az0", hd)))
                        act.activation(zs[:, hd, :], bank[b][:, 0:384], ACT.Copy).then_inc(*mark("sb_scores", ("z", hd)))
                elif kind == "sb_log":
                    for i in range(4):
                        c = slice(2 * i, 2 * i + 2)
                        act.wait_ge(*at(("z", 2 * i + 1)))
                        act.activation(sp_[:, c, :], sp_[:, c, :], ACT.Exp, scale=-1.0).then_inc(*mark("sb_logs", ("sbe", i)))
                    for i in range(4):
                        c = slice(2 * i, 2 * i + 2)
                        act.wait_ge(*at(("sbe", i)))
                        act.activation(sp_[:, c, :], sp_[:, c, :], ACT.Ln, bias=1.0).then_inc(*mark("sb_logs", ("sbl", i)))
                elif kind == "hg_out":
                    for t in range(TT):
                        act.wait_ge(*at(("hgo", t)))
                        if t == 0:
                            act.wait_ge(*at(("sc", len(LEVELS) - 1, 1)))
                        act.activation(prod4[:, t, :], bank[t][:, :], ACT.Square).then_inc(*mark("squared", ("hgsq", t)))
                elif kind == "hg_turn":
                    for j in range(2):
                        parts(two(2 + j), vec("hg_out_norm", 0)(0), XH[:, 4 + 2 * j:6 + 2 * j, :], ("xh", "hg", j),
                              ("tr", "hg", j), ("pe", last_of("va")))
                elif kind == "sb_weights":
                    i = args[0]
                    act.wait_ge(*at(("d", 2 * i + 1)))
                    c = slice(2 * i, 2 * i + 2)
                    act.activation(zs[:, c, :], zs[:, c, :], ACT.Exp).then_inc(*mark("sb_weights", ("w", i)))
                elif kind == "sb_out":
                    i = args[0]
                    parts(bank[4 + i][:, 0:T], None, XH[:, i, :], ("xh", "sb", i), ("sbo", i), ("pe", last_of("va")))
                elif kind == "up_tail":
                    l = args[0]
                    ffn_gate(l, FT - 1)
                    ffn_hi(l, FT - 2)
                    ffn_hi(l, FT - 1)
                elif kind == "ple_input":
                    l = args[0]
                    if l == 1:
                        act.wait_ge(*at(("pe", last_of("pp0"))))
                    parts(two(4), None, PTH[:, :, :], ("pth", l), ("pt", l, 1))
                elif kind == "sw_norm":
                    for t in range(TT):
                        act.wait_ge(*at(("ev", last_of("ks"))))
                        act.activation(sq[:, t, :], qk[:, t, :], ACT.Square).then_inc(*mark("squared", ("swsq", t)))
                    for j in range(6):
                        act.wait_ge(*at(("tr", "sw", j)))
                        if j < 4:
                            act.activation(qsT[:, 2 * j:2 * j + 2, :], two(4 + j % 4), ACT.Copy, scale=q_gain).then_inc(*mark("sw_turned", ("qsT", j)))
                        else:
                            act.activation(ksT[:, 2 * j - 8:2 * j - 6, :], two(4 + j % 4), ACT.Copy, scale=vec("k_norm", 0)(0)).then_inc(*mark("sw_turned", ("qsT", j)))
                elif kind == "sw_logits":
                    g = args[0]
                    act.wait_ge(*at(("swneg", g)))
                    for j in range(4):
                        for t in range(TT):
                            c = 2 * j + t
                            v = le_s[:, j, t, 0:P if t == 0 else T]
                            act.activation(v, v, ACT.Exp, bias=s_neg[:, c:c + 1], accum_out=s_sum[:, c:c + 1]).then_inc(*mark("exponentials", ("swe", g, j)))
                    act.activation(s_exp, s_exp, ACT.Exp).then_inc(*mark("exponentials", ("swx", g)))
                elif kind == "sw_weights":
                    g = args[0]
                    for j in (0, 2):
                        act.wait_ge(*at(("tr", "sww", g, j)))
                        if g:
                            act.wait_ge(*at(("swo", 2 * g - 1)))
                        act.activation(wT_s[:, j, :], bank[4 + j][:, 0:384], ACT.Copy).then_inc(*mark("turned_copied", ("swt", g, j)))
                elif kind == "sw_out":
                    g = args[0]
                    for q in range(2):
                        parts(bank[q][:, 0:T], None, XH[:, 2 * g + q, :], ("xh", "sw", 2 * g + q), ("swo", 2 * g + q), ("pe", last_of("gate0")))
                elif kind == "x_logits":
                    g = args[0]
                    for j in range(2):
                        soft("x", 2 * g + j, j, HEAD ** -0.5)
                elif kind == "a_logits":
                    g = args[0]
                    for j in range(2):
                        soft("a", 2 * g + j, j, HEAD ** -0.5)
                elif kind in ("x_weights", "a_weights"):
                    tag, g = kind[0], args[0]
                    hd = 2 * g
                    act.wait_ge(*at(("trw", tag, hd)))
                    if tag == "x" and g:
                        act.wait_ge(*at(("oz", "c", hd - 1)))
                    elif tag == "a":
                        act.wait_ge(*at(("oz", "a", hd - 1) if g else ("oz", "c", X_HEADS - 1)))
                    n = 2 * T if tag == "x" else 384
                    act.activation(wT[:, 0, :, :].rearrange("p a b -> p (a b)")[:, 0:n], bank[2][:, 0:n], ACT.Copy).then_inc(*mark("turned_copied", ("wT", tag, hd)))
                elif kind in ("x_out", "a_out"):
                    b, g = ("c" if kind[0] == "x" else "a"), args[0]
                    src = gc if b == "c" else ga
                    for j in range(2):
                        hd = 2 * g + j
                        act.wait_ge(*at(("og", b, hd)))
                        act.wait_ge(*at(("xn", "mem", 1)))
                        act.wait_ge(*at(("pe", last_of("down1"))))
                        act.activation(GH[:, OUT_AT[b] + hd, :], src[:, hd, :], ACT.Copy).then_inc(*mark("gated_hi", ("oh", b, hd)))
                elif kind == "rope_turn":
                    for j in (0, 2, 4):
                        act.wait_ge(*at(("tr", "rope", j)))
                        dst = qF if j < 3 else kF
                        act.activation(dst[:, (2 * j) % 6:(2 * j) % 6 + 2, :], two(2), ACT.Copy).then_inc(*mark("turned_copied", ("qkF", j)))
                elif kind == "spatial":
                    for j in range(2):
                        act.wait_ge(*at(("tr", "wsp", j)))
                        act.activation(wsp[:, 3 * j:3 * j + 3, :].rearrange("p g t -> p (g t)"), bank[2 + j][:, 0:384], ACT.Copy).then_inc(*mark("turned_copied", ("wspT", j)))
                elif kind == "layer_norm":
                    act.wait_ge(*at(("roped",)))
                    act.wait_ge(*at(("tr", "wsp", 1)))
                    for t in range(TT):
                        act.wait_ge(*at(("lnm",)))
                        act.activation(xn[:, t, 0:768], vb[:, t, :], ACT.Square, bias=ln_neg[:, t:t + 1], accum_out=ln_ss[:, t:t + 1]).then_inc(*mark("squared", ("lnsq", t)))
                elif kind == "mixed":
                    for g in range(GROUPS):
                        act.wait_ge(*at(("og", "b", g)))
                        act.activation(GH[:, OUT_AT["b"] + g, :], ubs[:, g, :], ACT.Copy).then_inc(*mark("gated_hi", ("oh", "b", g)))
                elif kind == "y_split":
                    for j in range(4):
                        parts(y[:, 2 * j:2 * j + 2, :], None, XH[:, 2 * j:2 * j + 2, :], ("xh", "y", j), ("yb", "a", j), ("pe", last_of("ma")))

        @block.vector
        def _(dve):
            def split(n):
                if n < len(PANELS):
                    dve.wait_ge(*at(("hi", n)))
                    dve.tensor_tensor(wlo[n % RING][:, :], raw[n % RAW][:, :], plain(whi[n % RING][:, :]), ALU.subtract).then_inc(*mark("weights_lo", ("lo", n)))

            def rest(src, gain, hi, lo, name, event, *first):
                for before in first:
                    dve.wait_ge(*at(before))
                if gain is None:
                    return dve.tensor_tensor(lo, src, plain(hi), ALU.subtract).then_inc(*mark(name, event))
                return dve.scalar_tensor_tensor(lo, src, gain, plain(hi), ALU.mult, ALU.subtract).then_inc(*mark(name, event))

            def inverse_root(x, out, tmp):
                dve.tensor_scalar(tmp.bitcast(I32), x.bitcast(I32), 1, None, ALU.logical_shift_right).then_inc(*chained())
                dve.wait_ge(*chain())
                dve.tensor_scalar(out.bitcast(I32), tmp.bitcast(I32), -1.0, MAGIC, ALU.mult, ALU.add).then_inc(*chained())
                dve.wait_ge(*chain())
                for _ in range(3):
                    dve.tensor_tensor(tmp, out, out, ALU.mult).then_inc(*chained())
                    dve.wait_ge(*chain())
                    dve.scalar_tensor_tensor(tmp, x, -0.5, tmp, ALU.mult, ALU.mult).then_inc(*chained())
                    dve.wait_ge(*chain())
                    dve.scalar_tensor_tensor(out, tmp, 1.5, out, ALU.add, ALU.mult).then_inc(*chained())
                    dve.wait_ge(*chain())

            def hg_level(li):
                if li < 0 or LEVELS[li]:
                    e = ex if li % 2 == 0 else exb
                    X = xs_buf[li % 2]
                    half = LEVELS[li] if li >= 0 else P
                    if li >= 1 or li == 0:
                        for before in ([("xs", li - 2)] if li >= 1 else []):
                            dve.wait_ge(*at(before))
                    if half >= HG_CHUNK:
                        ends = [bdec[:, :, HG_CHUNK * (c + 1) - 1:HG_CHUNK * (c + 1)].to_broadcast([P, HG_HEADS, HG_CHUNK]) for c in range(4)]
                        part = lambda x, c: x[:, :, HG_CHUNK * c:HG_CHUNK * (c + 1)]
                        left = (0, 1) if half == P else (0, 2)
                        for c in range(4):
                            if c in left:
                                dve.tensor_tensor(part(e, c), ends[c], part(bdec, c), ALU.subtract).then_inc(*mark("exponents", ("dd_left", li), ("dd", li)))
                            elif half == P and c == 3:
                                dve.tensor_tensor(part(e, c), ends[2], part(bdec, c), ALU.add).then_inc(*mark("exponents", ("dd", li)))
                            else:
                                dve.tensor_copy(part(e, c), part(bdec, c)).then_inc(*mark("exponents", ("dd", li)))
                        if half == P:
                            dve.wait_ge(*at(("dd_left", li)))
                            dve.tensor_tensor(part(e, 0), part(e, 0), ends[1], ALU.add).then_inc(*mark("exponents", ("dd", li)))
                    else:
                        halves = lambda x: x[:, :, :].rearrange("p h (n c) -> p (h n) c", c=2 * half)
                        mid = halves(bdec)[:, :, half - 1:half].to_broadcast([P, HG_HEADS * T // (2 * half), half])
                        l, r = halves(bdec)[:, :, 0:half], halves(bdec)[:, :, half:2 * half]
                        dve.tensor_tensor(halves(e)[:, :, 0:half], mid, l, ALU.subtract).then_inc(*mark("exponents", ("dd0", li)))
                        dve.tensor_tensor(halves(e)[:, :, half:2 * half], r, mid, ALU.subtract).then_inc(*mark("exponents", ("dd", li)))
                    dve.wait_ge(*at(("ex", li)))
                    if li >= 1:
                        dve.wait_ge(*at(("ps", li - 2, 1 if li >= 2 else 0)))
                    halves = lambda x: x[:, :, :].rearrange("p h (n c) -> p (h n) c", c=2 * half)
                    dve.tensor_tensor(halves(X)[:, :, 0:half], halves(e)[:, :, 0:half], halves(kk)[:, :, 0:half], ALU.mult).then_inc(*mark("decayed", ("xs0", li)))
                    dve.tensor_tensor(halves(X)[:, :, half:2 * half], halves(e)[:, :, half:2 * half], halves(qf)[:, :, half:2 * half], ALU.mult).then_inc(*mark("decayed", ("xs", li)))

            def hg_mask(li):
                if li < 0:
                    dve.wait_ge(*at(("ps", li, 0)))
                    dve.tensor_copy(sc[:, :, P:2 * P], bank[0][:, :].rearrange("p (h c) -> p h c", h=HG_HEADS)).then_inc(*mark("cross_scores", ("sc", -1, 0)))
                    return
                dve.wait_ge(*at(("loaded", "levels")))
                for j in range(2):
                    b = (2 * li + j + 2) % 4
                    dve.wait_ge(*at(("ps", li, j)))
                    for before in ([("sc", li - 1, j)] if li >= 2 else []):
                        dve.wait_ge(*at(before))
                    out = blocks_of(sc, 2 * j) if li == 0 else blocks_of_prod(j)
                    mask = masks[:, li, :].rearrange("p (a b c) -> p a b c", a=1, b=1).to_broadcast([P, 2, 2, P])
                    events = [("prod", li, j)] + ([("sc", 0, j)] if li == 0 else [])
                    dve.tensor_tensor(out, bank[b][:, :].rearrange("p (h t c) -> p h t c", h=2, t=2), mask, ALU.mult).then_inc(*mark("masked_scores", *events))

            def taps(n):
                stage, i = PANELS[n][:2]
                dve.wait_ge(*at(("a", n)))
                for tap in (1, 0):
                    d = 2 - tap
                    for c in range(2):
                        v = cc[i % 3][:, c, d:T]
                        if tap == 0:
                            dve.wait_ge(*at(("tap", n, c)))
                        dve.scalar_tensor_tensor(v, ub_[i % 2][:, c, 0:T - d], vec("ffn_conv", int(stage[-1]), tap)(c * FT + i), v, ALU.mult, ALU.add).then_inc(*mark("convolved", ("conv", int(stage[-1]), i) if tap == 0 else ("tap", n, c)))

            def ffn_lo(l, i):
                rest(gf[i % 2][:, :], None, GH[:, i, :], GL[:, i, :], "gated_lo", ("gl", l, i), ("gh", l, i))

            def panel(n):
                stage, i, name, kind, _where = PANELS[n]
                b = pb(n)
                c2, cT = slice(2 * i, 2 * i + 2), slice(256 * i, 256 * i + 256)
                ev = ("ev", n)
                if stage.startswith("wo"):
                    dve.wait_ge(*at(("pe", n)))
                    dve.tensor_tensor(h[:, :, cT], two(b), h[:, :, cT], ALU.add).then_inc(*mark("residual", ev))
                elif stage.startswith("up"):
                    l = int(stage[-1])
                    dve.wait_ge(*at(("pe", n)))
                    dve.wait_ge(*at(("rows", NORM_OF[stage])))
                    if i >= 2:
                        dve.wait_ge(*at(("a", n - 2)))
                    if i >= 2 or l:
                        dve.wait_ge(*at(("conv", l, i - 2) if i >= 2 else ("conv", l - 1, FT - 2 + i)))
                    dve.tensor_tensor(ub_[i % 2][:, :, :], two(b), row2(NORM_OF[stage]), ALU.mult).then_inc(*mark("scaled", ("scaled", n), ev))
                    if i >= 1:
                        dve.wait_ge(*at(("scaled", n - 1)))
                        taps(n - 1)
                    if i >= 3:
                        ffn_lo(l, i - 3)
                elif kind == "F" and stage != "mk":
                    dve.wait_ge(*at(("pe", n)))
                    dve.wait_ge(*at(("rows", NORM_OF[stage])))
                    if stage == "ga" and i == 0:
                        dve.wait_ge(*at(("tr", "rope", 5)))
                    if stage == "ma" and i == 0:
                        dve.wait_ge(*at(("yb", "c", 3)))
                    row = row2(NORM_OF[stage])
                    if stage == "qa":
                        dve.scalar_tensor_tensor(qaT[:, c2, :], two(b), SB_DIM ** -0.5, row, ALU.mult, ALU.mult).then_inc(*mark("scaled", ev))
                    elif stage == "ub":
                        dve.wait_ge(*at(("ev", n - 3)))
                        dve.tensor_tensor(ubs[:, c2, :], ubs[:, c2, :], row, ALU.mult).then_inc(*mark("scaled", ("gate_scaled", n)))
                        dve.wait_ge(*at(("gate_scaled", n)))
                        dve.tensor_tensor(ubs[:, c2, :], two(b), ubs[:, c2, :], ALU.mult).then_inc(*mark("scaled", ev))
                    else:
                        dst = {"qb": qf, "fb": bdec, "ka": kaT, "qc": qc, "gc": gc, "ga": ga, "gb2": ubs, "mc": msig[0], "mb": msig[1], "ma": msig[0]}[stage]
                        event = ev if stage in ("ka", "qc") else ("scaled", n)
                        dve.tensor_tensor(dst[:, c2, :], two(b), row, ALU.mult).then_inc(*mark("scaled", event))
                elif stage.startswith("gate"):
                    dve.wait_ge(*at(("a", n)))
                    dve.wait_ge(*at(("pe", last_of("pp" + stage[-1]))))
                    g = gate[i % 2]
                    for t in range(TT):
                        dve.tensor_tensor(g[:, t, :], g[:, t, :], bank[ppb(int(stage[-1]), t, i // 2)][:, (i % 2) * 256:(i % 2) * 256 + 256], ALU.mult).then_inc(*mark("ple", ("ple", n, t)))
                    dve.wait_ge(*at(("ple", n, 1)))
                    dve.tensor_tensor(h[:, :, cT], g[:, :, :], h[:, :, cT], ALU.add).then_inc(*mark("residual", ev))
                split(n + RING)
                if stage.startswith("down") and n == last_of(stage):
                    for t in range(TT):
                        dve.wait_ge(*at(("tok0", stage) if t == 0 else ("pe", n)))
                        for half in range(2):
                            a = h[:, t, half * 512:half * 512 + 512]
                            dve.tensor_tensor(a, bank[2 * t + half][:, :], a, ALU.add).then_inc(*mark("residual", ("h", stage, t)))

            def soften(tag, hd, j):
                dve.wait_ge(*at(("e", tag, hd)))
                c = slice(2 * j, 2 * j + 2)
                dve.reciprocal(s_sum[:, c], s_sum[:, c]).then_inc(*chained())
                dve.wait_ge(*chain())
                for t in range(TT):
                    v = le[:, j, t, 0:P if (t == 0 and tag == "a") else T]
                    dve.tensor_scalar(v, v, s_sum[:, 2 * j + t:2 * j + t + 1], None, ALU.mult).then_inc(*mark("softmax", ("n", tag, hd)))

            for step in SCHEDULE:
                kind, args = step[0], step[1:]
                if kind == "panel":
                    panel(args[0])
                elif kind == "split":
                    split(args[0])
                elif kind == "setup":
                    if not args[0]:
                        continue
                    dve.wait_ge(*at(("vec", 0)))
                    a = VEC["hg_lb_logits", 0]
                    dve.tensor_tensor(lb_tmp, vflat[:, a:a + 4], vflat[:, a:a + 4], ALU.subtract).then_inc(*chained(("lb0",)))
                    dve.wait_ge(*chain())
                    dve.wait_ge(*at(("lbe",)))
                    dve.reciprocal(lb, lb_tmp).then_inc(*chained())
                    dve.wait_ge(*chain())
                    dve.tensor_tensor(lb_tmp, lb, lb_tmp, ALU.mult).then_inc(*chained())
                    dve.wait_ge(*chain())
                    dve.tensor_tensor(lb, lb_tmp, lb_tmp, ALU.subtract).then_inc(*chained())
                    dve.wait_ge(*chain())
                    dve.tensor_scalar(oml, lb, -1.0, 1.0, ALU.mult, ALU.add).then_inc(*chained())
                    dve.wait_ge(*chain())
                    dve.tensor_scalar(q_gain, vec("q_norm", 0)(0), SW_DIM ** -0.5, None, ALU.mult).then_inc(*chained(("q_gain",)))
                    dve.wait_ge(*chain())
                elif kind == "stats":
                    k = args[0]
                    dve.wait_ge(*at(("sq", k, 7 if k == "mem" else 3)))
                    dve.tensor_reduce(rstd[k], ssq[k].rearrange("p (t j) -> p t j", t=TT), AX.X, ALU.add).then_inc(*chained())
                    dve.wait_ge(*chain())
                    dve.tensor_scalar(rstd[k], rstd[k], 1.0 / D, EPS, ALU.mult, ALU.add).then_inc(*mark("mean_square", ("ms", k)))
                    if k == "mem":
                        dve.wait_ge(*at(("rstd", k)))
                        dve.tensor_scalar(mem[:, 0, :], mem[:, 0, :], rstd[k][:, 0:1], None, ALU.mult).then_inc(*mark("normalized0", ("xn", k, 0)))
                    elif k == "final":
                        dve.wait_ge(*at(("rstd", k)))
                        dve.wait_ge(*at(("hgn", 3)))
                        dve.tensor_scalar(result[:, 0, :], result[:, 0, :], rstd[k][:, 0:1], None, ALU.mult).then_inc(*mark("result0", ("result", 0)))
                elif kind == "square" and args[0] == "final":
                    c = slice(256 * args[1], 256 * args[1] + 256)
                    dve.wait_ge(*at(("loaded", "gfin")))
                    dve.wait_ge(*at(("ev", FIRST["wo2"] + args[1])))
                    gain = gfin[:, c].rearrange("p (a c) -> p a c", a=1).to_broadcast([P, TT, 256])
                    dve.tensor_tensor(result[:, :, c], h[:, :, c], gain, ALU.mult).then_inc(*mark("final_gain", ("hgn", args[1])))
                elif kind in ("turn", "turn_last"):
                    k, j = args if kind == "turn" else (args[0], 3)
                    hi, lo = DEST[k]
                    for q in range(2):
                        kt = 2 * j + q
                        rest(two(turn_bank(k, j))[:, q, :], GAIN[k](kt), hi[:, kt, :], lo[:, kt, :], "input_lo", ("xl", k, j), ("xh", k, j))
                elif kind == "hg_decay":
                    dve.wait_ge(*at(("ev", last_of("fb"))))
                    for hd in range(HG_HEADS):
                        dve.tensor_scalar(bdec[:, hd, :], bdec[:, hd, :], oml[:, hd:hd + 1], lb[:, hd:hd + 1], ALU.mult, ALU.add).then_inc(*mark("decay", ("f0",)))
                        dve.tensor_scalar(kk[:, hd, :], kk[:, hd, :], oml[:, hd:hd + 1], None, ALU.mult).then_inc(*mark("decay", ("kk",)))
                    dve.wait_ge(*at(("f0",)))
                    dve.tensor_scalar(bdec[:, :, :], bdec[:, :, :], 2.0 ** -64, None, ALU.max).then_inc(*mark("decay", ("f",)))
                    dve.wait_ge(*at(("logf",)))
                    dve.wait_ge(*at(("loaded", "reset")))
                    flat = lambda x: x[:, :, :].rearrange("p a b -> p (a b)")
                    dve.tensor_tensor_scan(flat(bdec), reset[:, :], flat(ex), 0.0, ALU.mult, ALU.add).then_inc(*mark("decay", ("b",)))
                    dve.wait_ge(*at(("b",)))
                    dve.wait_ge(*at(("kk",)))
                elif kind == "hg_level":
                    hg_level(args[0])
                elif kind == "hg_mask":
                    hg_mask(args[0])
                elif kind == "sb_log":
                    for i in range(4):
                        c = slice(2 * i, 2 * i + 2)
                        dve.wait_ge(*at(("sbl", i)))
                        fl = lambda x: x[:, c, :].rearrange("p a b -> p (a b)")
                        dve.scalar_tensor_tensor(fl(sp_), fl(zs), 0.0, fl(sp_), ALU.max, ALU.add).then_inc(*mark("softplus", ("splus", i)))
                elif kind == "hg_out":
                    for t in range(TT):
                        dve.wait_ge(*at(("hgsq", t)))
                        dve.tensor_reduce(hg_ss[:, 4 * t:4 * t + 4], prod4[:, t, :].rearrange("p (h v) -> p h v", h=4), AX.X, ALU.add).then_inc(*chained())
                        dve.wait_ge(*chain())
                    dve.tensor_scalar(hg_ss, hg_ss, 1.0 / P, EPS, ALU.mult, ALU.add).then_inc(*chained())
                    dve.wait_ge(*chain())
                    inverse_root(hg_ss, hg_rs, hg_tmp)
                    for t in range(TT):
                        r4 = hg_rs[:, 4 * t:4 * t + 4].rearrange("p (h a) -> p h a", a=1).to_broadcast([P, 4, P])
                        dve.tensor_tensor(on[:, t, :, :], bank[t][:, :].rearrange("p (h v) -> p h v", h=4), r4, ALU.mult).then_inc(*chained(("on", t)))
                        dve.wait_ge(*chain())
                        o = on[:, t, :, :].rearrange("p h v -> p (h v)")
                        dve.tensor_tensor(o, o, gbs[:, t, :], ALU.mult).then_inc(*mark("hg_gated", ("gated", t)))
                elif kind == "hg_turn":
                    for j in range(2):
                        dve.wait_ge(*at(("xh", "hg", j)))
                        fl = lambda x: x.rearrange("p a b -> p (a b)")
                        dve.scalar_tensor_tensor(fl(XL[:, 4 + 2 * j:6 + 2 * j, :]), bank[2 + j][:, :], vec("hg_out_norm", 0)(0), plain(fl(XH[:, 4 + 2 * j:6 + 2 * j, :])), ALU.mult, ALU.subtract).then_inc(*mark("input_lo", ("xl", "hg", j)))
                elif kind == "sb_weights":
                    i = args[0]
                    for r in range(2):
                        hd = 2 * i + r
                        dve.wait_ge(*at(("sbr", hd)))
                        dve.tensor_tensor(zs[:, hd, :], zs[:, hd, :], bank[4 + hd % 4][:, 0:384], ALU.subtract).then_inc(*mark("sb_exponents", ("d", hd)))
                elif kind == "sb_out":
                    i = args[0]
                    rest(bank[4 + i][:, 0:T], None, XH[:, i, :], XL[:, i, :], "input_lo", ("xl", "sb", i), ("xh", "sb", i))
                elif kind == "up_tail":
                    l = args[0]
                    taps(last_of(f"up{l}"))
                    ffn_lo(l, FT - 3)
                    ffn_lo(l, FT - 2)
                    ffn_lo(l, FT - 1)
                elif kind == "ple_input":
                    l = args[0]
                    rest(two(4), None, PTH[:, :, :], PTL[:, :, :], "input_lo", ("ptl", l), ("pth", l))
                elif kind == "bias":
                    dve.wait_ge(*at(("brp",)))
                    dve.wait_ge(*at(("brow0",)))
                    dve.tensor_copy(brow[:, P:2 * P], bank[0][0:16, 0:P]).then_inc(*mark("bias_row", ("brow",)))
                elif kind == "sw_norm":
                    for t in range(TT):
                        dve.wait_ge(*at(("swsq", t)))
                        dve.tensor_reduce(sw_ss[:, 20 * t:20 * t + 20], sq[:, t, :].rearrange("p (h d) -> p h d", d=SW_DIM), AX.X, ALU.add).then_inc(*chained())
                        dve.wait_ge(*chain())
                    dve.tensor_scalar(sw_ss, sw_ss, 1.0 / SW_DIM, EPS, ALU.mult, ALU.add).then_inc(*chained())
                    dve.wait_ge(*chain())
                    inverse_root(sw_ss, sw_rs, sw_tmp)
                    for t in range(TT):
                        r = sw_rs[:, 20 * t:20 * t + 20]
                        src = qk[:, t, :].rearrange("p (h d) -> p h d", d=SW_DIM)
                        dve.tensor_tensor(qkn[:, t, 0:16, :], src[:, 0:16, :], r[:, 0:16].rearrange("p (h a) -> p h a", a=1).to_broadcast([P, 16, SW_DIM]), ALU.mult).then_inc(*mark("sw_normed", ("qkn0",)))
                        for two_ in range(2):
                            dst = qkn[:, t, 16:24, :].rearrange("p (g a) d -> p g a d", a=2)[:, :, two_, :]
                            dve.tensor_tensor(dst, src[:, 16:20, :], r[:, 16:20].rearrange("p (h a) -> p h a", a=1).to_broadcast([P, 4, SW_DIM]), ALU.mult).then_inc(*mark("sw_normed", ("qkn", t)))
                elif kind == "sw_logits":
                    g = args[0]
                    dve.wait_ge(*at(("loaded", "bias")))
                    dve.wait_ge(*at(("loaded", "sinks")))
                    for j in range(4):
                        hd = 4 * g + j
                        dve.wait_ge(*at(("swz", g, j)))
                        if g:
                            dve.wait_ge(*at(("tr", "sww", g - 1, j)))
                            dve.wait_ge(*at(("swn", g - 1, 3)))
                        for t in range(TT):
                            w = P if t == 0 else T
                            dve.tensor_tensor_reduce(le_s[:, j, t, 0:w], bank[j][:, t * T:t * T + w], bias[:, hd, T - w:T], 1.0, -3.0e38, ALU.add, ALU.max, s_max[:, 2 * j + t:2 * j + t + 1]).then_inc(*mark("logits", ("swm", g, j)))
                    dve.wait_ge(*at(("swm", g, 3)))
                    sk = sinks[:, 4 * g:4 * g + 4].rearrange("p (h a) -> p h a", a=1).to_broadcast([P, 4, 2])
                    v = lambda x: x.rearrange("p (h a) -> p h a", a=2)
                    dve.tensor_tensor(v(s_max), v(s_max), sk, ALU.max).then_inc(*chained())
                    dve.wait_ge(*chain())
                    dve.tensor_scalar(s_neg, s_max, -1.0, None, ALU.mult).then_inc(*chained())
                    dve.wait_ge(*chain())
                    dve.tensor_tensor(v(s_exp), v(s_neg), sk, ALU.add).then_inc(*chained(("swneg", g)))
                    dve.wait_ge(*chain())
                    dve.wait_ge(*at(("swx", g)))
                    dve.tensor_tensor(s_sum, s_sum, s_exp, ALU.add).then_inc(*chained())
                    dve.wait_ge(*chain())
                    dve.reciprocal(s_sum, s_sum).then_inc(*chained())
                    dve.wait_ge(*chain())
                    for j in range(4):
                        for t in range(TT):
                            a = le_s[:, j, t, 0:P if t == 0 else T]
                            dve.tensor_scalar(a, a, s_sum[:, 2 * j + t:2 * j + t + 1], None, ALU.mult).then_inc(*mark("softmax", ("swn", g, j)))
                elif kind == "sw_weights":
                    g = args[0]
                    for j in (1, 3):
                        dve.wait_ge(*at(("tr", "sww", g, j)))
                        if g:
                            dve.wait_ge(*at(("swo", 2 * g - 1)))
                        dve.tensor_copy(wT_s[:, j, :], bank[4 + j][:, 0:384]).then_inc(*mark("turned_copied2", ("swt", g, j)))
                elif kind == "sw_out":
                    g = args[0]
                    for q in range(2):
                        i = 2 * g + q
                        rest(bank[q][:, 0:T], None, XH[:, i, :], XL[:, i, :], "input_lo", ("xl", "sw", i), ("xh", "sw", i))
                elif kind == "x_logits":
                    g = args[0]
                    for j in range(2):
                        hd = 2 * g + j
                        dve.wait_ge(*at(("xz", hd)))
                        if g:
                            dve.wait_ge(*at(("n", "x", 2 * g - 1)))
                            dve.wait_ge(*at(("trw", "x", hd - 2)))
                        c = slice(2 * j, 2 * j + 2)
                        dve.tensor_reduce(s_max[:, c], two(j), AX.X, ALU.max).then_inc(*chained())
                        dve.wait_ge(*chain())
                        dve.tensor_scalar(s_neg[:, c], s_max[:, c], -HEAD ** -0.5, None, ALU.mult).then_inc(*chained(("neg", "x", hd)))
                        dve.wait_ge(*chain())
                    for j in range(2):
                        soften("x", 2 * g + j, j)
                elif kind == "a_logits":
                    g = args[0]
                    dve.wait_ge(*at(("loaded", "causal")))
                    for j in range(2):
                        hd = 2 * g + j
                        dve.wait_ge(*at(("az", hd)))
                        dve.wait_ge(*at(("trw", "a", hd - 2) if g else ("trw", "x", 2 + j)))
                        for t in range(TT):
                            w = P if t == 0 else T
                            dve.tensor_tensor_reduce(le[:, j, t, 0:w], bank[j][:, t * T:t * T + w], causal[:, T - w:T], 1.0, -3.0e38, ALU.add, ALU.max, s_max[:, 2 * j + t:2 * j + t + 1]).then_inc(*mark("logits", ("am", hd)))
                        dve.wait_ge(*at(("am", hd)))
                        dve.tensor_scalar(s_neg[:, 2 * j:2 * j + 2], s_max[:, 2 * j:2 * j + 2], -HEAD ** -0.5, None, ALU.mult).then_inc(*chained(("neg", "a", hd)))
                        dve.wait_ge(*chain())
                    for j in range(2):
                        soften("a", 2 * g + j, j)
                elif kind in ("x_weights", "a_weights"):
                    tag, g = kind[0], args[0]
                    hd = 2 * g + 1
                    dve.wait_ge(*at(("trw", tag, hd)))
                    if tag == "x" and g:
                        dve.wait_ge(*at(("oz", "c", hd - 2)))
                    elif tag == "a":
                        dve.wait_ge(*at(("oz", "a", hd - 2) if g else ("oz", "c", X_HEADS - 1)))
                    n = 2 * T if tag == "x" else 384
                    dve.tensor_copy(wT[:, 1, :, :].rearrange("p a b -> p (a b)")[:, 0:n], bank[3][:, 0:n]).then_inc(*mark("turned_copied2", ("wT", tag, hd)))
                elif kind in ("x_out", "a_out"):
                    b, g = ("c" if kind[0] == "x" else "a"), args[0]
                    src = gc if b == "c" else ga
                    dve.wait_ge(*at(("ev", last_of("gc" if b == "c" else "ga"))))
                    for j in range(2):
                        hd = 2 * g + j
                        dve.wait_ge(*at(("oz", b, hd)))
                        dve.tensor_tensor(src[:, hd, :], bank[j][:, 0:T], src[:, hd, :], ALU.mult).then_inc(*mark("gated", ("og", b, hd)))
                    for j in range(2):
                        hd = 2 * g + j
                        rest(src[:, hd, :], None, GH[:, OUT_AT[b] + hd, :], GL[:, OUT_AT[b] + hd, :], "gated_lo", ("ol", b, hd), ("oh", b, hd))
                elif kind == "rope":
                    dve.wait_ge(*at(("ev", last_of("qka"))))
                    dve.wait_ge(*at(("loaded", "rope")))
                    dve.wait_ge(*at(("pe", last_of("mv"))))
                    for t in range(TT):
                        q = qkm[:, t, :].rearrange("p (e d) -> p e d", d=HEAD)
                        x1, x2 = q[:, :, 0:16], q[:, :, 16:32]
                        cos, sin = (rope[:, t, c, :].rearrange("p (a f) -> p a f", a=1).to_broadcast([P, 12, 16]) for c in range(2))
                        if t:
                            dve.wait_ge(*at(("roped0",)))
                        for f, (a, m) in enumerate(((x1, cos), (x2, sin), (x2, cos), (x1, sin))):
                            dve.tensor_tensor(rtmp[:, f, :, :], a, m, ALU.mult).then_inc(*mark("rope", ("rope_m", t)))
                        dve.wait_ge(*at(("rope_m", t)))
                        dve.tensor_tensor(x1, rtmp[:, 0, :, :], rtmp[:, 1, :, :], ALU.subtract).then_inc(*mark("rope", ("rope_s", t)))
                        dve.tensor_tensor(x2, rtmp[:, 2, :, :], rtmp[:, 3, :, :], ALU.add).then_inc(*mark("rope", ("roped",) if t else ("roped0",)))
                elif kind == "rope_turn":
                    for j in (1, 3, 5):
                        dve.wait_ge(*at(("tr", "rope", j)))
                        dst = qF if j < 3 else kF
                        dve.tensor_copy(dst[:, (2 * j) % 6:(2 * j) % 6 + 2, :], two(3)).then_inc(*mark("turned_copied2", ("qkF", j)))
                elif kind == "layer_norm":
                    dve.wait_ge(*at(("ev", last_of("vb"))))
                    for t in range(TT):
                        dve.tensor_reduce(ln_sum[:, t:t + 1], vb[:, t, :], AX.X, ALU.add).then_inc(*chained())
                        dve.wait_ge(*chain())
                    dve.tensor_scalar(ln_neg, ln_sum, -1.0 / 768, None, ALU.mult).then_inc(*chained(("lnm",)))
                    dve.wait_ge(*chain())
                    dve.wait_ge(*at(("lnsq", 1)))
                    dve.tensor_scalar(ln_ss, ln_ss, 1.0 / 768, EPS, ALU.mult, ALU.add).then_inc(*chained())
                    dve.wait_ge(*chain())
                    inverse_root(ln_ss, ln_rs, ln_sum)
                    for t in range(TT):
                        dve.tensor_scalar(vb[:, t, :], vb[:, t, :], ln_neg[:, t:t + 1], ln_rs[:, t:t + 1], ALU.add, ALU.mult).then_inc(*mark("layer_normed", ("vn", t)))
                elif kind == "mixed":
                    dve.wait_ge(*at(("ev", last_of("ub"))))
                    dve.wait_ge(*at(("loaded", "bsp")))
                    for g in range(GROUPS):
                        dve.wait_ge(*at(("mixp", g // 2)))
                        tb = lambda x: x.rearrange("p (t c) -> p t c", t=TT)
                        bb = bsp[:, g, :].rearrange("p (a c) -> p a c", a=1).to_broadcast([P, TT, P])
                        dve.scalar_tensor_tensor(tb(mixt[:, g, :]), tb(two(g // 2)[:, g % 2, :]), vec("gmlp_ln_g_2", 0)(g), bb, ALU.mult, ALU.add).then_inc(*mark("mixed", ("mixg", g)))
                    for g in range(GROUPS):
                        dve.wait_ge(*at(("mixg", g)))
                        dve.tensor_tensor(ubs[:, g, :], mixt[:, g, :], ubs[:, g, :], ALU.mult).then_inc(*mark("gated", ("og", "b", g)))
                    for g in range(GROUPS):
                        rest(ubs[:, g, :], None, GH[:, OUT_AT["b"] + g, :], GL[:, OUT_AT["b"] + g, :], "gated_lo", ("ol", "b", g), ("oh", "b", g))
                elif kind == "branch_end":
                    b = args[0]
                    m = msig[b == "b"]
                    dve.wait_ge(*at(("pe", last_of("br" + b))))
                    dve.wait_ge(*at(("ev", last_of("m" + b))))
                    dve.wait_ge(*at(("og", "b", GROUPS - 1)))
                    for j in range(4):
                        c = slice(2 * j, 2 * j + 2)
                        if b == "c":
                            dve.tensor_tensor(y[:, c, :], two(j), m[:, c, :], ALU.mult).then_inc(*mark("branch_sum", ("yb", b, j)))
                        else:
                            dve.tensor_tensor(m[:, c, :], two(j), m[:, c, :], ALU.mult).then_inc(*chained())
                            dve.wait_ge(*chain())
                            dve.tensor_tensor(y[:, c, :], y[:, c, :], m[:, c, :], ALU.add).then_inc(*mark("branch_sum", ("yb", b, j)))
                elif kind == "y_split":
                    for j in range(4):
                        c = slice(2 * j, 2 * j + 2)
                        rest(y[:, c, :], None, XH[:, c, :], XL[:, c, :], "input_lo", ("xl", "y", j), ("xh", "y", j))

    return events


_INS = ["x", "p", "mix_norm", "ab_w_in", "hg_lb_logits", "hg_out_norm", "ab_w_out", "c_w_in", "q_norm", "k_norm", "sinks", "rel_bias",
        "c_w_out", "ffn_norm", "ffn_up", "ffn_conv", "ffn_conv_b", "ffn_down", "ple_norm", "ple_gate", "ple_proj", "mem_2", "norm_g_2",
        "mem_norm_g_2", "final_norm_g_2", "w_in_2", "w_mem_kv_2", "gmlp_ln_g_2", "w_spatial_2", "b_spatial_2", "w_branch_a_2",
        "w_branch_b_2", "w_branch_c_2", "w_out_2"]


def kernel(**inputs):
    import concourse.bacc as bacc
    from concourse.bass_utils import run_bass_kernel_spmd

    arrays = {f"in_{n}": np.ascontiguousarray(inputs[n]) for n in _INS}
    arrays.update(shape_constants())

    def build(known):
        nc = bacc.Bacc("TRN2", target_bir_lowering=False, num_devices=1)
        io = {}
        for name, a in arrays.items():
            io[name.removeprefix("in_")] = nc.dram_tensor(name, a.shape, mybir.dt.from_np(a.dtype), kind="ExternalInput").ap()
        out = nc.dram_tensor("out_dram", (1, T, D), F32, kind="ExternalOutput").ap()
        return nc, block_program(nc, io, out, known)

    said = build({})[1].said
    nc = build(said)[0]
    r = run_bass_kernel_spmd(nc, [arrays], core_ids=[0])
    return r.results[0]["out_dram"]
```

```python
from contextlib import ExitStack

import numpy as np

import concourse.bass as bass
from concourse import mybir

ALU = mybir.AluOpType
ACT = mybir.ActivationFunctionType
AX = mybir.AxisListType
F32 = mybir.dt.float32
F32R = mybir.dt.float32r
I32 = mybir.dt.int32

P = 128
T = 256
TT = T // P
D = 1024
KT = D // P
EPS = 1e-6
NEG = -1e30
SB_HEADS, SB_DIM = 8, 64
HG_HEADS, HG_CHUNK = 4, 64
SW_HEADS, SW_KV, SW_DIM, WINDOW = 16, 4, 64, 128
BUCKETS, MAX_DISTANCE = 32, 128
D_FF = 2816
FT = D_FF // P
MOBA_HEADS, X_HEADS, GROUPS, HEAD = 6, 4, 6, 128
ROT = HEAD // 4
LEVELS = [64, 32, 16, 8, 4, 2, 1, 0]
RAW, RING = 3, 3
MAGIC = float(0x5F3759DF)



def shape_constants():
    i = np.arange(P)
    s, t = i[:, None], i[None, :]
    levels = []
    for half in LEVELS:
        if half:
            levels.append((s // (2 * half) == t // (2 * half)) & (s % (2 * half) < half) & (t % (2 * half) >= half))
        else:
            levels.append(s == t)
    dist = 127 - i
    exact = BUCKETS // 2
    large = exact + (np.log(np.maximum(dist, exact) / exact) / np.log(MAX_DISTANCE / exact) * (BUCKETS - exact)).astype(np.int32)
    bucket = np.where(dist < exact, dist, np.minimum(large, BUCKETS - 1))
    inv_freq = np.float32(500000.0) ** (-np.arange(0, ROT, 2, dtype=np.float32) / np.float32(ROT))
    ang = (np.arange(T, dtype=np.float32)[:, None] * inv_freq[None, :]).astype(np.float32)
    return {
        "c_ident": np.eye(P, dtype=np.float32),
        "c_tri": (s >= t).astype(np.float32),
        "c_levels": np.stack(levels, 1).astype(np.float32).reshape(P, -1),
        "c_reset": np.tile((np.arange(HG_HEADS * T) % HG_CHUNK != 0).astype(np.float32), (P, 1)),
        "c_causal": np.where(np.arange(T)[None, :] - P <= s, 0.0, NEG).astype(np.float32),
        "c_bucket": (bucket[None, :] == np.arange(BUCKETS)[:, None]).astype(np.float32),
        "c_rope": np.stack([np.cos(ang), np.sin(ang)], 1).reshape(TT, P, 2, ROT // 2).transpose(1, 0, 2, 3).reshape(P, -1).astype(np.float32).copy(),
    }


VEC = {}
VEC_LOADS = []


def _vectors():
    at = 0
    for name, layer, n in [("mix_norm", 0, 8), ("mix_norm", 1, 8), ("ffn_norm", 0, 8), ("ffn_norm", 1, 8),
                           ("ple_norm", 0, 8), ("ple_norm", 1, 8), ("norm_g_2", 0, 8), ("mem_norm_g_2", 0, 8),
                           ("hg_out_norm", 0, 1), ("hg_lb_logits", 0, 4), ("gmlp_ln_g_2", 0, 6)]:
        VEC[name, layer] = at
        if layer == 0:
            VEC_LOADS.append((name, (0,), at, n) if n < 8 or name.endswith("_2") else (name, (), at, 2 * n))
        at += n
    for name in ("q_norm", "k_norm"):
        VEC[name, 0] = at
        VEC_LOADS.append((name, (0,), at, 1))
        at += 1
    at = P
    for layer in range(2):
        VEC["ffn_conv_b", layer] = at + 2 * FT * layer
        VEC_LOADS.append(("ffn_conv_b", (layer,), at + 2 * FT * layer, 2 * FT))
    for n, (layer, tap) in enumerate([(a, b) for a in range(2) for b in range(3)]):
        at = P * (2 + n // 2) + 2 * FT * (n % 2)
        VEC["ffn_conv", layer, tap] = at
        VEC_LOADS.append(("ffn_conv", (layer, tap), at, 2 * FT))


_vectors()
VEC_ROWS = [77, 4 * FT, 4 * FT, 4 * FT, 4 * FT]


class Events:

    def __init__(self, known, make):
        self.known, self.make = known, make
        self.sems, self.count, self.said, self.links = {}, {}, {}, 0

    def sem(self, name):
        if name not in self.sems:
            self.sems[name] = self.make(name)
        return self.sems[name]

    def mark(self, name, *events, by=1):
        self.count[name] = self.count.get(name, 0) + by
        for e in events:
            self.said[e] = (name, self.count[name])
        return self.sem(name), by

    def at(self, event):
        name, value = self.known[event] if self.known else ("first_pass", 1)
        return self.sem(name), value

    def chained(self, *events):
        self.links += 1
        return self.mark("vector_chain", ("link", self.links), *events)

    def chain(self):
        return self.at(("link", self.links))


def panels_of():
    out = []

    def cols(stage, name, at, n, kind, idx=()):
        for i in range(n):
            out.append((stage, i, name, kind, (idx, at + 256 * i)))

    def rows(stage, name, n, kind, idx=()):
        for i in range(n):
            out.append((stage, i, name, kind, (idx, 256 * i)))

    for stage, at, kind in (("fb", 2048, "F"), ("qb", 1536, "F"), ("qa", 0, "F"), ("ka", 512, "F"), ("ib", 2560, "T"),
                            ("va", 1024, "T"), ("gb", 3072, "T")):
        cols(stage, "ab_w_in", at, 2, kind, (0,))
    cols("wo0", "ab_w_out", 0, 4, "T", (0,))
    for layer in range(2):
        for i in range(FT):
            out.append((f"up{layer}", i, "ffn_up", "F", ((layer,), i * P)))
        rows(f"down{layer}", "ffn_down", FT // 2, "BT", (layer,))
        rows(f"pp{layer}", "ple_proj", 1, "BT", (layer,))
        cols(f"gate{layer}", "ple_gate", 0, 4, "T", (layer,))
        if layer == 0:
            cols("ks", "c_w_in", 1024, 1, "T", (0,))
            cols("vs", "c_w_in", 1280, 1, "T", (0,))
            cols("qs", "c_w_in", 0, 4, "T", (0,))
            cols("wo1", "c_w_out", 0, 4, "T", (0,))
    cols("mk", "w_mem_kv_2", 0, 2, "F", (0,))
    cols("mv", "w_mem_kv_2", 512, 2, "T", (0,))
    for stage, at, n, kind in (("qc", 5376, 2, "F"), ("gc", 5888, 2, "F"), ("qka", 0, 6, "T"), ("va2", 1536, 3, "T"),
                               ("ga", 2304, 3, "F"), ("vb", 3840, 3, "T"), ("gb2", 4608, 3, "F"), ("ub", 3072, 3, "F")):
        cols(stage, "w_in_2", at, n, kind, (0,))
    for b, at, n in (("c", 8448, 2), ("b", 7424, 3), ("a", 6400, 3)):
        cols("m" + b, "w_in_2", at, 4, "F", (0,))
        rows("br" + b, f"w_branch_{b}_2", n, "BF", (0,))
    cols("wo2", "w_out_2", 0, 4, "T", (0,))
    return out


PANELS = panels_of()
FIRST = {}
for _n, _p in enumerate(PANELS):
    FIRST.setdefault(_p[0], _n)


def last_of(stage):
    return max(n for n, p in enumerate(PANELS) if p[0] == stage)


TURNED_LATER = ("blk2", "final")
HEAD_TILES = {FIRST["wo0"]: 4, FIRST["wo0"] + 1: 4, FIRST["wo1"]: 4, FIRST["wo1"] + 1: 6}
PRODUCERS = ("wo0", "gate0", "wo1", "gate1", "wo2")


def splits_later(n):
    stage, i = PANELS[n][:2]
    return (stage in PRODUCERS and i >= 2) or stage.startswith("pp") or n in (last_of("gb"), last_of("bra") - 1, last_of("bra"))


def schedule():
    out = []

    def gemm(*stages):
        for s in stages:
            out.extend(("panel", n) for n, p in enumerate(PANELS) if p[0] == s)

    def producer(stage, k, between={}):
        first = FIRST[stage]
        for j in range(4):
            out.extend(between.get(j, []))
            out.append(("panel", first + j))
            if k and j < 3:
                out.append(("square", k, j))
            if k in TURNED_LATER:
                continue
            if k and j:
                out.append(("turn", k, j - 1))
        if k and k not in TURNED_LATER:
            out.append(("turn_last", k))
        out.extend(between.get(4, []))
        out.extend([("square", k, 3), ("stats", k)])
        out.extend([("split", first + 2 + RING), ("split", first + 3 + RING)])

    out.extend([("split", 0), ("setup", 0)])
    out.extend(("turn", "mix0", j) for j in range(4))
    out.append(("split", 1))
    out.extend(("square", "mix0", j) for j in range(4))
    out.extend([("stats", "mix0"), ("split", 2)])
    gemm("fb")
    out.extend([("setup", 1), ("hg_decay",)])
    gemm("qb")
    first = FIRST["qa"]
    out.extend([("hg_level", -1), ("panel", first), ("panel", first + 1), ("hg_level", 0), ("panel", first + 2)])
    for n, li in enumerate(range(-1, 6)):
        out.append(("hg_scores", li))
        if 2 <= n < 6:
            out.append(("sb_scores", n - 2))
        out.append(("hg_mask", li))
        if LEVELS[li + 2]:
            out.append(("hg_level", li + 2))
        else:
            out.append(("sb_log",))
        out.append(("panel", first + 3 + n))
    out.extend([("hg_scores", 6), ("hg_scores", 7), ("hg_mask", 6), ("hg_mask", 7), ("sb_weights", 0), ("sb_weights", 1)])
    out.extend([("sb_weights", 2), ("hg_out",), ("sb_weights", 3)])
    for i in range(SB_HEADS // 2):
        out.append(("sb_out", i))
    out.extend([("hg_norm",), ("split", last_of("gb") + RING)])
    out.extend([("panel_head", FIRST["wo0"]), ("panel_head", FIRST["wo0"] + 1), ("hg_turn",)])
    producer("wo0", "ffn0")
    for layer in range(2):
        out.append(("ffn_loads", layer))
        gemm(f"up{layer}")
        out.extend([("up_tail", layer), ("ple_input", layer)])
        if layer == 0:
            out.append(("bias",))
        gemm(f"down{layer}")
        gemm(f"pp{layer}")
        k = f"ple{layer}"
        out.extend([("turn", k, 0), ("turn", k, 1), ("turn", k, 2), ("turn_last", k)])
        out.extend(("square", k, j) for j in range(4))
        out.extend([("stats", k), ("split", last_of(f"pp{layer}") + RING)])
        if layer == 0:
            producer("gate0", "mix1")
            q = FIRST["qs"]
            gemm("ks", "vs")
            out.extend([("panel", q), ("panel", q + 1), ("sw_norm", 0), ("panel", q + 2), ("panel", q + 3), ("sw_turn", 0)])
            out.extend([("sw_logits", 0), ("sw_norm", 1), ("sw_exp", 0), ("sw_logits", 1), ("sw_turn", 1)])
            for g in range(SW_KV):
                out.append(("sw_weights", g))
                if g + 1 < SW_KV:
                    out.append(("sw_exp", g + 1))
                if g >= 2:
                    out.append(("panel_head", FIRST["wo1"] + g - 2))
                out.append(("sw_copy", g))
                if g + 2 < SW_KV:
                    out.append(("sw_logits", g + 2))
                out.append(("sw_out", g))
            producer("wo1", "ffn1")
    producer("gate1", "blk2", {1: [("stats", "mem")], 3: [("turn", "mem", 0), ("turn", "mem", 1)],
                               4: [("turn", "mem", 2), ("turn_last", "mem")]})
    for n, turned in enumerate(((0, 1), (2,), (3,), ())):
        out.append(("panel", FIRST["mk"] + n))
        out.extend(("turn", "blk2", j) for j in turned)

    def between(steps, *stages):
        panels = [n for s in stages for n, p in enumerate(PANELS) if p[0] == s]
        for n, before in zip(panels, steps + [[]] * len(panels)):
            out.extend(before)
            out.append(("panel", n))

    between([[], [], [], [("x_logits", 0)]], "qc", "gc")
    between([[("x_weights", 0)], [("x_out", 0), ("x_logits", 1)], [("x_weights", 1)], [("x_out", 1)]], "qka")
    between([[("rope",), ("spatial",)], [], [("rope_turn", 0)]], "va2")
    between([[("rope_turn", 1)], [("a_logits", 0)], [("a_weights", 0)]], "ga")
    between([[("a_out", 0), ("a_logits", 1)], [("a_weights", 1)], [("a_out", 1), ("a_logits", 2)]], "vb")
    between([[("a_weights", 2)], [("a_out", 2), ("layer_norm",)]], "gb2")
    gemm("ub")
    out.append(("mixed",))
    for b in "cba":
        gemm("m" + b, "br" + b)
        out.append(("branch_end", b))
    out.extend([("y_split",), ("split", last_of("bra") - 1 + RING), ("split", last_of("bra") + RING)])
    producer("wo2", "final")
    return out


LATE_TURN = {FIRST["up0"]: "ffn0", FIRST["gate0"]: "ple0", FIRST["ks"]: "mix1", FIRST["up1"]: "ffn1",
             FIRST["gate1"]: "ple1", FIRST["mk"]: "mem"}
ROWS_AFTER = {FIRST["fb"]: "mix0", FIRST["up0"]: "ffn0", FIRST["up1"]: "ffn1", FIRST["mv"]: "blk2"}
SCHEDULE = schedule()


def block_program(nc, io, out_ap, known):
    with ExitStack() as ctx:
        events = Events(known, lambda name: ctx.enter_context(nc.semaphore(name)))
        mark, at, chained, chain = events.mark, events.at, events.chained, events.chain
        top = [16512]

        def fixed(name, shape, dt=F32):
            n = 4 * int(np.prod(shape[1:]))
            n = (n + 31) // 32 * 32
            t = nc.alloc_sbuf_tensor_at(name, shape, dt, offset=top[0])
            top[0] += n
            return t

        raw = [fixed(f"w_raw{i}", [P, 2048]) for i in range(RAW)]
        whi = [fixed(f"w_hi{i}", [P, 2048], F32R) for i in range(RING)]
        wlo = [fixed(f"w_lo{i}", [P, 2048], F32R) for i in range(RING)]
        XH, XL = (fixed(n, [P, KT, T], F32R) for n in ("x_hi", "x_lo"))
        h = fixed("h", [P, TT, D])
        xn_at = top[0]
        xn = fixed("xn", [P, TT, D])
        ident = fixed("ident", [P, P])
        tri = fixed("tri", [P, P])
        vecs = fixed("vecs", [P, 5, P])
        small = fixed("small", [P, 320])
        g_at = top[0]
        GH, GL = (fixed(n, [P, FT, T], F32R) for n in ("g_hi", "g_lo"))
        t_at = top[0]
        end = nc.sbuf_usable_end

        class Region:

            def __init__(self, at, end):
                self.at, self.end = at, end

            def __call__(self, name, shape, dt=F32):
                n = 4 * int(np.prod(shape[1:]))
                t = nc.alloc_sbuf_tensor_at(name, shape, dt, offset=self.at)
                self.at += n
                assert self.at <= self.end, (name, self.at - self.end)
                return t

        r, g = Region(t_at, end), Region(g_at, t_at)
        qaT, kaT = r("qaT", [P, 4, T]), r("kaT", [P, 4, T])
        va, ib, gbs = r("va", [P, TT, 512]), r("ib", [P, TT, 512]), r("gbs", [P, TT, 512])
        qf, kk, bdec = r("qf", [P, HG_HEADS, T]), r("kk", [P, HG_HEADS, T]), r("bdec", [P, HG_HEADS, T])
        ex, prod = r("ex", [P, HG_HEADS, T]), r("prod", [P, len(LEVELS), P])
        masks = r("masks", [P, len(LEVELS), P])
        zs, sp_ = g("zs", [P, SB_HEADS, 384]), g("sp_", [P, SB_HEADS, 384])
        reset, sc, on = g("reset", [P, HG_HEADS * T]), g("sc", [P, HG_HEADS, 384]), g("on", [P, TT, HG_HEADS, P])
        exb = g("exb", [P, HG_HEADS, T])
        xs_buf = [r(f"xs{i}", [P, HG_HEADS, T]) for i in range(2)]
        ones = g("ones", [P, P])
        prod4 = prod[:, :, :].rearrange("p (t a) c -> p t (a c)", t=TT)

        def blocks_of(buf, h0):
            return buf[:, h0:h0 + 2, :].rearrange("p h (a c) -> p h a c", a=3)[:, :, 0:3:2, :]

        def blocks_of_prod(j):
            return prod[:, 4 * j:4 * j + 4, :].rearrange("p (h t) c -> p h t c", h=2)

        r = Region(t_at, end)
        cc = [r(f"cc{i}", [P, 2, T]) for i in range(3)]
        sgate = [r(f"sgate{i}", [P, T]) for i in range(2)]
        gf = [r(f"gf{i}", [P, T]) for i in range(2)]
        praw = r("praw", [P, TT, 256])
        PTH, PTL = r("pt_hi", [P, 2, T], F32R), r("pt_lo", [P, 2, T], F32R)
        gate = [r(f"gate{i}", [P, TT, 256]) for i in range(2)]
        conv_in = [r(f"conv_in{i}", [P, 2, T]) for i in range(2)]
        vsw = r("vsw", [P, TT, 256])
        bias = r("bias", [P, SW_HEADS, T])
        brow = r("brow", [16, 3 * P])
        relb, buck = r("relb", [32, 16]), r("buck", [32, P])
        YL = r("y_lo", [P, KT, T], F32R)
        YH = nc.alloc_sbuf_tensor_at("y_hi", [P, KT, T], F32R, offset=xn_at)
        row_early = r("row_early", [P, T])
        junk = [cc[t][:, 0, :] for t in range(TT)]
        r, g = Region(t_at, t_at + 4 * 4096), Region(g_at, t_at)
        qsT, le_s = r("qsT", [P, 8, T]), r("le_s", [P, 4, 2, T])
        qk = g("qk", [P, TT, 1280])
        sq_at = g.at
        sq = g("sq", [P, TT, 1280])
        qkn = g("qkn", [P, TT, 24, SW_DIM])
        wT_s = g("wT_s", [P, 4, 384])
        le_s = [le_s, nc.alloc_sbuf_tensor_at("le_s1", [P, 4, 2, T], F32, offset=sq_at)]
        ksT = g("ksT", [P, SW_KV, T])
        qF = nc.alloc_sbuf_tensor_at("qF", [P, MOBA_HEADS, T], F32, offset=g_at + 4 * T * 16)
        kF = nc.alloc_sbuf_tensor_at("kF", [P, MOBA_HEADS, T], F32, offset=g_at + 4 * T * (FT + 16))
        mem = nc.alloc_sbuf_tensor_at("mem", [P, TT, D], F32, offset=g_at)
        mem_junk = nc.alloc_sbuf_tensor_at("mem_junk", [P, D], F32, offset=g_at + 4 * TT * D)
        r = Region(t_at, end)
        qkm = r("qkm", [P, TT, 1536])
        qc, gc = r("qc", [P, X_HEADS, T]), r("gc", [P, X_HEADS, T])
        mk, mv = r("mk", [P, X_HEADS, T]), r("mv", [P, TT, 512])
        le, wT = r("le", [P, 2, 2, T]), r("wT", [P, 2, 2, T])
        va2, vb = r("va2", [P, TT, 768]), r("vb", [P, TT, 768])
        wsp, bsp = r("wsp", [P, GROUPS, P]), r("bsp", [P, GROUPS, P])
        causal = r("causal", [P, T])
        r = Region(t_at, t_at + 4 * 3072)
        ubs, ga = r("ubs", [P, GROUPS, T]), r("ga", [P, MOBA_HEADS, T])
        r = Region(t_at + 4 * 3072, end)
        msig = [r(f"msig{i}", [P, KT, T]) for i in range(2)]
        gfin, result = r("gfin", [P, D]), r("result", [P, TT, D])
        xflat = xn[:, :, :].rearrange("p a b -> p (a b)")
        y = xflat.rearrange("p (k t) -> p k t", k=KT)
        rtmp = xflat[:, 0:768].rearrange("p (f e j) -> p f e j", f=4, e=12)
        wsp_raw = xflat[:, 1024:1792].rearrange("p (g s) -> p g s", g=GROUPS)
        mixt = xflat[:, 0:1536].rearrange("p (g t) -> p g t", g=GROUPS)

        bank = [ctx.enter_context(nc.psum_tensor(f"bank{i}", [P, 512], F32)) for i in range(8)]
        BW = 3 * P
        scratch = nc.dram_tensor("bias_rows", [SW_HEADS, P, BW], F32, kind="Internal").ap()

        small_at = [64]

        def col(n):
            small_at[0] += n
            assert small_at[0] <= 320
            return small[:, small_at[0] - n:small_at[0]]

        rope = small[:, 0:64].rearrange("p (t c f) -> p t c f", t=TT, c=2)
        NORMS = ["mix0", "ffn0", "ple0", "mix1", "ffn1", "mem", "ple1", "blk2", "final"]
        ssq = {k: col(4 * TT) for k in NORMS}
        rstd = {k: col(TT) for k in NORMS}
        minus_half = col(TT)
        lb, oml, lb_tmp = col(HG_HEADS), col(HG_HEADS), col(HG_HEADS)
        q_gain, sinks = col(1), col(SW_HEADS)
        s_max, s_neg, s_sum, s_exp = col(8), col(8), col(8), col(8)
        ln_sum, ln_neg, ln_ss, ln_rs = col(TT), col(TT), col(TT), col(TT)
        sw_ss, sw_rs = col(40), col(40)
        sw_cols = [(s_max, s_neg, s_sum, s_exp), tuple(ssq[k] for k in ("mix0", "ffn0", "ple0", "mix1"))]
        hg_ss, hg_rs, hg_tmp = sw_ss[:, 0:8], sw_ss[:, 8:16], sw_ss[:, 16:24]
        sw_tmp = [qkn[:, 0, 23, :], qkn[:, 0, 15, :]]

        vflat = vecs[:, :, :].rearrange("p a b -> p (a b)")

        def vec(name, layer, *more):
            return lambda i: vflat[:, VEC[(name, layer, *more)] + i:VEC[(name, layer, *more)] + i + 1]

        GAIN = {"mix0": vec("mix_norm", 0), "mix1": vec("mix_norm", 1), "ffn0": vec("ffn_norm", 0), "ffn1": vec("ffn_norm", 1),
                "ple0": vec("ple_norm", 0), "ple1": vec("ple_norm", 1), "blk2": vec("norm_g_2", 0), "mem": vec("mem_norm_g_2", 0)}

        ROWS = {k: row_early[:, :] for k in ("mix0", "ffn0", "ffn1")}
        ROWS["blk2"] = vflat[:, P:P + T]

        def row2(k):
            return ROWS[k].rearrange("p (a t) -> p a t", a=1).to_broadcast([P, 2, T])

        def plain(ap):
            return ap.bitcast(F32)

        def two(b):
            return bank[b][:, :].rearrange("p (a c) -> p a c", a=2)

        def pb(n):
            stage = PANELS[n][0]
            return n % 2 if stage.startswith("gate") else n % 4 if stage == "wo1" else 4 + n % 4

        def ppb(l, t, half):
            return 4 + (FIRST["ks" if l == 0 else "mk"] + 2 * half + t) % 4

        def turn_bank(k, j):
            if k == "mem":
                return (2, 3, FIRST["gate1"] % 2, 2)[j]
            if k == "mix1":
                return 2 + j % 2
            return 4 + (FIRST["up1"] + j) % 4 if k == "ffn1" else j

        def columns_ready(k, j):
            stage = {"ffn0": "wo0", "mix1": "gate0", "ffn1": "wo1", "blk2": "gate1", "final": "wo2"}.get(k)
            if stage:
                return "ev", FIRST[stage] + j
            return ("loaded", f"x{j // 2}") if k == "mix0" else ("h", "down" + k[-1], 1)

        DEST = {k: (XH, XL) for k in ("mix0", "ple0", "ple1", "blk2")}
        DEST.update({k: (YH, YL) for k in ("ffn0", "mix1", "ffn1", "mem")})
        XUSED = {"ffn0": ("tr", "vec", 4), "ple0": ("pe", last_of("wo0")), "mix1": ("pe", last_of("up0")),
                 "ffn1": ("pe", last_of("qs")), "ple1": ("pe", last_of("wo1")), "mem": ("pe", last_of("up1")),
                 "blk2": ("pe", last_of("gate1"))}
        XIN = {}

        def normed(k):
            return (*DEST[k], 0, {2 * j: [("xl", k, j)] for j in range(4)})

        for s in ("qb", "gb", "fb", "qa", "ka", "ib", "va"):
            XIN[s] = normed("mix0")
        XIN["wo0"] = (XH, XL, 0, {**{k: [("xl", "sb", k)] for k in range(4)}, 4: [("xl", "hg", 0)], 6: [("xl", "hg", 1)]})
        XIN["wo1"] = (XH, XL, 0, {k: [("xl", "sw", k)] for k in range(8)})
        for l in range(2):
            XIN[f"up{l}"] = normed(f"ffn{l}")
            XIN[f"down{l}"] = (GH, GL, 0, {})
            XIN[f"pp{l}"] = (PTH, PTL, 0, {0: [("ptl", l)]})
            XIN[f"gate{l}"] = normed(f"ple{l}")
        for s in ("qs", "ks", "vs"):
            XIN[s] = normed("mix1")
        for s in ("mk", "mv"):
            XIN[s] = normed("mem")
        for s in ("qc", "gc", "qka", "va2", "ga", "vb", "gb2", "ub", "mc", "mb", "ma"):
            XIN[s] = normed("blk2")
        OUT_AT = {"a": 0, "b": MOBA_HEADS, "c": MOBA_HEADS + GROUPS}
        XIN["brc"] = (GH, GL, OUT_AT["c"], {0: [("ol", "c", X_HEADS - 1)]})
        XIN["brb"] = (GH, GL, OUT_AT["b"], {0: [("ol", "b", GROUPS - 1)]})
        XIN["bra"] = (GH, GL, OUT_AT["a"], {0: [("ol", "a", MOBA_HEADS - 1)]})
        XIN["wo2"] = (XH, XL, 0, {2 * j: [("xl", "y", j)] for j in range(4)})
        NORM_OF = {s: "mix0" for s in ("qb", "gb", "fb", "qa", "ka", "ib", "va")}
        NORM_OF.update({s: "mix1" for s in ("qs", "ks", "vs")})
        NORM_OF.update({"up0": "ffn0", "up1": "ffn1", "gate0": "ple0", "gate1": "ple1"})
        NORM_OF.update({s: "blk2" for s in ("qc", "gc", "qka", "va2", "ga", "vb", "gb2", "ub", "mc", "mb", "ma")})

        block = ctx.enter_context(nc.Block())

        @block.sync
        def _(sp):
            def load(dst, src, name):
                sp.dma_start(dst, src).then_inc(*mark(f"load_{name}", ("loaded", name), by=16))

            load(ident[:, :], io["c_ident"], "ident")

            def panel(n):
                stage, i, name, kind, (idx, where) = PANELS[n]
                w = io[name]
                for j in idx:
                    w = w[j]
                slot = n % RAW
                if n >= RAW:
                    sp.wait_ge(*at(("lo", n - RAW)))
                if kind in ("BT", "BF"):
                    src = w[where:where + 256, :].rearrange("(k p) n -> p k n", p=P)
                    sp.dma_start(raw[slot][:, :].rearrange("p (k n) -> p k n", k=2), src).then_inc(*mark(f"panel_loaded{slot}", ("raw", n), by=16))
                elif stage.startswith("up"):
                    dst = raw[slot][:, :].rearrange("p (k c n) -> p k c n", k=KT, c=2)
                    for c in range(2):
                        a = where + c * D_FF
                        sp.dma_start(dst[:, :, c, :], w[:, a:a + P].rearrange("(k p) n -> p k n", p=P)).then_inc(*mark(f"panel_loaded{slot}", ("raw", n), by=16))
                else:
                    src = w[:, where:where + 256].rearrange("(k p) n -> p k n", p=P)
                    sp.dma_start(raw[slot][:, :].rearrange("p (k n) -> p k n", k=KT), src).then_inc(*mark(f"panel_loaded{slot}", ("raw", n), by=16))

            for n in range(len(PANELS)):
                panel(n)
                if n == 0:
                    for half in range(2):
                        c = slice(512 * half, 512 * half + 512)
                        load(h[:, :, c], io["x"][0].rearrange("(t p) d -> p t d", p=P)[:, :, c], f"x{half}")
                if n == 3:
                    load(masks[:, :, :].rearrange("p a b -> p (a b)"), io["c_levels"], "levels")
                    load(reset[:, :], io["c_reset"], "reset")
                    load(tri[:, :], io["c_tri"], "tri")
            for tok in range(TT):
                sp.wait_ge(*at(("result", tok)))
                sp.dma_start(out_ap[0].rearrange("(t p) d -> p t d", p=P)[:, tok, :], result[:, tok, :]).then_inc(*mark("stored", ("stored", tok), by=16))
            sp.wait_ge(*at(("stored", 1)))

        @block.gpsimd
        def _(pool):
            def load(dst, src, name):
                pool.dma_start(dst, src).then_inc(*mark(f"load_{name}", ("loaded", name), by=16))

            def rows(name, pre):
                a = io[name]
                for j in pre:
                    a = a[j]
                return a

            def earlier_only(buf, hd, name, event):
                v = buf[:, hd, :].rearrange("p (a c) -> p a c", a=3)[:, 0:3:2, :]
                pool.affine_select(out=v, in_=v, compare_op=ALU.is_gt, fill=0.0, base=0, pattern=[[0, 2], [1, P]], channel_multiplier=-1).then_inc(*mark(name, event))

            def ffn_mul(l, i):
                pool.wait_ge(*at(("sg", l, i)))
                if i >= 2:
                    pool.wait_ge(*at(("gl", l, i - 2)))
                elif l:
                    pool.wait_ge(*at(("gl", l - 1, FT - 2 + i)))
                pool.tensor_tensor(gf[i % 2][:, :], sgate[i % 2][:, :], cc[i % 3][:, 1, :], ALU.mult).then_inc(*mark("gated", ("gf", l, i)))

            vrow = xn[:, 0, 0:640].rearrange("p (g c) -> p g c", g=5)
            for name, pre, r0, n in VEC_LOADS[1:]:
                src, g, q = rows(name, pre), r0 // P, r0 % P
                if name in ("q_norm", "k_norm"):
                    for k in range(2):
                        load(vrow[q:q + 1, g, 64 * k:64 * k + 64], src.rearrange("(a c) -> a c", a=1), "vectors")
                else:
                    src_rows = src.rearrange("l (a c) -> (l a) c", c=P) if len(src.shape) == 2 else src.rearrange("(a c) -> a c", c=P)
                    load(vrow[q:q + n, g, :], src_rows, "vectors")
            pool.memset(minus_half, -0.5).then_inc(*mark("pool_const", ("half",)))
            pool.memset(ones[:, :], 1.0).then_inc(*mark("pool_const", ("ones",)))
            for step in SCHEDULE:
                kind, args = step[0], step[1:]
                if kind == "stats":
                    k = args[0]
                    pool.wait_ge(*at(("half",)))
                    pool.wait_ge(*at(("ms", k)))
                    pool.tensor_tensor(rstd[k], rstd[k], minus_half, ALU.pow).then_inc(*mark("rstd", ("rstd", k)))
                elif kind == "panel" and PANELS[args[0]][0].startswith("up"):
                    stage, i = PANELS[args[0]][:2]
                    if i >= 2:
                        ffn_mul(int(stage[-1]), i - 2)
                elif kind == "up_tail":
                    ffn_mul(args[0], FT - 2)
                    ffn_mul(args[0], FT - 1)
                elif kind == "hg_mask":
                    li = args[0]
                    if li >= 1:
                        for j in range(2 if li < 6 else 1):
                            a = blocks_of(sc, 2 * j)
                            pool.wait_ge(*at(("prod", li, j)))
                            pool.tensor_tensor(a, a, blocks_of_prod(j), ALU.add).then_inc(*mark("scores_summed", ("sc", li, j)))
                elif kind == "sb_log":
                    for hd in range(SB_HEADS):
                        pool.wait_ge(*at(("splus", hd // 2)))
                        earlier_only(sp_, hd, "softplus_masked", ("spm", hd // 2))
                elif kind == "sb_weights":
                    i = args[0]
                    pool.wait_ge(*at(("w", i)))
                    for r in range(2):
                        earlier_only(zs, 2 * i + r, "weights_masked", ("wm", i))
                elif kind == "ffn_loads":
                    l = args[0]
                    if l == 1:
                        pool.wait_ge(*at(("pt", 0, 1)))
                    else:
                        pool.wait_ge(*at(("ev", last_of("wo0"))))
                    load(praw[:, :, :], io["p"][l, 0].rearrange("(t p) d -> p t d", p=P), f"p{l}")
                    if l == 0:
                        load(relb[:, :], io["rel_bias"], "rel")
                        load(buck[:, :], io["c_bucket"], "buck")
                        load(sinks, bass.AP(tensor=io["sinks"].tensor, offset=0, ap=[[0, P], [1, SW_HEADS]]), "sinks")
                        pool.memset(brow[:, :], NEG).then_inc(*mark("bias_row_clear", ("brow0",)))
                elif kind == "bias":
                    pool.wait_ge(*at(("brow",)))
                    load(scratch, brow[:, :].rearrange("h (a c) -> h a c", a=1).to_broadcast([SW_HEADS, P, BW]), "bias_rows")
                    pool.wait_ge(*at(("loaded", "bias_rows")))
                    load(bias[:, :, :], bass.AP(tensor=scratch.tensor, offset=P - 1, ap=[[BW - 1, P], [P * BW, SW_HEADS], [1, T]]), "bias")
                elif kind == "ple_input" and args[0] == 1:
                    pool.wait_ge(*at(("pe", last_of("down1"))))
                    load(mem[:, :, :], io["mem_2"][0].rearrange("(t p) d -> p t d", p=P), "mem")
                elif kind == "turn" and args == ("blk2", 3):
                    pool.wait_ge(*at(("pe", last_of("mv"))))
                    pool.wait_ge(*at(("ev", last_of("gate1"))))
                    load(wsp_raw, io["w_spatial_2"][0].rearrange("g t s -> t g s"), "wsp")
                    load(bsp[:, :, :].rearrange("p g t -> p (g t)"),
                         bass.AP(tensor=io["b_spatial_2"].tensor, offset=0, ap=[[0, P], [1, GROUPS * P]]), "bsp")
                    load(causal[:, :], io["c_causal"], "causal")
                    load(small[:, 0:64], io["c_rope"], "rope")
                    pool.wait_ge(*at(("loaded", "wsp")))
                    pool.affine_select(out=wsp_raw, in_=wsp_raw, compare_op=ALU.is_ge, fill=0.0, base=0, pattern=[[0, GROUPS], [-1, P]], channel_multiplier=1).then_inc(*mark("spatial_masked", ("wspm",)))
                elif kind == "y_split":
                    pool.wait_ge(*at(("yb", "a", 3)))
                    load(gfin[:, :], bass.AP(tensor=io["final_norm_g_2"].tensor, offset=0, ap=[[0, P], [1, D]]), "gfin")

        @block.tensor
        def _(pe):
            reader = {}

            def claim(b, event):
                if b in reader:
                    pe.wait_ge(*at(reader[b]))
                reader[b] = event

            def panel(n, head=False):
                stage, i, name, kind, _where = PANELS[n]
                xh, xl, k0, needs = XIN[stage]
                wh, wl = whi[n % RING], wlo[n % RING]
                parted = HEAD_TILES.get(n, 0)
                pe.wait_ge(*at(("lo", n)))

                def input_ready(k):
                    if k == 4 and n in LATE_TURN:
                        turn(LATE_TURN[n], 3)
                    for before in needs.get(k, ()):
                        pe.wait_ge(*at(before))
                if kind == "T":
                    b = pb(n)
                    if head or not parted:
                        claim(b, ("ev", n) if not stage.startswith("gate") else ("a", n))
                    wv = [w[:, :].rearrange("p (k n) -> p k n", k=KT) for w in (wh, wl)]
                    for t in range(TT):
                        for k in range(parted) if head else range(parted, KT):
                            if t == 0 and k == 2 and n - 1 in ROWS_AFTER:
                                norm_row(ROWS_AFTER[n - 1])
                            if t == 0 and i == 0:
                                input_ready(k)
                            for m, (x, w) in enumerate(((xh, 0), (xh, 1), (xl, 0))):
                                mm = pe.matmul(bank[b][:, t * 256:t * 256 + 256], x[:, k, t * P:(t + 1) * P], wv[w][:, k, :],
                                               start=(k == 0 and m == 0 and not (parted and t)), stop=(k == KT - 1 and m == 2),
                                               skip_group_check=parted > 0)
                    if head:
                        return
                elif kind == "F":
                    b = pb(n)
                    claim(b, ("ev", n))
                    wv = [w[:, :].rearrange("p (k n) -> p k n", k=KT) for w in (wh, wl)]
                    for c in range(2):
                        for k in range(KT):
                            if c == 0 and i == 0:
                                input_ready(k)
                            if c == 0 and k == 2 and n - 1 in ROWS_AFTER:
                                norm_row(ROWS_AFTER[n - 1])
                            for m, (x, w) in enumerate(((xh, 0), (xl, 0), (xh, 1))):
                                mm = pe.matmul(bank[b][:, c * 256:c * 256 + 256], wv[w][:, k, c * P:(c + 1) * P], x[:, k, :],
                                               start=(k == 0 and m == 0), stop=(k == KT - 1 and m == 2))
                elif kind == "BT":
                    last, l, down = n == last_of(stage), int(stage[-1]), stage.startswith("down")
                    if down:
                        pe.wait_ge(*at(("gl", l, 2 * i + 1)))
                    else:
                        input_ready(0)
                    out_bank = lambda t, half: 2 * t + half if down else ppb(l, t, half)
                    if i == 0:
                        for t in range(TT):
                            for half in range(2):
                                claim(out_bank(t, half), ("h", stage, t) if down else ("ev", FIRST[f"gate{l}"] + 2 * half + 1))
                    wv = [w[:, :].rearrange("p (k n) -> p k n", k=2) for w in (wh, wl)]
                    for t in range(TT):
                        for k in range(2):
                            for m, (x, w) in enumerate(((xh, 0), (xh, 1), (xl, 0))):
                                for half in range(2):
                                    mm = pe.matmul(bank[out_bank(t, half)][:, :], x[:, 2 * i + k, t * P:(t + 1) * P],
                                                   wv[w][:, k, half * 512:half * 512 + 512],
                                                   start=(i == 0 and k == 0 and m == 0), stop=(last and k == 1 and m == 2))
                        if last and t == 0:
                            mm.then_inc(*mark("product", ("tok0", stage)))
                else:
                    last = n == last_of(stage)
                    if i == 0:
                        input_ready(0)
                        for b in range(4):
                            claim(b, ("yb", stage[-1], b))
                    wv = [w[:, :].rearrange("p (k n) -> p k n", k=2) for w in (wh, wl)]
                    for f in range(KT):
                        for k in range(2):
                            for m, (x, w) in enumerate(((xh, 0), (xl, 0), (xh, 1))):
                                mm = pe.matmul(bank[f // 2][:, (f % 2) * 256:(f % 2) * 256 + 256],
                                               wv[w][:, k, f * P:(f + 1) * P], x[:, k0 + 2 * i + k, :],
                                               start=(i == 0 and k == 0 and m == 0 and f % 2 == 0),
                                               stop=(last and k == 1 and m == 2), skip_group_check=True)
                        if last and f % 2 and f < KT - 1:
                            mm.then_inc(*mark("product", ("summed", stage, f // 2)))
                mm.then_inc(*mark("product", ("pe", n), *([("summed", stage, 3)] if kind == "BF" and n == last_of(stage) else [])))

            def norm_row(k):
                pe.wait_ge(*at(("rstd", k)))
                claim(0, ("rows", k))
                for t in range(TT):
                    mm = pe.transpose(bank[0][:, t * P:(t + 1) * P], rstd[k][:, t:t + 1].to_broadcast([P, P]), ident[:, :])
                mm.then_inc(*mark("turned", ("tr", "rows", k)))

            def turn(k, j):
                src = mem if k == "mem" else h
                pe.wait_ge(*at(("loaded", "ident")))
                if k == "mem":
                    pe.wait_ge(*at(("xn", k, 0)))
                    pe.wait_ge(*at(("xn", k, 1)))
                else:
                    pe.wait_ge(*at(columns_ready(k, j)))
                b = turn_bank(k, j)
                claim(b, ("xl", k, j))
                for q in range(2):
                    for t in range(TT):
                        kt = 2 * j + q
                        mm = pe.transpose(bank[b][:, q * 256 + t * P:q * 256 + (t + 1) * P], src[:, t, kt * P:(kt + 1) * P], ident[:, :])
                mm.then_inc(*mark("turned", ("tr", k, j)))

            def three_blocks(b, src, width):
                pe.transpose(bank[b][:, 0:P], src[:, 0, 0:P], ident[:, :])
                pe.transpose(bank[b][:, P:2 * P], src[:, 1, 0:P], ident[:, :])
                return pe.transpose(bank[b][:, 2 * P:3 * P], src[:, 1, P:2 * P], ident[:, :])

            def weigh(dst, v0, v1, w):
                pe.matmul(dst(0), v0, w[:, 0:2 * P], start=True, stop=False)
                return pe.matmul(dst(P), v1, w[:, 2 * P:3 * P], start=False, stop=True)

            for step in SCHEDULE:
                kind, args = step[0], step[1:]
                if kind == "panel":
                    panel(args[0])
                elif kind == "panel_head":
                    panel(args[0], head=True)
                elif kind == "setup":
                    pe.wait_ge(*at(("loaded", "ident")))
                    if args[0] == 0:
                        pe.wait_ge(*at(("loaded", "mix_gain")))
                        claim(4, ("gain0",))
                        pe.transpose(bank[4][:, 0:2 * KT], xn[0:2 * KT, 0, 0:P], ident[0:2 * KT, 0:2 * KT]).then_inc(*mark("turned", ("tr", "gain0")))
                        continue
                    pe.wait_ge(*at(("loaded", "vectors")))
                    for g in range(5):
                        if g in (0, 4):
                            claim(1 + g // 4, ("vec", 3 if g == 0 else 4))
                        mm = pe.transpose(bank[1 + g // 4][:, g % 4 * P:g % 4 * P + VEC_ROWS[g]], xn[0:VEC_ROWS[g], 0, g * P:(g + 1) * P], ident[0:VEC_ROWS[g], 0:VEC_ROWS[g]])
                        mm.then_inc(*mark("turned", ("tr", "vec", g)))
                elif kind == "turn":
                    turn(*args)
                elif kind == "hg_scores":
                    li = args[0]
                    if li < 0:
                        pe.wait_ge(*at(("xs", li)))
                        claim(0, ("sc", -1, 0))
                        for hd in range(HG_HEADS):
                            X = xs_buf[1]
                            mm = pe.matmul(bank[0][:, hd * P:(hd + 1) * P], X[:, hd, 0:P], X[:, hd, P:T], start=True, stop=True)
                        mm.then_inc(*mark("scores", ("ps", -1, 0)))
                    else:
                        if LEVELS[li]:
                            pe.wait_ge(*at(("xs", li)))
                            A = B = xs_buf[li % 2]
                        else:
                            pe.wait_ge(*at(("kk",)))
                            A, B = kk, qf
                        for j in range(2):
                            b = (2 * li + j + 2) % 4
                            claim(b, ("prod", li, j))
                            for q in range(2):
                                for t in range(TT):
                                    hd = 2 * j + q
                                    mm = pe.matmul(bank[b][:, (2 * q + t) * P:(2 * q + t + 1) * P],
                                                   A[:, hd, t * P:(t + 1) * P], B[:, hd, t * P:(t + 1) * P], start=True, stop=True)
                            mm.then_inc(*mark("scores", ("ps", li, j)))
                elif kind == "hg_out":
                    pe.wait_ge(*at(("sc", len(LEVELS) - 1, 0)))
                    pe.wait_ge(*at(("sc", len(LEVELS) - 1, 1)))
                    pe.wait_ge(*at(("sc", -1, 0)))
                    pe.wait_ge(*at(("ev", last_of("ib"))))
                    for t in range(TT):
                        claim(t, ("on", t))
                        for hd in range(HG_HEADS):
                            o, v = bank[t][:, hd * P:(hd + 1) * P], ib[:, :, hd * P:(hd + 1) * P]
                            if t == 0:
                                mm = pe.matmul(o, sc[:, hd, 0:P], v[:, 0, :], start=True, stop=True)
                            else:
                                pe.matmul(o, sc[:, hd, P:2 * P], v[:, 0, :], start=True, stop=False)
                                mm = pe.matmul(o, sc[:, hd, 2 * P:3 * P], v[:, 1, :], start=False, stop=True)
                        mm.then_inc(*mark("weighted", ("hgo", t)))
                elif kind == "hg_turn":
                    pe.wait_ge(*at(("gated", 0)))
                    pe.wait_ge(*at(("gated", 1)))
                    for j in range(2):
                        claim(2 + j, ("xl", "hg", j))
                        for q in range(2):
                            for t in range(TT):
                                mm = pe.transpose(bank[2 + j][:, q * 256 + t * P:q * 256 + (t + 1) * P], on[:, t, 2 * j + q, :], ident[:, :])
                        mm.then_inc(*mark("turned", ("tr", "hg", j)))
                elif kind == "sb_scores":
                    i = args[0]
                    pe.wait_ge(*at(("ev", last_of("qa"))))
                    pe.wait_ge(*at(("ev", last_of("ka"))))
                    for r in range(2):
                        hd = 2 * i + r
                        b, q = 4 + hd % 4, slice(64 * r, 64 * r + 64)
                        claim(b, ("z", hd))
                        pe.matmul(bank[b][:, 0:T], kaT[q, i, 0:P], qaT[q, i, :], start=True, stop=True)
                        mm = pe.matmul(bank[b][:, T:T + P], kaT[q, i, P:T], qaT[q, i, P:T], start=True, stop=True)
                        mm.then_inc(*mark("scores", ("sbz", hd)))
                elif kind == "sb_weights":
                    i = args[0]
                    pe.wait_ge(*at(("spm", i)))
                    pe.wait_ge(*at(("loaded", "tri")))
                    pe.wait_ge(*at(("ones",)))
                    for r in range(2):
                        hd = 2 * i + r
                        b, a = 4 + hd % 4, sp_[:, hd, :]
                        claim(b, ("d", hd))
                        pe.matmul(bank[b][:, 0:T], tri[:, :], a[:, 0:T], start=True, stop=False)
                        pe.matmul(bank[b][:, P:T], ones[:, :], a[:, T:T + P], start=False, stop=True)
                        mm = pe.matmul(bank[b][:, T:T + P], tri[:, :], a[:, T:T + P], start=True, stop=True)
                        mm.then_inc(*mark("weighted", ("sbr", hd)))
                elif kind == "sb_out":
                    i = args[0]
                    b = 4 + i
                    pe.wait_ge(*at(("wm", i)))
                    pe.wait_ge(*at(("ev", last_of("va"))))
                    claim(b, ("xl", "sb", i))
                    for r in range(2):
                        hd = 2 * i + r
                        mm = weigh(lambda c: bank[b][64 * r:64 * r + 64, c:T], va[:, 0, hd * 64:hd * 64 + 64],
                                   va[:, 1, hd * 64:hd * 64 + 64], zs[:, hd, :])
                    mm.then_inc(*mark("weighted", ("sbo", i)))
                elif kind == "ple_input":
                    l = args[0]
                    pe.wait_ge(*at(("loaded", f"p{l}")))
                    claim(4, ("ptl", l))
                    for q in range(2):
                        for t in range(TT):
                            mm = pe.transpose(bank[4][:, q * 256 + t * P:q * 256 + (t + 1) * P], praw[:, t, q * P:(q + 1) * P], ident[:, :])
                    mm.then_inc(*mark("turned", ("pt", l, 1)))
                elif kind == "bias":
                    pe.wait_ge(*at(("loaded", "rel")))
                    pe.wait_ge(*at(("loaded", "buck")))
                    claim(5, ("brow",))
                    pe.matmul(bank[5][0:16, 0:P], relb[:, :], buck[:, :], start=True, stop=True).then_inc(*mark("weighted", ("brp",)))
                elif kind == "sw_turn":
                    half = args[0]
                    for j in ((4, 5, 0, 1) if half == 0 else (2, 3)):
                        pe.wait_ge(*at(("qkn", half, 0)))
                        pe.wait_ge(*at(("qkn", half, 1)))
                        b = 4 + j % 4
                        claim(b, ("qsT", j))
                        for q in range(2):
                            for t in range(TT):
                                mm = pe.transpose(bank[b][:, q * 256 + t * P:q * 256 + (t + 1) * P],
                                                  qkn[:, t, 4 * j + 2 * q:4 * j + 2 * q + 2, :].rearrange("p a d -> p (a d)"), ident[:, :])
                        mm.then_inc(*mark("turned", ("tr", "sw", j)))
                elif kind == "sw_logits":
                    g = args[0]
                    for j in ((4, 5, 0, 1) if g < 2 else (2, 3)):
                        pe.wait_ge(*at(("qsT", j)))
                    for j in range(4):
                        hd = 4 * g + j
                        q = slice(64 * (hd % 2), 64 * (hd % 2) + 64)
                        claim(j, ("swm", g, j))
                        pe.matmul(bank[j][:, 0:P], qsT[q, hd // 2, 0:P], ksT[q, g, 0:P], start=True, stop=True)
                        mm = pe.matmul(bank[j][:, T:2 * T], qsT[q, hd // 2, P:T], ksT[q, g, :], start=True, stop=True)
                        mm.then_inc(*mark("scores", ("swz", g, j)))
                elif kind == "sw_weights":
                    g = args[0]
                    for j in range(4):
                        pe.wait_ge(*at(("swn", g, j, 0)))
                        pe.wait_ge(*at(("swn", g, j, 1)))
                        claim(4 + j, ("swt", g, j))
                        three_blocks(4 + j, le_s[g % 2][:, j, :, :], T).then_inc(*mark("turned", ("tr", "sww", g, j)))
                elif kind == "sw_out":
                    g = args[0]
                    for q in range(2):
                        pe.wait_ge(*at(("swt", g, 2 * q)))
                        pe.wait_ge(*at(("swt", g, 2 * q + 1)))
                        pe.wait_ge(*at(("ev", last_of("vs"))))
                        b = 4 + q
                        claim(b, ("xl", "sw", 2 * g + q))
                        for r in range(2):
                            mm = weigh(lambda c: bank[b][64 * r:64 * r + 64, c:T], vsw[:, 0, 64 * g:64 * g + 64],
                                       vsw[:, 1, 64 * g:64 * g + 64], wT_s[:, 2 * q + r, :])
                        mm.then_inc(*mark("weighted", ("swo", 2 * g + q)))
                elif kind == "x_logits":
                    g = args[0]
                    pe.wait_ge(*at(("ev", last_of("mk"))))
                    pe.wait_ge(*at(("ev", last_of("qc"))))
                    for j in range(2):
                        hd = 2 * g + j
                        claim(j, ("e", "x", hd))
                        for t in range(TT):
                            mm = pe.matmul(bank[j][:, t * T:(t + 1) * T], qc[:, hd, t * P:(t + 1) * P], mk[:, hd, :], start=True, stop=True)
                        mm.then_inc(*mark("scores", ("xz", hd)))
                elif kind == "x_weights":
                    g = args[0]
                    for j in range(2):
                        hd = 2 * g + j
                        pe.wait_ge(*at(("n", "x", hd)))
                        claim(2 + j, ("wT", "x", hd))
                        for m in range(2):
                            for t in range(TT):
                                mm = pe.transpose(bank[2 + j][:, m * T + t * P:m * T + (t + 1) * P], le[:, j, t, m * P:(m + 1) * P], ident[:, :])
                        mm.then_inc(*mark("turned", ("trw", "x", hd)))
                elif kind == "x_out":
                    g = args[0]
                    for j in range(2):
                        hd = 2 * g + j
                        pe.wait_ge(*at(("wT", "x", hd)))
                        pe.wait_ge(*at(("ev", last_of("mv"))))
                        claim(2 + j, ("og", "c", hd))
                        for m in range(2):
                            mm = pe.matmul(bank[2 + j][:, 0:T], mv[:, m, hd * P:(hd + 1) * P], wT[:, j, m, :], start=(m == 0), stop=(m == 1))
                        mm.then_inc(*mark("weighted", ("oz", "c", hd)))
                elif kind == "rope_turn":
                    pe.wait_ge(*at(("roped",)))
                    for j in range(3 * args[0], 3 * args[0] + 3):
                        b = j % 4
                        claim(b, ("qkF", j))
                        for q in range(2):
                            for t in range(TT):
                                c = (2 * j + q) * P
                                mm = pe.transpose(bank[b][:, q * T + t * P:q * T + (t + 1) * P], qkm[:, t, c:c + P], ident[:, :])
                        mm.then_inc(*mark("turned", ("tr", "rope", j)))
                elif kind == "spatial":
                    pe.wait_ge(*at(("wspm",)))
                    for j in range(2):
                        claim(2 + j, ("wspT", j))
                        for q in range(3):
                            mm = pe.transpose(bank[2 + j][:, q * P:(q + 1) * P], wsp_raw[:, 3 * j + q, :], ident[:, :])
                        mm.then_inc(*mark("turned", ("tr", "wsp", j)))
                elif kind == "a_logits":
                    g = args[0]
                    pe.wait_ge(*at(("qkF", 4)))
                    pe.wait_ge(*at(("qkF", 5)))
                    for j in range(2):
                        hd = 2 * g + j
                        claim(j, ("am", hd))
                        pe.matmul(bank[j][:, 0:P], qF[:, hd, 0:P], kF[:, hd, 0:P], start=True, stop=True)
                        mm = pe.matmul(bank[j][:, T:2 * T], qF[:, hd, P:T], kF[:, hd, :], start=True, stop=True)
                        mm.then_inc(*mark("scores", ("az", hd)))
                elif kind == "a_weights":
                    g = args[0]
                    for j in range(2):
                        hd = 2 * g + j
                        pe.wait_ge(*at(("n", "a", hd)))
                        claim(2 + j, ("wT", "a", hd))
                        three_blocks(2 + j, le[:, j, :, :], T).then_inc(*mark("turned", ("trw", "a", hd)))
                elif kind == "a_out":
                    g = args[0]
                    for j in range(2):
                        hd = 2 * g + j
                        pe.wait_ge(*at(("wT", "a", hd)))
                        pe.wait_ge(*at(("ev", last_of("va2"))))
                        claim(2 + j, ("og", "a", hd))
                        w = wT[:, j, :, :].rearrange("p a b -> p (a b)")
                        mm = weigh(lambda c: bank[2 + j][:, c:T], va2[:, 0, hd * P:(hd + 1) * P], va2[:, 1, hd * P:(hd + 1) * P], w)
                        mm.then_inc(*mark("weighted", ("oz", "a", hd)))
                elif kind == "mixed":
                    pe.wait_ge(*at(("vn", 0)))
                    pe.wait_ge(*at(("vn", 1)))
                    pe.wait_ge(*at(("wspT", 0)))
                    pe.wait_ge(*at(("wspT", 1)))
                    for j in range(3):
                        claim(j, ("mixg", 2 * j + 1))
                        for q in range(2):
                            g = 2 * j + q
                            for t in range(TT):
                                mm = pe.matmul(bank[j][:, q * T + t * P:q * T + (t + 1) * P], vb[:, t, g * P:(g + 1) * P], wsp[:, g, :], start=True, stop=True)
                        mm.then_inc(*mark("weighted", ("mixp", j)))

        @block.scalar
        def _(act):
            def split(n):
                if n < len(PANELS):
                    act.wait_ge(*at(("raw", n)))
                    if n >= RING:
                        act.wait_ge(*at(("pe", n - RING)))
                    act.activation(whi[n % RING][:, :], raw[n % RAW][:, :], ACT.Copy).then_inc(*mark("weights_hi", ("hi", n)))

            act.dma_start(xn[0:2 * KT, 0, 0:P], io["mix_norm"].rearrange("l (a c) -> (l a) c", c=P)).then_inc(*mark("load_mix_gain", ("loaded", "mix_gain"), by=16))

            act.wait_ge(*at(("loaded", "ident")))
            act.activation(lb_tmp[:, 0:1], ident[:, 0:1], ACT.Silu).then_inc(*mark("tables", ("table",)))

            def parts(src, gain, dst, event, *first):
                for before in first:
                    act.wait_ge(*at(before))
                if gain is None:
                    act.activation(dst, src, ACT.Copy).then_inc(*mark("input_hi", event))
                else:
                    act.activation(dst, src, ACT.Copy, scale=gain).then_inc(*mark("input_hi", event))

            def ffn_gate(l, i):
                act.wait_ge(*at(("conv", l, i)))
                if l > 0 or i >= 2:
                    act.wait_ge(*at(("gf", l, i - 2) if i >= 2 else ("gf", l - 1, FT - 2 + i)))
                act.activation(sgate[i % 2][:, :], cc[i % 3][:, 0, :], ACT.Silu).then_inc(*mark("gate_done", ("sg", l, i)))

            def ffn_hi(l, i):
                act.wait_ge(*at(("gf", l, i)))
                act.activation(GH[:, i, :], gf[i % 2][:, :], ACT.Copy).then_inc(*mark("gated_hi", ("gh", l, i)))

            def panel(n):
                stage, i, name, kind, _where = PANELS[n]
                b = pb(n)
                c2, cT = slice(2 * i, 2 * i + 2), slice(256 * i, 256 * i + 256)
                ev = ("ev", n)
                if kind != "T" and not splits_later(n):
                    split(n + RING)
                if n in ROWS_AFTER:
                    k = ROWS_AFTER[n]
                    act.wait_ge(*at(("tr", "rows", k)))
                    act.activation(ROWS[k], bank[0][:, 0:T], ACT.Copy).then_inc(*mark("rows", ("rows", k)))
                if kind == "T" and stage in NORM_OF:
                    norm = NORM_OF[stage]
                    if stage.startswith("gate"):
                        if i >= 2:
                            act.wait_ge(*at(("ev", n - 2)))
                        elif stage == "gate1":
                            act.wait_ge(*at(("ev", last_of("gate0"))))
                        dst, func, event = gate[i % 2][:, :, :], ACT.Sigmoid, ("a", n)
                    else:
                        func, event = ACT.Silu if stage == "gb" else ACT.Copy, ev
                        a = 1024 if stage == "ks" else 256 * i
                        dst = {"ib": ib, "gb": gbs, "va": va, "qs": qk, "ks": qk, "vs": vsw, "qka": qkm, "va2": va2, "vb": vb}[stage][:, :, a:a + 256]
                    act.wait_ge(*at(("rstd", norm)))
                    act.wait_ge(*at(("pe", n)))
                    for t in range(TT):
                        act.activation(dst[:, t, :], two(b)[:, t, :], func, scale=rstd[norm][:, t:t + 1]).then_inc(*mark("projected", event))
                elif kind == "F" and stage in ("qb", "gc", "ga", "gb2", "mc", "mb", "ma"):
                    dst = {"qb": qf, "gc": gc, "ga": ga, "gb2": ubs, "mc": msig[0], "mb": msig[1], "ma": msig[0]}[stage][:, c2, :]
                    act.wait_ge(*at(("scaled", n)))
                    act.activation(dst, dst, ACT.Sigmoid if stage[0] == "m" else ACT.Silu).then_inc(*mark("projected", ev))
                elif stage == "fb":
                    act.wait_ge(*at(("scaled", n)))
                    act.activation(kk[:, c2, :], bdec[:, c2, :], ACT.Sigmoid, scale=-1.0).then_inc(*mark("projected", ("sig", i)))
                    act.activation(bdec[:, c2, :], bdec[:, c2, :], ACT.Sigmoid).then_inc(*mark("projected", ev))
                elif stage.startswith("up"):
                    l = int(stage[-1])
                    if l > 0 or i >= 3:
                        act.wait_ge(*at(("gf", l, i - 3) if i >= 3 else ("gf", l - 1, FT - 1)))
                    act.wait_ge(*at(("scaled", n)))
                    for c in range(2):
                        j = c * FT + i
                        act.activation(cc[i % 3][:, c, :], conv_in[i % 2][:, c, :], ACT.Identity, scale=vec("ffn_conv", l, 2)(j), bias=vec("ffn_conv_b", l)(j)).then_inc(*mark("projected", ("a", n)))
                elif stage == "mk":
                    act.wait_ge(*at(("pe", n)))
                    act.activation(mk[:, c2, :], two(b), ACT.Copy).then_inc(*mark("projected", ev))
                elif stage == "mv":
                    act.wait_ge(*at(("pe", n)))
                    act.activation(mv[:, :, cT], two(b), ACT.Copy).then_inc(*mark("projected", ev))
                if kind == "T" and not splits_later(n):
                    split(n + RING)
                if stage.startswith("up"):
                    if i >= 1:
                        ffn_gate(l, i - 1)
                    if i >= 2:
                        ffn_hi(l, i - 2)

            def soft(tag, hd, j, scale):
                act.wait_ge(*at(("neg", tag, hd)))
                for t in range(TT):
                    c = 2 * j + t
                    if tag == "x":
                        src, dst = bank[j][:, t * T:(t + 1) * T], le[:, j, t, :]
                    else:
                        w = slice(0, P) if t == 0 else slice(0, T)
                        src = dst = le[:, j, t, w]
                    act.activation(dst, src, ACT.Exp, scale=scale, bias=s_neg[:, c:c + 1], accum_out=s_sum[:, c:c + 1]).then_inc(*mark("exponentials", ("e", tag, hd)))

            for step in SCHEDULE:
                kind, args = step[0], step[1:]
                if kind == "panel":
                    panel(args[0])
                elif kind == "split":
                    split(args[0])
                elif kind == "setup":
                    if args[0] == 0:
                        act.wait_ge(*at(("tr", "gain0")))
                        act.activation(vecs[:, 0, 0:2 * KT], bank[4][:, 0:2 * KT], ACT.Copy).then_inc(*mark("vectors", ("gain0",)))
                        continue
                    for g in range(5):
                        c = 0 if g else 2 * KT
                        act.wait_ge(*at(("tr", "vec", max(g, 3))))
                        act.activation(vecs[:, g, c:VEC_ROWS[g]], bank[1 + g // 4][:, g % 4 * P + c:g % 4 * P + VEC_ROWS[g]], ACT.Copy).then_inc(*mark("vectors", ("vec", g)))
                    act.wait_ge(*at(("lb0",)))
                    act.activation(lb_tmp, lb_tmp, ACT.Exp).then_inc(*mark("vectors", ("lbe",)))
                elif kind == "square":
                    k, j = args
                    act.wait_ge(*at(columns_ready(k, j)))
                    if k == "final" and j == 0:
                        act.wait_ge(*at(("xl", "y", 3)))
                    if j:
                        act.wait_ge(*at(("sq", k, j - 1)))
                    for t in range(TT):
                        dst = xn[:, t, 0:256] if k == "final" else junk[t]
                        act.activation(dst, h[:, t, 256 * j:256 * j + 256], ACT.Square, accum_out=ssq[k][:, 4 * t + j:4 * t + j + 1]).then_inc(*mark("squared", ("sq", k, j)))
                elif kind == "stats":
                    k = args[0]
                    if k == "mem":
                        act.wait_ge(*at(("loaded", "mem")))
                        for t in range(TT):
                            for j in range(4):
                                if t or j:
                                    act.wait_ge(*at(("sq", k, 4 * t + j - 1)))
                                act.activation(mem_junk[:, 0:256], mem[:, t, 256 * j:256 * j + 256], ACT.Square, accum_out=ssq[k][:, 4 * t + j:4 * t + j + 1]).then_inc(*mark("squared", ("sq", k, 4 * t + j)))
                        act.wait_ge(*at(("rstd", k)))
                        act.activation(mem[:, 1, :], mem[:, 1, :], ACT.Copy, scale=rstd[k][:, 1:2]).then_inc(*mark("normalized", ("xn", k, 1)))
                    elif k == "final":
                        act.wait_ge(*at(("rstd", k)))
                        act.wait_ge(*at(("hgn", 3)))
                        act.activation(result[:, 1, :], result[:, 1, :], ACT.Copy, scale=rstd[k][:, 1:2]).then_inc(*mark("result1", ("result", 1)))
                elif kind in ("turn", "turn_last"):
                    k, j = args if kind == "turn" else (args[0], 3)
                    if k in XUSED:
                        act.wait_ge(*at(XUSED[k]))
                    act.wait_ge(*at(("gain0",) if k == "mix0" else ("vec", 0)))
                    act.wait_ge(*at(("tr", k, j)))
                    for q in range(2):
                        kt = 2 * j + q
                        act.activation(DEST[k][0][:, kt, :], two(turn_bank(k, j))[:, q, :], ACT.Copy, scale=GAIN[k](kt)).then_inc(*mark("input_hi", ("xh", k, j)))
                elif kind == "hg_decay":
                    act.wait_ge(*at(("f",)))
                    act.activation(ex[:, :, :], bdec[:, :, :], ACT.Ln).then_inc(*mark("levels", ("logf",)))
                elif kind == "hg_level":
                    li = args[0]
                    if li < 0 or LEVELS[li]:
                        e = ex if li % 2 == 0 else exb
                        act.wait_ge(*at(("dd", li)))
                        act.activation(e[:, :, :], e[:, :, :], ACT.Exp).then_inc(*mark("levels", ("ex", li)))
                elif kind == "sb_scores":
                    i = args[0]
                    if i == 0:
                        act.wait_ge(*at(("loaded", "reset")))
                    for r in range(2):
                        hd = 2 * i + r
                        b = 4 + hd % 4
                        act.wait_ge(*at(("sbz", hd)))
                        act.activation(sp_[:, hd, :], bank[b][:, 0:384], ACT.Abs).then_inc(*mark("sb_scores", ("az0", hd)))
                        act.activation(zs[:, hd, :], bank[b][:, 0:384], ACT.Copy).then_inc(*mark("sb_scores", ("z", hd)))
                elif kind == "sb_log":
                    for i in range(4):
                        c = slice(2 * i, 2 * i + 2)
                        act.wait_ge(*at(("z", 2 * i + 1)))
                        act.activation(sp_[:, c, :], sp_[:, c, :], ACT.Exp, scale=-1.0).then_inc(*mark("sb_logs", ("sbe", i)))
                    for i in range(4):
                        c = slice(2 * i, 2 * i + 2)
                        act.wait_ge(*at(("sbe", i)))
                        act.activation(sp_[:, c, :], sp_[:, c, :], ACT.Ln, bias=1.0).then_inc(*mark("sb_logs", ("sbl", i)))
                elif kind == "hg_out":
                    for t in range(TT):
                        act.wait_ge(*at(("hgo", t)))
                        if t == 0:
                            act.wait_ge(*at(("sc", len(LEVELS) - 1, 1)))
                        act.activation(prod4[:, t, :], bank[t][:, :], ACT.Square).then_inc(*mark("squared", ("hgsq", t)))
                elif kind == "hg_turn":
                    for j in range(2):
                        parts(two(2 + j), vec("hg_out_norm", 0)(0), XH[:, 4 + 2 * j:6 + 2 * j, :], ("xh", "hg", j),
                              ("tr", "hg", j), ("pe", last_of("gb")))
                elif kind == "sb_weights":
                    i = args[0]
                    act.wait_ge(*at(("d", 2 * i + 1)))
                    c = slice(2 * i, 2 * i + 2)
                    act.activation(zs[:, c, :], zs[:, c, :], ACT.Exp).then_inc(*mark("sb_weights", ("w", i)))
                elif kind == "sb_out":
                    i = args[0]
                    parts(bank[4 + i][:, 0:T], None, XH[:, i, :], ("xh", "sb", i), ("sbo", i), ("pe", last_of("gb")))
                elif kind == "up_tail":
                    l = args[0]
                    ffn_gate(l, FT - 1)
                    ffn_hi(l, FT - 2)
                    ffn_hi(l, FT - 1)
                elif kind == "ple_input":
                    l = args[0]
                    if l == 1:
                        act.wait_ge(*at(("pe", last_of("pp0"))))
                    parts(two(4), None, PTH[:, :, :], ("pth", l), ("pt", l, 1))
                elif kind == "sw_norm":
                    half = args[0]
                    act.wait_ge(*at(("ev", FIRST["qs"] + 2 * half + 1)))
                    for t in range(TT):
                        for c in ((slice(0, 512), slice(1024, 1280)) if half == 0 else (slice(512, 1024),)):
                            act.activation(sq[:, t, c], qk[:, t, c], ACT.Square).then_inc(*mark("squared", ("swsq", half, t)))
                elif kind == "sw_turn":
                    half = args[0]
                    for j in ((4, 5, 0, 1) if half == 0 else (2, 3)):
                        act.wait_ge(*at(("tr", "sw", j)))
                        if j < 4:
                            act.activation(qsT[:, 2 * j:2 * j + 2, :], two(4 + j % 4), ACT.Copy, scale=q_gain).then_inc(*mark("sw_turned", ("qsT", j)))
                        else:
                            act.activation(ksT[:, 2 * j - 8:2 * j - 6, :], two(4 + j % 4), ACT.Copy, scale=vec("k_norm", 0)(0)).then_inc(*mark("sw_turned", ("qsT", j)))
                elif kind == "sw_exp":
                    g = args[0]
                    s_max, s_neg, s_sum, s_exp = sw_cols[g % 2]
                    act.wait_ge(*at(("swneg", g)))
                    for j in range(4):
                        for t in range(TT):
                            c = 2 * j + t
                            v = le_s[g % 2][:, j, t, 0:P if t == 0 else T]
                            act.activation(v, v, ACT.Exp, bias=s_neg[:, c:c + 1], accum_out=s_sum[:, c:c + 1]).then_inc(*mark("exponentials", ("swe", g, j)))
                    act.activation(s_exp, s_exp, ACT.Exp).then_inc(*mark("exponentials", ("swx", g)))
                elif kind == "sw_weights":
                    g = args[0]
                    s_sum = sw_cols[g % 2][2]
                    act.wait_ge(*at(("swr", g)))
                    for j in range(4):
                        a = le_s[g % 2][:, j, 0, 0:P]
                        act.activation(a, a, ACT.Copy, scale=s_sum[:, 2 * j:2 * j + 1]).then_inc(*mark("softmax0", ("swn", g, j, 0)))
                elif kind == "sw_copy":
                    g = args[0]
                    for j in (0, 2):
                        act.wait_ge(*at(("tr", "sww", g, j)))
                        if g:
                            act.wait_ge(*at(("swo", 2 * g - 1)))
                        act.activation(wT_s[:, j, :], bank[4 + j][:, 0:384], ACT.Copy).then_inc(*mark("turned_copied", ("swt", g, j)))
                elif kind == "sw_out":
                    g = args[0]
                    for q in range(2):
                        parts(bank[4 + q][:, 0:T], None, XH[:, 2 * g + q, :], ("xh", "sw", 2 * g + q), ("swo", 2 * g + q), ("pe", last_of("gate0")))
                elif kind == "x_logits":
                    g = args[0]
                    for j in range(2):
                        soft("x", 2 * g + j, j, HEAD ** -0.5)
                elif kind == "a_logits":
                    g = args[0]
                    for j in range(2):
                        soft("a", 2 * g + j, j, HEAD ** -0.5)
                elif kind in ("x_weights", "a_weights"):
                    tag, g = kind[0], args[0]
                    hd = 2 * g
                    act.wait_ge(*at(("trw", tag, hd)))
                    if tag == "x" and g:
                        act.wait_ge(*at(("oz", "c", hd - 1)))
                    elif tag == "a":
                        act.wait_ge(*at(("oz", "a", hd - 1) if g else ("oz", "c", X_HEADS - 1)))
                    n = 2 * T if tag == "x" else 384
                    act.activation(wT[:, 0, :, :].rearrange("p a b -> p (a b)")[:, 0:n], bank[2][:, 0:n], ACT.Copy).then_inc(*mark("turned_copied", ("wT", tag, hd)))
                elif kind in ("x_out", "a_out"):
                    b, g = ("c" if kind[0] == "x" else "a"), args[0]
                    src = gc if b == "c" else ga
                    for j in range(2):
                        hd = 2 * g + j
                        act.wait_ge(*at(("og", b, hd)))
                        act.wait_ge(*at(("xn", "mem", 1)))
                        act.wait_ge(*at(("pe", last_of("down1"))))
                        act.activation(GH[:, OUT_AT[b] + hd, :], src[:, hd, :], ACT.Copy).then_inc(*mark("gated_hi", ("oh", b, hd)))
                elif kind == "rope_turn":
                    for j in ((0, 2), (4,))[args[0]]:
                        act.wait_ge(*at(("tr", "rope", j)))
                        dst = qF if j < 3 else kF
                        act.activation(dst[:, (2 * j) % 6:(2 * j) % 6 + 2, :], two(j % 4), ACT.Copy).then_inc(*mark("turned_copied", ("qkF", j)))
                elif kind == "spatial":
                    for j in range(2):
                        act.wait_ge(*at(("tr", "wsp", j)))
                        act.activation(wsp[:, 3 * j:3 * j + 3, :].rearrange("p g t -> p (g t)"), bank[2 + j][:, 0:384], ACT.Copy).then_inc(*mark("turned_copied", ("wspT", j)))
                elif kind == "layer_norm":
                    act.wait_ge(*at(("roped",)))
                    act.wait_ge(*at(("tr", "wsp", 1)))
                    for t in range(TT):
                        act.wait_ge(*at(("lnm",)))
                        act.activation(xn[:, t, 0:768], vb[:, t, :], ACT.Square, bias=ln_neg[:, t:t + 1], accum_out=ln_ss[:, t:t + 1]).then_inc(*mark("squared", ("lnsq", t)))
                elif kind == "mixed":
                    for g in range(GROUPS):
                        act.wait_ge(*at(("og", "b", g)))
                        act.activation(GH[:, OUT_AT["b"] + g, :], ubs[:, g, :], ACT.Copy).then_inc(*mark("gated_hi", ("oh", "b", g)))
                elif kind == "y_split":
                    for j in range(4):
                        parts(y[:, 2 * j:2 * j + 2, :], None, XH[:, 2 * j:2 * j + 2, :], ("xh", "y", j), ("yb", "a", j), ("pe", last_of("ma")))

        @block.vector
        def _(dve):
            def split(n):
                if n < len(PANELS):
                    dve.wait_ge(*at(("hi", n)))
                    dve.tensor_tensor(wlo[n % RING][:, :], raw[n % RAW][:, :], plain(whi[n % RING][:, :]), ALU.subtract).then_inc(*mark("weights_lo", ("lo", n)))

            def rest(src, gain, hi, lo, name, event, *first):
                for before in first:
                    dve.wait_ge(*at(before))
                if gain is None:
                    return dve.tensor_tensor(lo, src, plain(hi), ALU.subtract).then_inc(*mark(name, event))
                return dve.scalar_tensor_tensor(lo, src, gain, plain(hi), ALU.mult, ALU.subtract).then_inc(*mark(name, event))

            def inverse_root(x, out, tmp):
                dve.tensor_scalar(tmp.bitcast(I32), x.bitcast(I32), 1, None, ALU.logical_shift_right).then_inc(*chained())
                dve.wait_ge(*chain())
                dve.tensor_scalar(out.bitcast(I32), tmp.bitcast(I32), -1.0, MAGIC, ALU.mult, ALU.add).then_inc(*chained())
                dve.wait_ge(*chain())
                for _ in range(3):
                    dve.tensor_tensor(tmp, out, out, ALU.mult).then_inc(*chained())
                    dve.wait_ge(*chain())
                    dve.scalar_tensor_tensor(tmp, x, -0.5, tmp, ALU.mult, ALU.mult).then_inc(*chained())
                    dve.wait_ge(*chain())
                    dve.scalar_tensor_tensor(out, tmp, 1.5, out, ALU.add, ALU.mult).then_inc(*chained())
                    dve.wait_ge(*chain())

            def hg_level(li):
                if li < 0 or LEVELS[li]:
                    e = ex if li % 2 == 0 else exb
                    X = xs_buf[li % 2]
                    half = LEVELS[li] if li >= 0 else P
                    if li >= 1 or li == 0:
                        for before in ([("xs", li - 2)] if li >= 1 else []):
                            dve.wait_ge(*at(before))
                    if half >= HG_CHUNK:
                        ends = [bdec[:, :, HG_CHUNK * (c + 1) - 1:HG_CHUNK * (c + 1)].to_broadcast([P, HG_HEADS, HG_CHUNK]) for c in range(4)]
                        part = lambda x, c: x[:, :, HG_CHUNK * c:HG_CHUNK * (c + 1)]
                        left = (0, 1) if half == P else (0, 2)
                        for c in range(4):
                            if c in left:
                                dve.tensor_tensor(part(e, c), ends[c], part(bdec, c), ALU.subtract).then_inc(*mark("exponents", ("dd_left", li), ("dd", li)))
                            elif half == P and c == 3:
                                dve.tensor_tensor(part(e, c), ends[2], part(bdec, c), ALU.add).then_inc(*mark("exponents", ("dd", li)))
                            else:
                                dve.tensor_copy(part(e, c), part(bdec, c)).then_inc(*mark("exponents", ("dd", li)))
                        if half == P:
                            dve.wait_ge(*at(("dd_left", li)))
                            dve.tensor_tensor(part(e, 0), part(e, 0), ends[1], ALU.add).then_inc(*mark("exponents", ("dd", li)))
                    else:
                        halves = lambda x: x[:, :, :].rearrange("p h (n c) -> p (h n) c", c=2 * half)
                        mid = halves(bdec)[:, :, half - 1:half].to_broadcast([P, HG_HEADS * T // (2 * half), half])
                        l, r = halves(bdec)[:, :, 0:half], halves(bdec)[:, :, half:2 * half]
                        dve.tensor_tensor(halves(e)[:, :, 0:half], mid, l, ALU.subtract).then_inc(*mark("exponents", ("dd0", li)))
                        dve.tensor_tensor(halves(e)[:, :, half:2 * half], r, mid, ALU.subtract).then_inc(*mark("exponents", ("dd", li)))
                    dve.wait_ge(*at(("ex", li)))
                    if li >= 1:
                        dve.wait_ge(*at(("ps", li - 2, 1 if li >= 2 else 0)))
                    halves = lambda x: x[:, :, :].rearrange("p h (n c) -> p (h n) c", c=2 * half)
                    dve.tensor_tensor(halves(X)[:, :, 0:half], halves(e)[:, :, 0:half], halves(kk)[:, :, 0:half], ALU.mult).then_inc(*mark("decayed", ("xs0", li)))
                    dve.tensor_tensor(halves(X)[:, :, half:2 * half], halves(e)[:, :, half:2 * half], halves(qf)[:, :, half:2 * half], ALU.mult).then_inc(*mark("decayed", ("xs", li)))

            def hg_mask(li):
                if li < 0:
                    dve.wait_ge(*at(("ps", li, 0)))
                    dve.tensor_copy(sc[:, :, P:2 * P], bank[0][:, :].rearrange("p (h c) -> p h c", h=HG_HEADS)).then_inc(*mark("cross_scores", ("sc", -1, 0)))
                    return
                dve.wait_ge(*at(("loaded", "levels")))
                for j in range(2):
                    b = (2 * li + j + 2) % 4
                    dve.wait_ge(*at(("ps", li, j)))
                    for before in ([("sc", li - 1, j)] if li >= 2 else []):
                        dve.wait_ge(*at(before))
                    out = blocks_of(sc, 2 * j) if li == 0 else blocks_of_prod(j)
                    mask = masks[:, li, :].rearrange("p (a b c) -> p a b c", a=1, b=1).to_broadcast([P, 2, 2, P])
                    events = [("prod", li, j)] + ([("sc", 0, j)] if li == 0 else [])
                    dve.tensor_tensor(out, bank[b][:, :].rearrange("p (h t c) -> p h t c", h=2, t=2), mask, ALU.mult).then_inc(*mark("masked_scores", *events))
                    if li >= 6 and j == 1:
                        a = blocks_of(sc, 2 * j)
                        dve.wait_ge(*at(("prod", li, j)))
                        dve.wait_ge(*at(("sc", li - 1, j)))
                        dve.tensor_tensor(a, a, blocks_of_prod(j), ALU.add).then_inc(*mark("scores_summed_v", ("sc", li, j)))

            def taps(n):
                stage, i = PANELS[n][:2]
                dve.wait_ge(*at(("a", n)))
                for tap in (1, 0):
                    d = 2 - tap
                    for c in range(2):
                        v = cc[i % 3][:, c, d:T]
                        if tap == 0:
                            dve.wait_ge(*at(("tap", n, c)))
                        dve.scalar_tensor_tensor(v, conv_in[i % 2][:, c, 0:T - d], vec("ffn_conv", int(stage[-1]), tap)(c * FT + i), v, ALU.mult, ALU.add).then_inc(*mark("convolved", ("conv", int(stage[-1]), i) if tap == 0 else ("tap", n, c)))

            def ffn_lo(l, i):
                rest(gf[i % 2][:, :], None, GH[:, i, :], GL[:, i, :], "gated_lo", ("gl", l, i), ("gh", l, i))

            def panel(n):
                stage, i, name, kind, _where = PANELS[n]
                b = pb(n)
                c2, cT = slice(2 * i, 2 * i + 2), slice(256 * i, 256 * i + 256)
                ev = ("ev", n)
                if stage.startswith("wo"):
                    dve.wait_ge(*at(("pe", n)))
                    dve.tensor_tensor(h[:, :, cT], two(b), h[:, :, cT], ALU.add).then_inc(*mark("residual", ev))
                elif stage.startswith("up"):
                    l = int(stage[-1])
                    dve.wait_ge(*at(("pe", n)))
                    dve.wait_ge(*at(("rows", NORM_OF[stage])))
                    if i >= 2:
                        dve.wait_ge(*at(("a", n - 2)))
                    if i >= 2 or l:
                        dve.wait_ge(*at(("conv", l, i - 2) if i >= 2 else ("conv", l - 1, FT - 2 + i)))
                    dve.tensor_tensor(conv_in[i % 2][:, :, :], two(b), row2(NORM_OF[stage]), ALU.mult).then_inc(*mark("scaled", ("scaled", n), ev))
                    if i >= 1:
                        dve.wait_ge(*at(("scaled", n - 1)))
                        taps(n - 1)
                    if i >= 3:
                        ffn_lo(l, i - 3)
                elif kind == "F" and stage != "mk":
                    dve.wait_ge(*at(("pe", n)))
                    dve.wait_ge(*at(("rows", NORM_OF[stage])))
                    if stage == "ga" and i == 0:
                        dve.wait_ge(*at(("tr", "rope", 5)))
                    if stage == "ma" and i == 0:
                        dve.wait_ge(*at(("yb", "c", 3)))
                    row = row2(NORM_OF[stage])
                    if stage == "qa":
                        dve.scalar_tensor_tensor(qaT[:, c2, :], two(b), SB_DIM ** -0.5, row, ALU.mult, ALU.mult).then_inc(*mark("scaled", ev))
                    elif stage == "ub":
                        dve.wait_ge(*at(("ev", n - 3)))
                        dve.tensor_tensor(ubs[:, c2, :], ubs[:, c2, :], row, ALU.mult).then_inc(*mark("scaled", ("gate_scaled", n)))
                        dve.wait_ge(*at(("gate_scaled", n)))
                        dve.tensor_tensor(ubs[:, c2, :], two(b), ubs[:, c2, :], ALU.mult).then_inc(*mark("scaled", ev))
                    else:
                        dst = {"qb": qf, "fb": bdec, "ka": kaT, "qc": qc, "gc": gc, "ga": ga, "gb2": ubs, "mc": msig[0], "mb": msig[1], "ma": msig[0]}[stage]
                        event = ev if stage in ("ka", "qc") else ("scaled", n)
                        dve.tensor_tensor(dst[:, c2, :], two(b), row, ALU.mult).then_inc(*mark("scaled", event))
                elif stage.startswith("gate"):
                    dve.wait_ge(*at(("a", n)))
                    dve.wait_ge(*at(("pe", last_of("pp" + stage[-1]))))
                    g = gate[i % 2]
                    for t in range(TT):
                        dve.tensor_tensor(g[:, t, :], g[:, t, :], bank[ppb(int(stage[-1]), t, i // 2)][:, (i % 2) * 256:(i % 2) * 256 + 256], ALU.mult).then_inc(*mark("ple", ("ple", n, t)))
                    dve.wait_ge(*at(("ple", n, 1)))
                    dve.tensor_tensor(h[:, :, cT], g[:, :, :], h[:, :, cT], ALU.add).then_inc(*mark("residual", ev))
                if stage.startswith("down") and n == last_of(stage):
                    for t in range(TT):
                        dve.wait_ge(*at(("tok0", stage) if t == 0 else ("pe", n)))
                        for half in range(2):
                            a = h[:, t, half * 512:half * 512 + 512]
                            dve.tensor_tensor(a, bank[2 * t + half][:, :], a, ALU.add).then_inc(*mark("residual", ("h", stage, t)))
                if not splits_later(n):
                    split(n + RING)

            def y_lo(j):
                c = slice(2 * j, 2 * j + 2)
                rest(y[:, c, :], None, XH[:, c, :], XL[:, c, :], "input_lo", ("xl", "y", j), ("xh", "y", j))

            def soften(tag, hd, j):
                dve.wait_ge(*at(("e", tag, hd)))
                c = slice(2 * j, 2 * j + 2)
                dve.reciprocal(s_sum[:, c], s_sum[:, c]).then_inc(*chained())
                dve.wait_ge(*chain())
                for t in range(TT):
                    v = le[:, j, t, 0:P if (t == 0 and tag == "a") else T]
                    dve.tensor_scalar(v, v, s_sum[:, 2 * j + t:2 * j + t + 1], None, ALU.mult).then_inc(*mark("softmax", ("n", tag, hd)))

            for step in SCHEDULE:
                kind, args = step[0], step[1:]
                if kind == "panel":
                    panel(args[0])
                elif kind == "split":
                    split(args[0])
                elif kind == "setup":
                    if not args[0]:
                        continue
                    dve.wait_ge(*at(("vec", 0)))
                    a = VEC["hg_lb_logits", 0]
                    dve.wait_ge(*at(("table",)))
                    dve.tensor_tensor(lb_tmp, vflat[:, a:a + 4], vflat[:, a:a + 4], ALU.subtract).then_inc(*chained(("lb0",)))
                    dve.wait_ge(*chain())
                    dve.wait_ge(*at(("lbe",)))
                    dve.reciprocal(lb, lb_tmp).then_inc(*chained())
                    dve.wait_ge(*chain())
                    dve.tensor_tensor(lb_tmp, lb, lb_tmp, ALU.mult).then_inc(*chained())
                    dve.wait_ge(*chain())
                    dve.tensor_tensor(lb, lb_tmp, lb_tmp, ALU.subtract).then_inc(*chained())
                    dve.wait_ge(*chain())
                    dve.tensor_scalar(oml, lb, -1.0, 1.0, ALU.mult, ALU.add).then_inc(*chained())
                    dve.wait_ge(*chain())
                    dve.tensor_scalar(q_gain, vec("q_norm", 0)(0), SW_DIM ** -0.5, None, ALU.mult).then_inc(*chained(("q_gain",)))
                    dve.wait_ge(*chain())
                elif kind == "stats":
                    k = args[0]
                    dve.wait_ge(*at(("sq", k, 7 if k == "mem" else 3)))
                    dve.tensor_reduce(rstd[k], ssq[k].rearrange("p (t j) -> p t j", t=TT), AX.X, ALU.add).then_inc(*chained())
                    dve.wait_ge(*chain())
                    dve.tensor_scalar(rstd[k], rstd[k], 1.0 / D, EPS, ALU.mult, ALU.add).then_inc(*mark("mean_square", ("ms", k)))
                    if k == "mem":
                        dve.wait_ge(*at(("rstd", k)))
                        dve.tensor_scalar(mem[:, 0, :], mem[:, 0, :], rstd[k][:, 0:1], None, ALU.mult).then_inc(*mark("normalized0", ("xn", k, 0)))
                    elif k == "final":
                        dve.wait_ge(*at(("rstd", k)))
                        dve.wait_ge(*at(("hgn", 3)))
                        dve.tensor_scalar(result[:, 0, :], result[:, 0, :], rstd[k][:, 0:1], None, ALU.mult).then_inc(*mark("result0", ("result", 0)))
                elif kind == "square" and args[0] == "final":
                    c = slice(256 * args[1], 256 * args[1] + 256)
                    dve.wait_ge(*at(("loaded", "gfin")))
                    dve.wait_ge(*at(("ev", FIRST["wo2"] + args[1])))
                    gain = gfin[:, c].rearrange("p (a c) -> p a c", a=1).to_broadcast([P, TT, 256])
                    dve.tensor_tensor(result[:, :, c], h[:, :, c], gain, ALU.mult).then_inc(*mark("final_gain", ("hgn", args[1])))
                elif kind in ("turn", "turn_last"):
                    k, j = args if kind == "turn" else (args[0], 3)
                    hi, lo = DEST[k]
                    for q in range(2):
                        kt = 2 * j + q
                        rest(two(turn_bank(k, j))[:, q, :], GAIN[k](kt), hi[:, kt, :], lo[:, kt, :], "input_lo", ("xl", k, j), ("xh", k, j))
                elif kind == "hg_decay":
                    dve.wait_ge(*at(("ev", last_of("fb"))))
                    for hd in range(HG_HEADS):
                        dve.tensor_scalar(bdec[:, hd, :], bdec[:, hd, :], oml[:, hd:hd + 1], lb[:, hd:hd + 1], ALU.mult, ALU.add).then_inc(*mark("decay", ("f0",)))
                        dve.tensor_scalar(kk[:, hd, :], kk[:, hd, :], oml[:, hd:hd + 1], None, ALU.mult).then_inc(*mark("decay", ("kk",)))
                    dve.wait_ge(*at(("f0",)))
                    dve.tensor_scalar(bdec[:, :, :], bdec[:, :, :], 2.0 ** -64, None, ALU.max).then_inc(*mark("decay", ("f",)))
                    dve.wait_ge(*at(("logf",)))
                    dve.wait_ge(*at(("loaded", "reset")))
                    flat = lambda x: x[:, :, :].rearrange("p a b -> p (a b)")
                    dve.tensor_tensor_scan(flat(bdec), reset[:, :], flat(ex), 0.0, ALU.mult, ALU.add).then_inc(*mark("decay", ("b",)))
                    dve.wait_ge(*at(("b",)))
                    dve.wait_ge(*at(("kk",)))
                elif kind == "hg_level":
                    hg_level(args[0])
                elif kind == "hg_mask":
                    hg_mask(args[0])
                elif kind == "sb_log":
                    for i in range(4):
                        c = slice(2 * i, 2 * i + 2)
                        dve.wait_ge(*at(("sbl", i)))
                        fl = lambda x: x[:, c, :].rearrange("p a b -> p (a b)")
                        dve.scalar_tensor_tensor(fl(sp_), fl(zs), 0.0, fl(sp_), ALU.max, ALU.add).then_inc(*mark("softplus", ("splus", i)))
                elif kind == "hg_norm":
                    for t in range(TT):
                        dve.wait_ge(*at(("hgsq", t)))
                        dve.tensor_reduce(hg_ss[:, 4 * t:4 * t + 4], prod4[:, t, :].rearrange("p (h v) -> p h v", h=4), AX.X, ALU.add).then_inc(*chained())
                        dve.wait_ge(*chain())
                    dve.tensor_scalar(hg_ss, hg_ss, 1.0 / P, EPS, ALU.mult, ALU.add).then_inc(*chained())
                    dve.wait_ge(*chain())
                    inverse_root(hg_ss, hg_rs, hg_tmp)
                    for t in range(TT):
                        r4 = hg_rs[:, 4 * t:4 * t + 4].rearrange("p (h a) -> p h a", a=1).to_broadcast([P, 4, P])
                        dve.tensor_tensor(on[:, t, :, :], bank[t][:, :].rearrange("p (h v) -> p h v", h=4), r4, ALU.mult).then_inc(*chained(("on", t)))
                        dve.wait_ge(*chain())
                        o = on[:, t, :, :].rearrange("p h v -> p (h v)")
                        dve.tensor_tensor(o, o, gbs[:, t, :], ALU.mult).then_inc(*mark("hg_gated", ("gated", t)))
                elif kind == "hg_turn":
                    for j in range(2):
                        dve.wait_ge(*at(("xh", "hg", j)))
                        fl = lambda x: x.rearrange("p a b -> p (a b)")
                        dve.scalar_tensor_tensor(fl(XL[:, 4 + 2 * j:6 + 2 * j, :]), bank[2 + j][:, :], vec("hg_out_norm", 0)(0), plain(fl(XH[:, 4 + 2 * j:6 + 2 * j, :])), ALU.mult, ALU.subtract).then_inc(*mark("input_lo", ("xl", "hg", j)))
                elif kind == "sb_weights":
                    i = args[0]
                    for r in range(2):
                        hd = 2 * i + r
                        dve.wait_ge(*at(("sbr", hd)))
                        dve.tensor_tensor(zs[:, hd, :], zs[:, hd, :], bank[4 + hd % 4][:, 0:384], ALU.subtract).then_inc(*mark("sb_exponents", ("d", hd)))
                elif kind == "sb_out":
                    i = args[0]
                    rest(bank[4 + i][:, 0:T], None, XH[:, i, :], XL[:, i, :], "input_lo", ("xl", "sb", i), ("xh", "sb", i))
                elif kind == "up_tail":
                    l = args[0]
                    taps(last_of(f"up{l}"))
                    ffn_lo(l, FT - 3)
                    ffn_lo(l, FT - 2)
                    ffn_lo(l, FT - 1)
                elif kind == "ple_input":
                    l = args[0]
                    rest(two(4), None, PTH[:, :, :], PTL[:, :, :], "input_lo", ("ptl", l), ("pth", l))
                elif kind == "bias":
                    dve.wait_ge(*at(("brp",)))
                    dve.wait_ge(*at(("brow0",)))
                    dve.tensor_copy(brow[:, P:2 * P], bank[5][0:16, 0:P]).then_inc(*mark("bias_row", ("brow",)))
                elif kind == "sw_norm":
                    half = args[0]
                    groups = ((0, 8, 0), (16, 4, 16)) if half == 0 else ((8, 8, 24),)
                    n = 24 if half == 0 else 16
                    c = slice(24 * half, 24 * half + n)
                    for t in range(TT):
                        dve.wait_ge(*at(("swsq", half, t)))
                        for h0, nh, c0 in groups:
                            o = c0 + nh * t
                            dve.tensor_reduce(sw_ss[:, o:o + nh], sq[:, t, 64 * h0:64 * (h0 + nh)].rearrange("p (h d) -> p h d", d=SW_DIM), AX.X, ALU.add).then_inc(*chained())
                    dve.wait_ge(*chain())
                    dve.tensor_scalar(sw_ss[:, c], sw_ss[:, c], 1.0 / SW_DIM, EPS, ALU.mult, ALU.add).then_inc(*chained())
                    dve.wait_ge(*chain())
                    inverse_root(sw_ss[:, c], sw_rs[:, c], sw_tmp[half][:, 0:n])
                    for t in range(TT):
                        for h0, nh, c0 in groups:
                            r = sw_rs[:, c0 + nh * t:c0 + nh * t + nh].rearrange("p (h a) -> p h a", a=1).to_broadcast([P, nh, SW_DIM])
                            src = qk[:, t, 64 * h0:64 * (h0 + nh)].rearrange("p (h d) -> p h d", d=SW_DIM)
                            if h0 < 16:
                                dve.tensor_tensor(qkn[:, t, h0:h0 + nh, :], src, r, ALU.mult).then_inc(*mark("sw_normed", ("qkn", half, t)))
                                continue
                            for copy in range(2):
                                dst = qkn[:, t, 16:24, :].rearrange("p (g a) d -> p g a d", a=2)[:, :, copy, :]
                                dve.tensor_tensor(dst, src, r, ALU.mult).then_inc(*mark("sw_normed", ("qkn", half, t)))
                elif kind == "sw_logits":
                    g = args[0]
                    s_max, s_neg, s_sum, s_exp = sw_cols[g % 2]
                    dve.wait_ge(*at(("loaded", "bias")))
                    dve.wait_ge(*at(("loaded", "sinks")))
                    for j in range(4):
                        hd = 4 * g + j
                        dve.wait_ge(*at(("swz", g, j)))
                        if g >= 2:
                            dve.wait_ge(*at(("tr", "sww", g - 2, j)))
                        for t in range(TT):
                            w = P if t == 0 else T
                            dve.tensor_tensor_reduce(le_s[g % 2][:, j, t, 0:w], bank[j][:, t * T:t * T + w], bias[:, hd, T - w:T], 1.0, -3.0e38, ALU.add, ALU.max, s_max[:, 2 * j + t:2 * j + t + 1]).then_inc(*mark("logits", ("swm", g, j)))
                    dve.wait_ge(*at(("swm", g, 3)))
                    sk = sinks[:, 4 * g:4 * g + 4].rearrange("p (h a) -> p h a", a=1).to_broadcast([P, 4, 2])
                    v = lambda x: x.rearrange("p (h a) -> p h a", a=2)
                    dve.tensor_tensor(v(s_max), v(s_max), sk, ALU.max).then_inc(*chained())
                    dve.wait_ge(*chain())
                    dve.tensor_scalar(s_neg, s_max, -1.0, None, ALU.mult).then_inc(*chained())
                    dve.wait_ge(*chain())
                    dve.tensor_tensor(v(s_exp), v(s_neg), sk, ALU.add).then_inc(*mark("logits", ("swneg", g)))
                elif kind == "sw_weights":
                    g = args[0]
                    s_max, s_neg, s_sum, s_exp = sw_cols[g % 2]
                    dve.wait_ge(*at(("swx", g)))
                    dve.tensor_tensor(s_sum, s_sum, s_exp, ALU.add).then_inc(*chained())
                    dve.wait_ge(*chain())
                    dve.reciprocal(s_sum, s_sum).then_inc(*chained(("swr", g)))
                    dve.wait_ge(*chain())
                    for j in range(4):
                        a = le_s[g % 2][:, j, 1, :]
                        dve.tensor_scalar(a, a, s_sum[:, 2 * j + 1:2 * j + 2], None, ALU.mult).then_inc(*mark("softmax", ("swn", g, j, 1)))
                elif kind == "sw_copy":
                    g = args[0]
                    for j in (1, 3):
                        dve.wait_ge(*at(("tr", "sww", g, j)))
                        if g:
                            dve.wait_ge(*at(("swo", 2 * g - 1)))
                        dve.tensor_copy(wT_s[:, j, :], bank[4 + j][:, 0:384]).then_inc(*mark("turned_copied2", ("swt", g, j)))
                elif kind == "sw_out":
                    g = args[0]
                    for q in range(2):
                        i = 2 * g + q
                        rest(bank[4 + q][:, 0:T], None, XH[:, i, :], XL[:, i, :], "input_lo", ("xl", "sw", i), ("xh", "sw", i))
                elif kind == "x_logits":
                    g = args[0]
                    for j in range(2):
                        hd = 2 * g + j
                        dve.wait_ge(*at(("xz", hd)))
                        if g:
                            dve.wait_ge(*at(("n", "x", 2 * g - 1)))
                            dve.wait_ge(*at(("trw", "x", hd - 2)))
                        c = slice(2 * j, 2 * j + 2)
                        dve.tensor_reduce(s_max[:, c], two(j), AX.X, ALU.max).then_inc(*chained())
                        dve.wait_ge(*chain())
                        dve.tensor_scalar(s_neg[:, c], s_max[:, c], -HEAD ** -0.5, None, ALU.mult).then_inc(*chained(("neg", "x", hd)))
                        dve.wait_ge(*chain())
                    for j in range(2):
                        soften("x", 2 * g + j, j)
                elif kind == "a_logits":
                    g = args[0]
                    dve.wait_ge(*at(("loaded", "causal")))
                    for j in range(2):
                        hd = 2 * g + j
                        dve.wait_ge(*at(("az", hd)))
                        dve.wait_ge(*at(("trw", "a", hd - 2) if g else ("trw", "x", 2 + j)))
                        for t in range(TT):
                            w = P if t == 0 else T
                            dve.tensor_tensor_reduce(le[:, j, t, 0:w], bank[j][:, t * T:t * T + w], causal[:, T - w:T], 1.0, -3.0e38, ALU.add, ALU.max, s_max[:, 2 * j + t:2 * j + t + 1]).then_inc(*mark("logits", ("am", hd)))
                        dve.wait_ge(*at(("am", hd)))
                        dve.tensor_scalar(s_neg[:, 2 * j:2 * j + 2], s_max[:, 2 * j:2 * j + 2], -HEAD ** -0.5, None, ALU.mult).then_inc(*chained(("neg", "a", hd)))
                        dve.wait_ge(*chain())
                    for j in range(2):
                        soften("a", 2 * g + j, j)
                elif kind in ("x_weights", "a_weights"):
                    tag, g = kind[0], args[0]
                    hd = 2 * g + 1
                    dve.wait_ge(*at(("trw", tag, hd)))
                    if tag == "x" and g:
                        dve.wait_ge(*at(("oz", "c", hd - 2)))
                    elif tag == "a":
                        dve.wait_ge(*at(("oz", "a", hd - 2) if g else ("oz", "c", X_HEADS - 1)))
                    n = 2 * T if tag == "x" else 384
                    dve.tensor_copy(wT[:, 1, :, :].rearrange("p a b -> p (a b)")[:, 0:n], bank[3][:, 0:n]).then_inc(*mark("turned_copied2", ("wT", tag, hd)))
                elif kind in ("x_out", "a_out"):
                    b, g = ("c" if kind[0] == "x" else "a"), args[0]
                    src = gc if b == "c" else ga
                    dve.wait_ge(*at(("ev", last_of("gc" if b == "c" else "ga"))))
                    for j in range(2):
                        hd = 2 * g + j
                        dve.wait_ge(*at(("oz", b, hd)))
                        dve.tensor_tensor(src[:, hd, :], bank[2 + j][:, 0:T], src[:, hd, :], ALU.mult).then_inc(*mark("gated", ("og", b, hd)))
                    for j in range(2):
                        hd = 2 * g + j
                        rest(src[:, hd, :], None, GH[:, OUT_AT[b] + hd, :], GL[:, OUT_AT[b] + hd, :], "gated_lo", ("ol", b, hd), ("oh", b, hd))
                elif kind == "rope":
                    dve.wait_ge(*at(("ev", last_of("qka"))))
                    dve.wait_ge(*at(("loaded", "rope")))
                    dve.wait_ge(*at(("pe", last_of("mv"))))
                    for t in range(TT):
                        q = qkm[:, t, :].rearrange("p (e d) -> p e d", d=HEAD)
                        x1, x2 = q[:, :, 0:16], q[:, :, 16:32]
                        cos, sin = (rope[:, t, c, :].rearrange("p (a f) -> p a f", a=1).to_broadcast([P, 12, 16]) for c in range(2))
                        if t:
                            dve.wait_ge(*at(("roped0",)))
                        for f, (a, m) in enumerate(((x1, cos), (x2, sin), (x2, cos), (x1, sin))):
                            dve.tensor_tensor(rtmp[:, f, :, :], a, m, ALU.mult).then_inc(*mark("rope", ("rope_m", t)))
                        dve.wait_ge(*at(("rope_m", t)))
                        dve.tensor_tensor(x1, rtmp[:, 0, :, :], rtmp[:, 1, :, :], ALU.subtract).then_inc(*mark("rope", ("rope_s", t)))
                        dve.tensor_tensor(x2, rtmp[:, 2, :, :], rtmp[:, 3, :, :], ALU.add).then_inc(*mark("rope", ("roped",) if t else ("roped0",)))
                elif kind == "rope_turn":
                    for j in ((1,), (3, 5))[args[0]]:
                        dve.wait_ge(*at(("tr", "rope", j)))
                        dst = qF if j < 3 else kF
                        dve.tensor_copy(dst[:, (2 * j) % 6:(2 * j) % 6 + 2, :], two(j % 4)).then_inc(*mark("turned_copied2", ("qkF", j)))
                elif kind == "layer_norm":
                    dve.wait_ge(*at(("ev", last_of("vb"))))
                    for t in range(TT):
                        dve.tensor_reduce(ln_sum[:, t:t + 1], vb[:, t, :], AX.X, ALU.add).then_inc(*chained())
                        dve.wait_ge(*chain())
                    dve.tensor_scalar(ln_neg, ln_sum, -1.0 / 768, None, ALU.mult).then_inc(*chained(("lnm",)))
                    dve.wait_ge(*chain())
                    dve.wait_ge(*at(("lnsq", 1)))
                    dve.tensor_scalar(ln_ss, ln_ss, 1.0 / 768, EPS, ALU.mult, ALU.add).then_inc(*chained())
                    dve.wait_ge(*chain())
                    inverse_root(ln_ss, ln_rs, ln_sum)
                    for t in range(TT):
                        dve.tensor_scalar(vb[:, t, :], vb[:, t, :], ln_neg[:, t:t + 1], ln_rs[:, t:t + 1], ALU.add, ALU.mult).then_inc(*mark("layer_normed", ("vn", t)))
                elif kind == "mixed":
                    dve.wait_ge(*at(("ev", last_of("ub"))))
                    dve.wait_ge(*at(("loaded", "bsp")))
                    for g in range(GROUPS):
                        dve.wait_ge(*at(("mixp", g // 2)))
                        tb = lambda x: x.rearrange("p (t c) -> p t c", t=TT)
                        bb = bsp[:, g, :].rearrange("p (a c) -> p a c", a=1).to_broadcast([P, TT, P])
                        dve.scalar_tensor_tensor(tb(mixt[:, g, :]), tb(two(g // 2)[:, g % 2, :]), vec("gmlp_ln_g_2", 0)(g), bb, ALU.mult, ALU.add).then_inc(*mark("mixed", ("mixg", g)))
                    for g in range(GROUPS):
                        dve.wait_ge(*at(("mixg", g)))
                        dve.tensor_tensor(ubs[:, g, :], mixt[:, g, :], ubs[:, g, :], ALU.mult).then_inc(*mark("gated", ("og", "b", g)))
                    for g in range(GROUPS):
                        rest(ubs[:, g, :], None, GH[:, OUT_AT["b"] + g, :], GL[:, OUT_AT["b"] + g, :], "gated_lo", ("ol", "b", g), ("oh", "b", g))
                elif kind == "branch_end":
                    b = args[0]
                    m = msig[b == "b"]
                    dve.wait_ge(*at(("ev", last_of("m" + b))))
                    dve.wait_ge(*at(("og", "b", GROUPS - 1)))
                    for j in range(4):
                        c = slice(2 * j, 2 * j + 2)
                        dve.wait_ge(*at(("summed", "br" + b, j)))
                        if b == "c":
                            dve.tensor_tensor(y[:, c, :], two(j), m[:, c, :], ALU.mult).then_inc(*mark("branch_sum", ("yb", b, j)))
                        else:
                            dve.tensor_tensor(m[:, c, :], two(j), m[:, c, :], ALU.mult).then_inc(*chained())
                            dve.wait_ge(*chain())
                            dve.tensor_tensor(y[:, c, :], y[:, c, :], m[:, c, :], ALU.add).then_inc(*mark("branch_sum", ("yb", b, j)))
                        if b == "a" and j:
                            y_lo(j - 1)
                elif kind == "y_split":
                    y_lo(3)

    return events


_INS = ["x", "p", "mix_norm", "ab_w_in", "hg_lb_logits", "hg_out_norm", "ab_w_out", "c_w_in", "q_norm", "k_norm", "sinks", "rel_bias",
        "c_w_out", "ffn_norm", "ffn_up", "ffn_conv", "ffn_conv_b", "ffn_down", "ple_norm", "ple_gate", "ple_proj", "mem_2", "norm_g_2",
        "mem_norm_g_2", "final_norm_g_2", "w_in_2", "w_mem_kv_2", "gmlp_ln_g_2", "w_spatial_2", "b_spatial_2", "w_branch_a_2",
        "w_branch_b_2", "w_branch_c_2", "w_out_2"]


def kernel(**inputs):
    import concourse.bacc as bacc
    from concourse.bass_utils import run_bass_kernel_spmd

    arrays = {f"in_{n}": np.ascontiguousarray(inputs[n]) for n in _INS}
    arrays.update(shape_constants())

    def build(known):
        nc = bacc.Bacc("TRN2", target_bir_lowering=False, num_devices=1)
        io = {}
        for name, a in arrays.items():
            io[name.removeprefix("in_")] = nc.dram_tensor(name, a.shape, mybir.dt.from_np(a.dtype), kind="ExternalInput").ap()
        out = nc.dram_tensor("out_dram", (1, T, D), F32, kind="ExternalOutput").ap()
        return nc, block_program(nc, io, out, known)

    said = build({})[1].said
    nc = build(said)[0]
    r = run_bass_kernel_spmd(nc, [arrays], core_ids=[0])
    return r.results[0]["out_dram"]
```
